# Optimizing a Trainium2 kernel written in Bass

```python
import math
import jax, jax.numpy as jnp
from jax import lax
import numpy as np

D_MODEL = 1024
BATCH = 1
SEQ = 256
DEPTH = 1

BRANCH_WIDTH = D_MODEL // 2
N_BRANCH = 3
ATT_HEADS = 4
ATT_HEAD_DIM = BRANCH_WIDTH // (2 * ATT_HEADS)
ATT_V_DIM = 2 * ATT_HEAD_DIM
ROPE_THETA = 10000.0
Q_BLOCK = 128
HY_WIDTH = BRANCH_WIDTH
HY_ORDER = 2
HY_SHORT = 3
HY_BANDS = 16
HY_EMB = 1 + 2 * HY_BANDS
HY_FILTER_HIDDEN = 64
HY_FAST_DECAY = 0.3
HY_SLOW_DECAY = 1.5
HY_TARGET = 1e-2
HY_SHIFT = 0.05
CF_WIDTH = BRANCH_WIDTH
CF_KERNEL = 31
Q_COLS = ATT_HEADS * 2 * ATT_HEAD_DIM
K_COLS = ATT_HEADS * 2 * ATT_HEAD_DIM
V_COLS = ATT_HEADS * ATT_V_DIM
HY_COLS = (HY_ORDER + 1) * HY_WIDTH
CF_COLS = 2 * CF_WIDTH
GATE_COLS = N_BRANCH * D_MODEL
IN_COLS = Q_COLS + K_COLS + V_COLS + HY_COLS + CF_COLS + GATE_COLS
N_EXPERTS = 32
TOP_K = 4
EXPERT_FF = D_MODEL
SWIGLU_LIMIT = 7.0
SWIGLU_ALPHA = 1.702
EPS = 1e-6

kernel_name = 'hybrid_parallel_diffattn_hyena_conformer_moe'

def rmsnorm(x, g):
    xf = x.astype(jnp.float32)
    y = xf * lax.rsqrt(jnp.mean(xf * xf, axis=-1, keepdims=True) + EPS)
    return (y * g.astype(jnp.float32)).astype(x.dtype)

def layernorm(x, g, b):
    xf = x.astype(jnp.float32)
    mu = jnp.mean(xf, axis=-1, keepdims=True)
    var = jnp.mean(jnp.square(xf - mu), axis=-1, keepdims=True)
    y = (xf - mu) * lax.rsqrt(var + EPS)
    return (y * g.astype(jnp.float32) + b.astype(jnp.float32)).astype(x.dtype)

def dwconv(u, w, b):
    k, ch = w.shape
    y = lax.conv_general_dilated(u, w[:, None, :], window_strides=(1,),
                                 padding=[(k // 2, k // 2)],
                                 dimension_numbers=('NWC', 'WIO', 'NWC'),
                                 feature_group_count=ch)
    return y + b

def rope_tables(seq, dtype):
    pos = jnp.arange(seq, dtype=jnp.float32)
    inv = 1.0 / (ROPE_THETA ** (jnp.arange(0, ATT_HEAD_DIM, 2, dtype=jnp.float32) / ATT_HEAD_DIM))
    ang = pos[:, None] * inv[None, :]
    ang = jnp.concatenate([ang, ang], axis=-1)
    return jnp.cos(ang).astype(dtype), jnp.sin(ang).astype(dtype)

def apply_rope(t, cos, sin):
    c = cos[None, :, None, None, :]
    s = sin[None, :, None, None, :]
    t1, t2 = jnp.split(t, 2, axis=-1)
    return t * c + jnp.concatenate([-t2, t1], axis=-1) * s

def diff_attention(q, k, v, lam, lam_init, subln_g):
    bsz, seq, heads, _, d = q.shape
    n_blk = seq // Q_BLOCK
    qb = q.reshape(bsz, n_blk, Q_BLOCK, heads, 2, d).transpose(1, 0, 2, 3, 4, 5)
    scale = d ** -0.5

    def block(qi):
        s = jnp.einsum('bqhcd,bkhcd->bhcqk', qi, k).astype(jnp.float32) * scale
        p = jax.nn.softmax(s, axis=-1)
        a = (p[:, :, 0] - lam * p[:, :, 1]).astype(v.dtype)
        return jnp.einsum('bhqk,bkhe->bqhe', a, v)

    o = lax.map(block, qb)
    o = o.transpose(1, 0, 2, 3, 4).reshape(bsz, seq, heads, ATT_V_DIM)
    o = rmsnorm(o, subln_g) * (1.0 - lam_init)
    return o.reshape(bsz, seq, heads * ATT_V_DIM)

def hyena_filters(seq, w1, b1, w2, b2, w3, b3, freq, w4):
    f32 = jnp.float32
    pos = jnp.arange(seq, dtype=f32)
    t = jnp.linspace(0.0, 1.0, seq, dtype=f32)[:, None]
    bands = jnp.linspace(1e-4, HY_BANDS - 1, HY_BANDS, dtype=f32)
    ang = (2.0 * math.pi / seq) * pos[:, None] * bands[None, :]
    z = jnp.concatenate([t, jnp.cos(ang), -jnp.sin(ang)], axis=-1).astype(w1.dtype)
    hdn = jnp.sin(freq * (z @ w1 + b1))
    hdn = jnp.sin(freq * (hdn @ w2 + b2))
    hdn = jnp.sin(freq * (hdn @ w3 + b3))
    h = (hdn @ w4).reshape(seq, HY_ORDER, 2, HY_WIDTH)
    deltas = jnp.abs(jnp.linspace(math.log(HY_TARGET) / HY_FAST_DECAY,
                                  math.log(HY_TARGET) / HY_SLOW_DECAY, HY_WIDTH, dtype=f32))
    window = (jnp.exp(-t * deltas[None, :]) + HY_SHIFT).astype(h.dtype)
    return h * window[:, None, None, :]

def bidir_long_conv(u, h_fwd, h_bwd):
    seq = u.shape[1]
    n = 2 * seq
    kern = jnp.concatenate([h_fwd[:1] + h_bwd[:1], h_fwd[1:], jnp.zeros_like(h_fwd[:1]),
                            h_bwd[:0:-1]], axis=0).astype(jnp.float32)
    uf = jnp.fft.rfft(u.astype(jnp.float32), n=n, axis=1)
    kf = jnp.fft.rfft(kern, n=n, axis=0)
    y = jnp.fft.irfft(uf * kf[None], n=n, axis=1)[:, :seq]
    return y.astype(u.dtype)

def hyena_mixer(u, conv_w, conv_b, filters, d_bias):
    u = dwconv(u, conv_w, conv_b)
    v, x1, x2 = jnp.split(u, 3, axis=-1)
    z = v
    for n, xg in enumerate((x1, x2)):
        z = xg * (bidir_long_conv(z, filters[:, n, 0], filters[:, n, 1]) + d_bias[n] * z)
    return z

def conformer_conv(u, dw_w, dw_b, ln_g, ln_b):
    a, g = jnp.split(u, 2, axis=-1)
    u = a * jax.nn.sigmoid(g)
    u = dwconv(u, dw_w, dw_b)
    u = layernorm(u, ln_g, ln_b)
    return jax.nn.silu(u)

def moe(h, w_r, b_r, w_gu, b_gu, w_dn, b_dn):
    bsz, seq, d = h.shape
    t = h.reshape(bsz * seq, d)
    logits = (t @ w_r + b_r).astype(jnp.float32)
    top_v, top_i = lax.top_k(logits, TOP_K)
    top_w = jax.nn.softmax(top_v, axis=-1)
    comb = jnp.sum(jax.nn.one_hot(top_i, N_EXPERTS, dtype=jnp.float32) * top_w[..., None],
                   axis=1).astype(t.dtype)

    def body(e, acc):
        gu = t @ w_gu[e] + b_gu[e]
        g, u = jnp.split(gu, 2, axis=-1)
        g = jnp.minimum(g, SWIGLU_LIMIT)
        u = jnp.clip(u, -SWIGLU_LIMIT, SWIGLU_LIMIT)
        hdn = (u + 1.0) * (g * jax.nn.sigmoid(SWIGLU_ALPHA * g))
        y = hdn @ w_dn[e] + b_dn[e]
        return acc + comb[:, e][:, None] * y

    out = lax.fori_loop(0, N_EXPERTS, body, jnp.zeros_like(t))
    return out.reshape(bsz, seq, d)

def setup_inputs(seed: int = 0) -> dict:
    key = jax.random.key(seed)
    ks = iter(jax.random.split(key, 48))
    f32 = jnp.float32
    D = D_MODEL
    L = DEPTH

    def nrm(shape, scale):
        return jax.random.normal(next(ks), shape, f32) * scale

    def gain(shape):
        return 1.0 + nrm(shape, 0.02)

    return {
        'x': nrm((BATCH, SEQ, D), 1.0),
        'c': nrm((BATCH, D), 1.0),
        'norm1_g': gain((L, D)),
        'norm2_g': gain((L, D)),
        'w_ada': nrm((L, D, 6 * D), 0.5 * D ** -0.5),
        'b_ada': nrm((L, 6 * D), 0.01),
        'w_in': nrm((L, D, IN_COLS), D ** -0.5),
        'b_in': nrm((L, IN_COLS), 0.02),
        'q_norm_g': gain((L, ATT_HEAD_DIM)),
        'k_norm_g': gain((L, ATT_HEAD_DIM)),
        'lam_q1': nrm((L, ATT_HEAD_DIM), 0.1),
        'lam_k1': nrm((L, ATT_HEAD_DIM), 0.1),
        'lam_q2': nrm((L, ATT_HEAD_DIM), 0.1),
        'lam_k2': nrm((L, ATT_HEAD_DIM), 0.1),
        'subln_g': gain((L, ATT_V_DIM)),
        'hy_conv_w': nrm((L, HY_SHORT, HY_COLS), HY_SHORT ** -0.5),
        'hy_conv_b': nrm((L, HY_COLS), 0.02),
        'hf_w1': nrm((L, HY_EMB, HY_FILTER_HIDDEN), HY_EMB ** -0.5),
        'hf_b1': nrm((L, HY_FILTER_HIDDEN), 0.02),
        'hf_w2': nrm((L, HY_FILTER_HIDDEN, HY_FILTER_HIDDEN), HY_FILTER_HIDDEN ** -0.5),
        'hf_b2': nrm((L, HY_FILTER_HIDDEN), 0.02),
        'hf_w3': nrm((L, HY_FILTER_HIDDEN, HY_FILTER_HIDDEN), HY_FILTER_HIDDEN ** -0.5),
        'hf_b3': nrm((L, HY_FILTER_HIDDEN), 0.02),
        'hf_freq': gain((L, HY_FILTER_HIDDEN)),
        'hf_w4': nrm((L, HY_FILTER_HIDDEN, HY_ORDER * 2 * HY_WIDTH), 0.05 * HY_FILTER_HIDDEN ** -0.5),
        'hy_bias': nrm((L, HY_ORDER, HY_WIDTH), 0.5),
        'cf_dw_w': nrm((L, CF_KERNEL, CF_WIDTH), CF_KERNEL ** -0.5),
        'cf_dw_b': nrm((L, CF_WIDTH), 0.02),
        'cf_ln_g': gain((L, CF_WIDTH)),
        'cf_ln_b': nrm((L, CF_WIDTH), 0.02),
        'w_branch': nrm((L, N_BRANCH, BRANCH_WIDTH, D), BRANCH_WIDTH ** -0.5),
        'w_out': nrm((L, D, D), D ** -0.5),
        'w_router': nrm((L, D, N_EXPERTS), D ** -0.5),
        'b_router': nrm((L, N_EXPERTS), 0.01),
        'w_gu': nrm((L, N_EXPERTS, D, 2 * EXPERT_FF), D ** -0.5),
        'b_gu': nrm((L, N_EXPERTS, 2 * EXPERT_FF), 0.02),
        'w_down': nrm((L, N_EXPERTS, EXPERT_FF, D), EXPERT_FF ** -0.5),
        'b_down': nrm((L, N_EXPERTS, D), 0.02),
    }

def reference(x, c, norm1_g, norm2_g, w_ada, b_ada, w_in, b_in, q_norm_g, k_norm_g,
              lam_q1, lam_k1, lam_q2, lam_k2, subln_g, hy_conv_w, hy_conv_b,
              hf_w1, hf_b1, hf_w2, hf_b2, hf_w3, hf_b3, hf_freq, hf_w4, hy_bias,
              cf_dw_w, cf_dw_b, cf_ln_g, cf_ln_b, w_branch, w_out,
              w_router, b_router, w_gu, b_gu, w_down, b_down):
    bsz, seq, _ = x.shape
    cos, sin = rope_tables(seq, x.dtype)
    cond = jax.nn.silu(c)
    splits = np.cumsum([Q_COLS, K_COLS, V_COLS, HY_COLS, CF_COLS]).tolist()
    for l in range(DEPTH):
        mod = cond @ w_ada[l] + b_ada[l]
        sh1, sc1, g1, sh2, sc2, g2 = jnp.split(mod[:, None, :], 6, axis=-1)

        h = rmsnorm(x, norm1_g[l]) * (1.0 + sc1) + sh1
        proj = h @ w_in[l] + b_in[l]
        q, k, v, hy_in, cf_in, gates = jnp.split(proj, splits, axis=-1)

        q = q.reshape(bsz, seq, ATT_HEADS, 2, ATT_HEAD_DIM)
        k = k.reshape(bsz, seq, ATT_HEADS, 2, ATT_HEAD_DIM)
        v = v.reshape(bsz, seq, ATT_HEADS, ATT_V_DIM)
        q = apply_rope(rmsnorm(q, q_norm_g[l]), cos, sin)
        k = apply_rope(rmsnorm(k, k_norm_g[l]), cos, sin)
        lam_init = 0.8 - 0.6 * math.exp(-0.3 * l)
        lam = (jnp.exp(jnp.sum((lam_q1[l] * lam_k1[l]).astype(jnp.float32)))
               - jnp.exp(jnp.sum((lam_q2[l] * lam_k2[l]).astype(jnp.float32))) + lam_init)
        o_att = diff_attention(q, k, v, lam, lam_init, subln_g[l])

        filt = hyena_filters(seq, hf_w1[l], hf_b1[l], hf_w2[l], hf_b2[l], hf_w3[l], hf_b3[l],
                             hf_freq[l], hf_w4[l])
        o_hy = hyena_mixer(hy_in, hy_conv_w[l], hy_conv_b[l], filt, hy_bias[l])

        o_cf = conformer_conv(cf_in, cf_dw_w[l], cf_dw_b[l], cf_ln_g[l], cf_ln_b[l])

        br = jnp.stack([o_att, o_hy, o_cf], axis=2)
        gate = jax.nn.sigmoid(gates.reshape(bsz, seq, N_BRANCH, D_MODEL))
        merged = jnp.sum(jnp.einsum('bsnw,nwd->bsnd', br, w_branch[l]) * gate, axis=2)
        x = x + g1 * (merged @ w_out[l])

        h = rmsnorm(x, norm2_g[l]) * (1.0 + sc2) + sh2
        x = x + g2 * moe(h, w_router[l], b_router[l], w_gu[l], b_gu[l], w_down[l], b_down[l])
    return x


_drawn_inputs = setup_inputs


def setup_inputs(seed=0):
    import zlib

    import numpy as np

    out = dict(_drawn_inputs(seed))
    spreads = {}
    factors = {'norm1_g': 8.0,
     'norm2_g': 29.44,
     'b_ada': 2.977,
     'b_in': 4.292,
     'q_norm_g': 64.0,
     'k_norm_g': 64.0,
     'lam_q1': 200.0,
     'lam_k1': 2.705,
     'lam_q2': 39.008,
     'lam_k2': 23.432,
     'subln_g': 200.0,
     'hy_conv_b': 8.0,
     'hf_b1': 8.0,
     'hf_b2': 7.799,
     'hf_b3': 8.0,
     'hf_freq': 8.0,
     'cf_dw_b': 64.0,
     'cf_ln_g': 200.0,
     'cf_ln_b': 200.0,
     'b_router': 186.242,
     'b_gu': 64.0,
     'b_down': 200.0}
    for name, (base, spread) in spreads.items():
        noise = np.random.default_rng([zlib.crc32(name.encode()), seed]).standard_normal(out[name].shape)
        drawn = base * np.exp(spread * noise) if base else spread * noise
        out[name] = __import__('jax').numpy.asarray(drawn.astype(out[name].dtype))
    for name, factor in factors.items():
        out[name] = (out[name] * factor).astype(out[name].dtype)
    return out
```

```python
import math
from contextlib import ExitStack

import numpy as np
import concourse.bass as bass
from concourse import mybir

P = 128
D = 1024
SEQ = 256
TT = SEQ // P
KT = D // P
W = 512
WT = W // P
HEADS, HD = 4, 64
GROUPS = 2 * HEADS
HY_T = 3 * WT
BANDS, HF_EMB, HF_HID = 16, 33, 64
TAPS = 31
EXPERTS, TOPK, FF = 32, 4, 1024
EPS = 1e-6
LIMIT, ALPHA = 7.0, 1.702
LAM_INIT = 0.8 - 0.6 * math.exp(-0.3 * 0)
SCALE = HD ** -0.5

WEIGHT_SLOTS = 6
CHUNK = 4096

SLOTS = 64
PASSES = SEQ // SLOTS
PAIRS = EXPERTS // 2
BODIES = PAIRS // 2
PAIR_CHUNKS = 12
FAR = 4096.0

F32 = mybir.dt.float32
I32 = mybir.dt.int32
U32 = mybir.dt.uint32
ALU = mybir.AluOpType
ACT = mybir.ActivationFunctionType
AX_X = mybir.AxisListType.X

V_ADA, V_N1, V_BIN, V_SUB, V_DWB, V_LNG, V_LNB, V_C, V_HYB = 0, 16, 24, 68, 69, 73, 77, 81, 89

PI_A, PI_B, PI_C = 6.28125, 0.0019350051879882812, 3.0199159819e-07
ROUND = 12582912.0

HY_CHUNKS, CF_GATE, CF_VALUE, QKV_CHUNKS, GATE_CHUNKS = (3, 4, 5), 7, 6, (0, 1, 2), range(8, 14)


def front_jobs():
    jobs = [(f"mlp{i}", "dve") for i in range(3)]
    jobs += [(f"filter{o}{s}{t}", "dve") for o in range(2) for s in range(2) for t in range(TT)]
    jobs += [("ada0", "act"), ("ada1", "act")]
    jobs += [(f"spectrum0{j}", "act") for j in range(5)]
    jobs += [("ada2", "act"), ("ada3", "act")]
    jobs += [("xT0", "act"), ("xT2", "act"), ("modcol", "dve"), ("xT1", "dve"), ("xT3", "dve")]
    jobs += [("cg0", "act"), ("cg1", "act"), ("ca0", "dve"), ("ca1", "dve")]
    jobs += [(f"hy{i}", "act") for i in range(6)]
    jobs += [(f"spectrum1{j}", "act") for j in range(5)]
    jobs += [(f"hyT{g}{t}", "act") for g in range(3) for t in range(TT)]
    jobs += [(f"u0{m}", "dve") for m in (0, 2, 1, 3)] + [("mean", "dve"), ("q0", "dve"), ("q1", "dve")]
    jobs += [("inv00", "dve"), ("inv01", "dve"), ("var", "dve"), ("k0", "dve"), ("k1", "dve")]
    jobs += [(f"u1{m}", "dve") for m in (0, 2, 1, 3)] + [("v0", "dve"), ("v1", "dve")]
    jobs += [("inv10", "dve"), ("inv11", "dve"), ("gate0", "act"), ("zT0", "act"), ("zT1", "act")]
    jobs += [(f"qkT{j}{t}", "act") for j in range(2) for t in range(TT)]
    for h in range(HEADS + 1):
        if h < HEADS:
            jobs += [(f"score{h}{c}", "act") for c in range(2)]
        if h:
            jobs += [(f"gate{h}", "act"), (f"aT{h - 1}", "act"), (f"o{h - 1}", "dve")]
    jobs += [("gate5", "act"), ("gate6", "act"), ("oT0", "act"), ("oT1", "act")]
    jobs += [(f"gate{i}", "act") for i in range(7, 12)]
    jobs += [(f"merge{n}{m}", "dve") for n in (0, 1) for m in range(4)]
    jobs += [(f"adab{i}", "act") for i in range(8)]
    jobs += [(f"merge2{m}", "dve") for m in range(4)]
    jobs += [(f"out{t}{c}", "dve") for t in range(TT) for c in range(2)]
    jobs += [(f"h2T{i}", "act") for i in range(4)] + [("logits", "dve"), ("rank", "dve")]
    return jobs


JOBS = front_jobs()
JOB = {name: n for n, (name, _) in enumerate(JOBS)}
EMPTIED_BY = dict(JOBS)
ORDINAL = {}
for _e in ("act", "dve"):
    for _n, _name in enumerate(n for n, e in JOBS if e == _e):
        ORDINAL[_name] = _n + 1

CHUNKS = [("ada", i, f"ada{i}") for i in range(4)]
CHUNKS += [("in", CF_GATE, "cg1"), ("in", CF_VALUE, "ca1")]
CHUNKS += [("in", c, f"hy{2 * i + 1}") for i, c in enumerate(HY_CHUNKS)]
CHUNKS += [("in", 0, "q1"), ("in", 1, "k1"), ("in", 2, "v1")]
_gates = [("in", c, f"gate{2 * i + 1}") for i, c in enumerate(GATE_CHUNKS)]
_ada = [("ada", 4 + i, i + 1) for i in range(8)]
_branch = [("branch", n, f"merge{n}3") for n in range(3)]
CHUNKS += _gates[0:4] + _ada[0:2] + _gates[4:5] + _ada[2:4] + _gates[5:6] + _ada[4:6]
CHUNKS += _branch[0:1] + _ada[6:7] + _branch[1:2] + _ada[7:8] + _branch[2:3]
CHUNKS += [("wout", i, "out11") for i in range(2)]
CHUNK_NO = {(kind, i): n for n, (kind, i, _) in enumerate(CHUNKS)}
NF = len(CHUNKS)

MISC = [(f"gather{i}", "act") for i in range(4)]
MISC += [("turn_a", "act"), ("hidT_a0", "act"), ("hidT_a1", "act")]
MISC += [(f"add_a{i}", "dve") for i in range(4)]
MISC += [("turn_b", "act"), ("hidT_b0", "act"), ("hidT_b1", "act")]
MISC += [(f"add_b{i}", "dve") for i in range(4)]
MISC_NO = {name: n for n, (name, _) in enumerate(MISC)}
MISC_BY = dict(MISC)
MISC_ORD = {}
MISC_COUNT = {}
for _e in ("act", "dve"):
    _names = [n for n, e in MISC if e == _e]
    MISC_COUNT[_e] = len(_names)
    for _n, _name in enumerate(_names):
        MISC_ORD[_name] = _n + 1


class Steps:

    def __init__(self, eng, sem):
        self.eng, self.sem, self.n = eng, sem, 0

    def __call__(self, instruction):
        instruction.then_inc(self.sem, 1)
        self.n += 1
        return self.n

    def wait(self, n=None):
        self.eng.wait_ge(self.sem, self.n if n is None else n)


class LoopSteps:

    def __init__(self, eng, sem, before):
        self.eng, self.sem, self.before, self.n = eng, sem, before, 0

    def __call__(self, instruction):
        instruction.then_inc(self.sem, 1)
        self.n += 1

    def wait(self):
        self.eng.wait_ge(self.sem, self.before + self.n)


BODY_STEPS = 4 + 3


def build_layer(nc, a, out):
    ctx = ExitStack()
    with ctx:
        def sb(name, shape, dt=F32):
            return ctx.enter_context(nc.sbuf_tensor(f"{name}_sb", shape, dt))

        def sem(name):
            return ctx.enter_context(nc.semaphore(name))

        bank = [ctx.enter_context(nc.psum_tensor(f"bank{i}", [P, 512], F32)) for i in range(8)]

        ring = sb("ring", [P, WEIGHT_SLOTS, CHUNK])
        ident = sb("ident", [P, P])
        ones = sb("ones", [P, P])
        vec = sb("vec", [P, 3, P])
        small = sb("small", [P, 256])
        area_h = sb("area_h", [P, 2048])
        area_1 = sb("area_1", [P, 4096])
        area_2 = sb("area_2", [P, 5120])
        area_3 = sb("area_3", [P, 4096])
        area_4 = sb("area_4", [P, 2048])
        area_5 = sb("area_5", [P, 2176])
        area_6 = sb("area_6", [P, 3072])
        area_7 = sb("area_7", [P, 2560])
        area_8 = sb("area_8", [P, 1024])
        rope = sb("rope", [P, 2, TT, HD])
        head_rows = sb("head_rows", [P, 6 * HD])
        gain = head_rows[:, 0:2 * HD].rearrange("p (n d) -> p n d", d=HD)
        lam_v = head_rows[:, 2 * HD:].rearrange("p (n d) -> p n d", d=HD)
        pos = sb("pos", [P, TT, EXPERTS + 4])
        comb = sb("comb", [P, TT, EXPERTS + 4])
        iota = sb("iota", [P, SLOTS])
        before = sb("before", [P, P])
        row_sel = sb("row_sel", [2, P])
        flag = sb("flag", [P, 1], I32)

        def view(area, start, shape):
            n = math.prod(shape)
            v = area[:, start:start + n]
            if len(shape) == 1:
                return v
            names = "abcd"[:len(shape)]
            return v.rearrange(f"p ({' '.join(names)}) -> p {' '.join(names)}",
                               **dict(zip(names[1:], shape[1:])))

        hT = view(area_h, 0, [KT, SEQ])
        merged = hT
        w4 = view(area_1, 0, [2, 2, W])
        w4s = view(area_4, 0, [2, 2, W])
        x_n = view(area_2, 2560, [TT, D])
        hy_in = view(area_1, 0, [HY_T, SEQ + 2])
        hy_cv = view(area_6, 0, [HY_T, SEQ])
        dft_f = view(area_7, 0, [TT, 768])
        dft_i = view(area_7, 1536, [4, SEQ])
        gates = [view(area_7, 0, [KT, SEQ]), view(area_1, 0, [KT, SEQ]), view(area_1, 2048, [KT, SEQ])]
        w_router = view(area_7, 2048, [KT, EXPERTS])
        spectra = view(area_2, 0, [2, 5, W])
        mod_rows = view(area_2, 0, [4, D])
        g1, sh2, sc2, g2 = (mod_rows[:, i, :] for i in range(4))
        filt = view(area_3, 0, [TT, 2, 2, W])
        hy = view(area_3, 0, [3, TT, W])
        hy_tmp = view(area_3, 3072, [2, W])
        qkT = view(area_3, 0, [2, HEADS, SEQ])
        prob = view(area_3, 2048, [2, 2, TT, SEQ])
        part = view(area_4, 0, [4, 512])
        ysp = view(area_4, 0, [4, W])
        br_hy = view(area_4, 0, [WT, SEQ])
        br_at = view(area_4, 1024, [WT, SEQ])
        window = view(area_6, 512, [TT, W])
        x = view(area_5, 0, [TT, D])
        cf_in = view(area_5, 0, [WT, SEQ + TAPS - 1])
        cf_cv = view(area_5, WT * (SEQ + TAPS - 1), [4, SEQ])
        cf_sq = view(area_5, 0, [WT, SEQ])
        ln_ms, ln_rt, ln_r, ln_t = (area_5[:, i * SEQ:(i + 1) * SEQ] for i in range(4))
        attT = view(area_5, 0, [2, TT, SEQ])
        att = view(area_5, 1024, [TT, W])
        qkv = view(area_6, 0, [3, TT, W])
        xT = view(area_1, 0, [KT, 4 * SLOTS])
        hid = view(area_1, 2048, [FF])
        gate_s = view(area_1, 3072, [FF])
        up_s = view(area_7, 0, [FF])
        sig_s = view(area_7, 1024, [FF])
        h2 = view(area_3, 0, [TT, D])
        total = view(area_3, 2048, [TT, D])
        h2T = hT
        hidT = view(area_4, 0, [KT, P])
        y_s = view(area_4, 1024, [D])
        bias = area_6
        member = view(area_7, 2048, [TT, 4, SLOTS])
        weighted = view(area_8, 0, [TT, 4, SLOTS])
        turned = view(area_8, 512, [SEQ])
        scratch = view(area_6, 2048, [D])

        cond, cond_sig = small[:, 0:8], small[:, 8:16]
        n1_gain = small[:, 16:24]
        shift1 = small[:, 24:32]
        x_ss, x_ms, x_rt, x_r, x_t = (small[:, 32 + 2 * i:34 + 2 * i] for i in range(5))
        lam_s = small[:, 42:48]
        s_max = small[:, 52:68].rearrange("p (h c t) -> p h c t", c=2, t=TT)
        s_sum = small[:, 68:84].rearrange("p (h c t) -> p h c t", c=2, t=TT)
        s_inv = small[:, 84:100].rearrange("p (h c t) -> p h c t", c=2, t=TT)
        o_ms, o_rt, o_r, o_t = (small[:, 100 + 16 * i:116 + 16 * i] for i in range(4))
        top = small[:, 164:180].rearrange("p (t k) -> p t k", t=TT)
        top_w = small[:, 180:188].rearrange("p (t k) -> p t k", t=TT)
        top_s = small[:, 188:194].rearrange("p (t k) -> p t k", t=TT)
        g2_ss, g2_ms, g2_rt, g2_r, g2_t = (small[:, 196 + 2 * i:198 + 2 * i] for i in range(5))
        most = small[:, 206:207]
        mean_col = small[:, 208:210]
        sub_gain = small[:, 210:211]
        o_sel = sb("o_sel", [P, 24])
        top_i = sb("top_i", [P, TT, 8], U32)
        top_f = sb("top_f", [P, TT, 8])
        mask = sb("mask", [P, TT, EXPERTS])
        logit = sb("logit", [P, TT, EXPERTS])
        expert_no = sb("expert_no", [P, EXPERTS])
        b_router = sb("b_router", [P, EXPERTS])
        
        cond_rep = view(area_h, 1472, [KT, 32])
        mlp_y = view(area_h, 0, [4, SEQ])[0:HF_HID]
        mlp_all = area_1[0:HF_HID, 0:2048 + SEQ + 3 * HF_HID + 4]
        zT = area_1[0:HF_EMB, 2048:2048 + SEQ]
        mlp_w = area_1[0:HF_HID, 2304:2304 + 3 * HF_HID].rearrange("p (n m) -> p n m", n=3)
        hf_col = area_1[0:HF_HID, 2496:2500]
        qk_ss = sb("qk_ss", [P, 5, 2, GROUPS])
        hy_bias = view(area_8, 0, [2, W])
        br_cf = view(area_8, 0, [WT, SEQ])

        products_ready = sem("products_ready")
        emptied = {"act": sem("emptied_by_act"), "dve": sem("emptied_by_dve")}
        slot_landed = [sem(f"slot_landed{i}") for i in range(WEIGHT_SLOTS)]
        ada_summed = sem("ada_summed")
        consts_made = sem("consts_made")
        vec_landed = sem("vec_landed")
        mlp_landed = sem("mlp_landed")
        x_landed = sem("x_landed")
        x_again_landed = sem("x_again_landed")
        window_landed = sem("window_landed")
        dft_landed = sem("dft_landed")
        hyena_landed = sem("hyena_landed")
        attn_landed = sem("attn_landed")
        router_landed = sem("router_landed")
        mod_bias_landed = sem("mod_bias_landed")
        gain2_landed = sem("gain2_landed")
        total_zeroed = sem("total_zeroed")
        dve_step = sem("dve_step")
        act_step = sem("act_step")
        pool_step = sem("pool_step")
        sqrt_asked = sem("sqrt_asked")
        sqrt_done = sem("sqrt_done")
        sin_asked = sem("sin_asked")
        sin_done = sem("sin_done")
        w4_summed = sem("w4_summed")
        cond_ready = sem("cond_ready")
        xn_ready = sem("xn_ready")
        x_squared = sem("x_squared")
        r_ready = sem("r_ready")
        modcol_ready = sem("modcol_ready")
        hy_conv_done = sem("hy_conv_done")
        pads_zeroed = sem("pads_zeroed")
        sig_ready = sem("sig_ready")
        spectra_mixed = sem("spectra_mixed")
        z_ready = sem("z_ready")
        conv_done = sem("conv_done")
        centred = sem("centred")
        cf_scaled = sem("cf_scaled")
        cf_act = sem("cf_act")
        br_cf_ready = sem("br_cf_ready")
        roped = sem("roped")
        max_ready = sem("max_ready")
        lam_ready = sem("lam_ready")
        lam_exp = sem("lam_exp")
        att_ready = sem("att_ready")
        o_ready = sem("o_ready")
        gates_ready = sem("gates_ready")
        mod_zeroed = sem("mod_zeroed")
        merged_ready = sem("merged_ready")
        h2_ready = sem("h2_ready")
        top_ready = sem("top_ready")
        top_exp = sem("top_exp")
        mask_ready = sem("mask_ready")
        flag_ready = sem("flag_ready")
        stored = sem("stored")
        out_ready = sem("out_ready")
        weights_used = sem("weights_used")
        gate_up_done = sem("gate_up_done")
        gate_up_read = sem("gate_up_read")
        y_done = sem("y_done")
        y_read = sem("y_read")
        misc_done = sem("misc_done")
        misc_out = {"act": sem("misc_out_act"), "dve": sem("misc_out_dve")}
        bias_landed = sem("bias_landed")
        bias_used = sem("bias_used")
        gate_min = sem("gate_min")
        sigmoid_done = sem("sigmoid_done")
        hid_ready = sem("hid_ready")
        member_ready = sem("member_ready")
        moe_step = sem("moe_step")
        moe_primed = sem("moe_primed")
        pass_step = sem("pass_step")

        def slot_of(kind, i):
            return ring[:, CHUNK_NO[kind, i] % WEIGHT_SLOTS, :]

        def wait_chunk(eng, kind, i):
            n = CHUNK_NO[kind, i]
            eng.wait_ge(slot_landed[n % WEIGHT_SLOTS], 16 * (n // WEIGHT_SLOTS + 1))

        def wait_emptied(eng, name):
            eng.wait_ge(emptied[EMPTIED_BY[name]], ORDINAL[name])

        def open_bank(pe, name):
            n = JOB[name]
            if n >= 8:
                wait_emptied(pe, JOBS[n - 8][0])
            return bank[n % 8]

        def product(eng, name):
            eng.wait_ge(products_ready, JOB[name] + 1)
            return bank[JOB[name] % 8]

        def chunk_source(kind, i):
            if kind == "ada":
                return a["w_ada"][0, :, i * W:(i + 1) * W].rearrange("(k p) m -> p k m", p=P)
            if kind == "in":
                return a["w_in"][0, :, i * W:(i + 1) * W].rearrange("(k p) m -> p k m", p=P)
            if kind == "branch":
                return a["w_branch"][0, i].rearrange("(k p) m -> p k m", p=P)
            return a["w_out"][0, i * W:(i + 1) * W, :].rearrange("(k p) m -> p k m", p=P)

        def slot_view(kind, i):
            cols = W if kind in ("ada", "in") else D
            return slot_of(kind, i).rearrange("p (k m) -> p k m", m=cols)

        def moe_slot(b, c):
            return ring[:, (NF + PAIR_CHUNKS * b + c) % WEIGHT_SLOTS, :]

        def wait_moe_chunk(eng, i, b, c):
            m = NF + PAIR_CHUNKS * b + c
            per_body = 2 * PAIR_CHUNKS // WEIGHT_SLOTS
            eng.wait_ge(slot_landed[m % WEIGHT_SLOTS],
                        i * (16 * per_body) + 16 * (m // WEIGHT_SLOTS + 1))

        def moe_bank(name):
            return bank[6 + MISC_NO[name] % 2]

        def open_misc(pe, i, name):
            n = MISC_NO[name]
            prev = MISC[n - 2][0]
            by = MISC_BY[prev]
            body = 1 if n >= 2 else 0
            pe.wait_ge(misc_out[by], i * MISC_COUNT[by] + body * MISC_COUNT[by] + MISC_ORD[prev])
            return moe_bank(name)

        def misc_product(eng, i, name):
            eng.wait_ge(misc_done, i * len(MISC) + MISC_NO[name] + 1)
            return moe_bank(name)

        def wait_misc_out(pe, i, name):
            by = MISC_BY[name]
            pe.wait_ge(misc_out[by], i * MISC_COUNT[by] + MISC_COUNT[by] + MISC_ORD[name])

        block = ctx.enter_context(nc.Block())

        @block.sync
        def _(sp):
            sp.dma_start(vec[:, :, :], a["columns"].rearrange("p (i j) -> p i j", j=P)).then_inc(vec_landed, 16)
            sp.dma_start(mlp_all, a["filter_net"]).then_inc(mlp_landed, 16)

            def load_chunk(n):
                kind, i, _ = CHUNKS[n]
                if n >= WEIGHT_SLOTS:
                    wait_freed(n - WEIGHT_SLOTS)
                sp.dma_start(slot_view(kind, i), chunk_source(kind, i))\
                    .then_inc(slot_landed[n % WEIGHT_SLOTS], 16)

            def wait_freed(n):
                user = CHUNKS[n][2]
                if isinstance(user, str):
                    sp.wait_ge(products_ready, JOB[user] + 1)
                else:
                    sp.wait_ge(ada_summed, user)

            load_chunk(0)
            sp.dma_start(window, a["window"].rearrange("(t p) m -> p t m", p=P)).then_inc(window_landed, 16)
            sp.dma_start(x[:, :, :], a["x"][0].rearrange("(t p) m -> p t m", p=P)).then_inc(x_landed, 16)
            load_chunk(1)
            sp.dma_start(dft_f, a["dft_f"].rearrange("(t p) m -> p t m", p=P)).then_inc(dft_landed, 16)
            load_chunk(2)
            load_chunk(3)
            sp.dma_start(dft_i, a["dft_i"].rearrange("(t p) m -> p t m", p=P)).then_inc(hyena_landed, 16)
            sp.dma_start(hy_bias, a["hy_bias"][0:1].to_broadcast([P, 2, W])).then_inc(hyena_landed, 16)
            for n in range(4, NF):
                load_chunk(n)

            def load_moe(i, b, c, j, first=False):
                if first:
                    wait_freed(NF + c - WEIGHT_SLOTS)
                elif c == 0:
                    sp.wait_ge(weights_used, i * 20 + 10 * b - 10 + 7)
                elif c == 1:
                    sp.wait_ge(gate_up_done, i * 4 + 2 * b)
                elif c < 5:
                    sp.wait_ge(weights_used, i * 20 + 10 * b - 10 + 6 + c)
                elif c == 5:
                    sp.wait_ge(y_done, i * 4 + 2 * b)
                else:
                    sp.wait_ge(weights_used, i * 20 + 10 * b + c - 5)
                e0 = j * 4 + 2 * b
                m = NF + PAIR_CHUNKS * b + c
                if c < 8:
                    src = a["w_gu"][0, bass.ds(e0, 2), c * P:(c + 1) * P, :].rearrange("e p m -> p e m")
                    dst = moe_slot(b, c).rearrange("p (e m) -> p e m", e=2)
                    sp.dma_start(dst, src).then_inc(slot_landed[m % WEIGHT_SLOTS], 16)
                else:
                    k = 2 * (c - 8)
                    dst = moe_slot(b, c).rearrange("p (e m) -> p e m", e=2)
                    src = a["w_down"][0, bass.ds(e0, 2), k * P:(k + 2) * P, :]\
                        .rearrange("e (p k) m -> p e (k m)", k=2)
                    sp.dma_start(dst, src).then_inc(slot_landed[m % WEIGHT_SLOTS], 16)

            def load_bias(i, b, j):
                e0 = j * 4 + 2 * b
                sp.dma_start(bias[0:2, :], a["b_experts"][bass.ds(e0, 2), :]).then_inc(bias_landed, 16)

            def body(i, j, last):
                for b in range(2):
                    for c in range(6, PAIR_CHUNKS):
                        load_moe(i, b, c, j)
                    if not (last and b == 1):
                        for c in range(6):
                            load_moe(i, b + 1, c, j)
                            if c == 2:
                                sp.wait_ge(bias_used, i * 2 + b + 1)
                                load_bias(i, b + 1, j)

            def one_pass(p, first=False):
                i0 = p * BODIES
                for c in range(6):
                    load_moe(i0, 0, c, 0, first=first)
                if first:
                    sp.wait_ge(h2_ready, TT)
                else:
                    sp.wait_ge(bias_used, p * (2 * BODIES))
                load_bias(i0, 0, 0)
                with sp.Fori(0, BODIES - 1) as j:
                    body(i0 + j, j, False)
                body(i0 + (BODIES - 1), BODIES - 1, True)

            one_pass(0, first=True)
            sp.wait_ge(flag_ready, 1)
            over = sp.value_load(flag[0:1, 0:1], min_val=0, max_val=SEQ)
            with sp.If(over > SLOTS):
                with sp.Fori(1, PASSES) as p:
                    one_pass(p)

            for t in range(TT):
                sp.wait_ge(out_ready, t + 1)
                sp.dma_start(out[0, t * P:(t + 1) * P, :], total[:, t, :]).then_inc(stored, 16)
            sp.wait_ge(stored, 16 * TT)

        @block.gpsimd
        def _(pool):
            step = Steps(pool, pool_step)
            step(pool.memset(ident[:, :], 0.0))
            step(pool.memset(before[:, :], 1.0))
            step(pool.memset(row_sel[:, :], 1.0))
            step.wait()
            step(pool.affine_select(out=ident[:, :], in_=ident[:, :], compare_op=ALU.not_equal, fill=1.0,
                                    base=0, pattern=[[-1, P]], channel_multiplier=1))
            step(pool.affine_select(out=before[:, :], in_=before[:, :], compare_op=ALU.is_gt, fill=0.0,
                                    base=0, pattern=[[1, P]], channel_multiplier=-1))
            step(pool.affine_select(out=row_sel[:, :], in_=row_sel[:, :], compare_op=ALU.is_ge, fill=0.0,
                                    base=0, pattern=[[1, P]], channel_multiplier=-SLOTS))
            step.wait()
            step(pool.affine_select(out=row_sel[:, :], in_=row_sel[:, :], compare_op=ALU.is_ge, fill=0.0,
                                    base=SLOTS - 1, pattern=[[-1, P]], channel_multiplier=SLOTS))
            step(pool.iota(iota[:, :], pattern=[[1, SLOTS]], base=0, channel_multiplier=0,
                           allow_small_or_imprecise_dtypes=True))
            step(pool.iota(expert_no[:, :], pattern=[[1, EXPERTS]], base=0, channel_multiplier=0,
                           allow_small_or_imprecise_dtypes=True))
            step(pool.memset(ones[:, :], 1.0))
            step(pool.memset(pos[:, :, :], FAR))
            step(pool.memset(comb[:, :, :], 0.0))
            step.wait()
            pool.memset(mean_col, 1.0 / 32).then_inc(consts_made, 1)
            pool.wait_ge(products_ready, JOB["hyT21"] + 1)
            for t in range(TT):
                pool.dma_start(qkv[:, :, t, :], a["b_in"][0:1, 0:3 * W].rearrange("o (j m) -> o j m", m=W)
                               .to_broadcast([P, 3, W])).then_inc(attn_landed, 16)
            pool.dma_start(rope[:, :, :, :], a["rope"].rearrange("c (t p) m -> p c t m", p=P)).then_inc(attn_landed, 16)
            pool.dma_start(head_rows[:, :], a["head_rows"].to_broadcast([P, 6 * HD])).then_inc(attn_landed, 16)
            pool.wait_ge(products_ready, JOB["inv11"] + 1)
            pool.dma_start(w_router[:, :, :], a["w_router"][0].rearrange("(k p) m -> p k m", p=P)).then_inc(router_landed, 16)
            pool.dma_start(b_router[:, :], a["b_router"].to_broadcast([P, EXPERTS])).then_inc(router_landed, 16)
            pool.wait_ge(spectra_mixed, 4)
            pool.memset(mod_rows[:, :, :], 0.0).then_inc(mod_zeroed, 1)
            pool.wait_ge(mod_zeroed, 1)
            pool.dma_start(area_2[0:1, 0:4 * D], a["b_ada"][0:1, 2 * D:6 * D]).then_inc(mod_bias_landed, 16)
            pool.wait_ge(products_ready, JOB["oT1"] + 1)
            pool.dma_start(x[:, :, :], a["x"][0].rearrange("(t p) m -> p t m", p=P)).then_inc(x_again_landed, 16)
            pool.dma_start(scratch, a["norm2_g"].to_broadcast([P, D])).then_inc(gain2_landed, 16)
            pool.wait_ge(h2_ready, TT)
            pool.memset(total, 0.0).then_inc(total_zeroed, 1)

        @block.tensor
        def _(pe):
            def job(name):
                return open_bank(pe, name)

            def end(ins):
                ins.then_inc(products_ready, 1)

            pe.wait_ge(consts_made, 1)
            pe.wait_ge(mlp_landed, 16)
            b = job("mlp0")
            end(pe.matmul(b[0:HF_HID, 0:SEQ], mlp_w[0:HF_EMB, 0, :], zT[:, :], start=True, stop=True))
            for n in (1, 2):
                b = job(f"mlp{n}")
                pe.wait_ge(sin_done, n)
                end(pe.matmul(b[0:HF_HID, 0:SEQ], mlp_w[:, n, :], mlp_y[:, 3, :], start=True, stop=True))
            pe.wait_ge(sin_done, 3)
            pe.wait_ge(w4_summed, 1)
            for o in range(2):
                for s in range(2):
                    for t in range(TT):
                        b = job(f"filter{o}{s}{t}")
                        end(pe.matmul(b[:, :], mlp_y[:, 3, t * P:(t + 1) * P], w4s[0:HF_HID, o, s, :],
                                      start=True, stop=True))

            def ada(i):
                b = job(f"ada{i}")
                w = slot_view("ada", i)
                pe.wait_ge(cond_ready, 1)
                wait_chunk(pe, "ada", i)
                for k in range(KT):
                    g = k % 4
                    ins = pe.matmul(b[32 * g:32 * g + 32, :], cond_rep[:, k, :], w[:, k, :],
                                    start=k < 4, stop=k >= 4, skip_group_check=True)
                end(ins)

            def spectrum(o):
                parts = [(0, 0), (P, 0), (512, 0), (640, 1), (384, 1)]
                for j, (col, s) in enumerate(parts):
                    b = job(f"spectrum{o}{j}")
                    for t in range(TT):
                        ins = pe.matmul(b[:, :], dft_f[:, t, col:col + P], filt[:, t, o, s, :],
                                        start=t == 0, stop=t == TT - 1)
                    end(ins)

            ada(0)
            ada(1)
            pe.wait_ge(dft_landed, 16)
            wait_emptied(pe, "filter011")
            spectrum(0)
            ada(2)
            ada(3)
            pe.wait_ge(xn_ready, TT)

            def turn_x(i):
                b = job(f"xT{i}")
                for kk in range(2):
                    for t in range(TT):
                        c = (2 * i + kk) * P
                        ins = pe.transpose(b[:, (kk * TT + t) * P:(kk * TT + t + 1) * P],
                                           x_n[:, t, c:c + P], ident[:, :])
                end(ins)

            turn_x(0)
            turn_x(2)
            b = job("modcol")
            for i in range(4):
                wait_emptied(pe, f"ada{i}")
                for m in range(4):
                    c = 4 * i + m
                    ins = pe.matmul(b[:, c:c + 1], part[:, i, m * P:(m + 1) * P], mean_col[:, 0:1],
                                    start=True, stop=True)
            end(ins)
            turn_x(1)
            turn_x(3)

            def channel_major(name, kind, i, m0):
                b = job(name)
                w = slot_view(kind, i)
                wait_chunk(pe, kind, i)
                for m in range(2):
                    for k in range(KT):
                        ins = pe.matmul(b[:, m * SEQ:(m + 1) * SEQ], w[:, k, (m0 + m) * P:(m0 + m + 1) * P],
                                        hT[:, k, :], start=k == 0, stop=k == KT - 1)
                end(ins)

            def token_major(name, i, t):
                b = job(name)
                w = slot_view("in", i)
                wait_chunk(pe, "in", i)
                for k in range(KT):
                    ins = pe.matmul(b[:, :], hT[:, k, t * P:(t + 1) * P], w[:, k, :],
                                    start=k == 0, stop=k == KT - 1)
                end(ins)

            wait_emptied(pe, "xT2")
            wait_emptied(pe, "xT3")
            for i in range(2):
                channel_major(f"cg{i}", "in", CF_GATE, 2 * i)
            for i in range(2):
                channel_major(f"ca{i}", "in", CF_VALUE, 2 * i)
            for i in range(6):
                channel_major(f"hy{i}", "in", HY_CHUNKS[i // 2], 2 * (i % 2))
            wait_emptied(pe, "filter111")
            spectrum(1)

            for g in range(3):
                pe.wait_ge(hy_conv_done, WT * (g + 1))
                for t in range(TT):
                    b = job(f"hyT{g}{t}")
                    for m in range(WT):
                        ins = pe.transpose(b[:, m * P:(m + 1) * P],
                                           hy_cv[:, g * WT + m, t * P:(t + 1) * P], ident[:, :])
                    end(ins)

            def to_frequency(o):
                for m in (0, 2, 1, 3):
                    b = job(f"u{o}{m}")
                    for t in range(TT):
                        ins = pe.matmul(b[:, :], dft_f[:, t, m * P:(m + 1) * P], hy[:, 0, t, :],
                                        start=t == 0, stop=t == TT - 1)
                    end(ins)

            def to_time(o):
                pe.wait_ge(spectra_mixed, 2 * o + 2)
                for t in range(TT):
                    b = job(f"inv{o}{t}")
                    for m in range(4):
                        ins = pe.matmul(b[:, :], dft_i[:, m, t * P:(t + 1) * P], ysp[:, m, :],
                                        start=m == 0, stop=m == 3)
                    end(ins)

            wait_emptied(pe, "hyT01")
            to_frequency(0)
            b = job("mean")
            pe.wait_ge(conv_done, 1)
            for m in range(WT):
                ins = pe.matmul(b[:, 0:SEQ], ones[:, :], cf_cv[:, m, :], start=m == 0, stop=m == WT - 1)
            end(ins)
            for t in range(TT):
                token_major(f"q{t}", 0, t)
            pe.wait_ge(hyena_landed, 32)
            to_time(0)
            b = job("var")
            pe.wait_ge(centred, 1)
            for m in range(WT):
                ins = pe.matmul(b[:, 0:SEQ], ones[:, :], cf_sq[:, m, :], start=m == 0, stop=m == WT - 1)
            end(ins)
            for t in range(TT):
                token_major(f"k{t}", 1, t)
            pe.wait_ge(z_ready, TT)
            to_frequency(1)
            for t in range(TT):
                token_major(f"v{t}", 2, t)
            to_time(1)

            def gate(i):
                channel_major(f"gate{i}", "in", GATE_CHUNKS[i // 2], 2 * (i % 2))

            gate(0)
            pe.wait_ge(z_ready, 2 * TT)
            for i in range(2):
                b = job(f"zT{i}")
                for m in range(2):
                    for t in range(TT):
                        c = (2 * i + m) * P
                        ins = pe.transpose(b[:, (m * TT + t) * P:(m * TT + t + 1) * P],
                                           hy[:, 0, t, c:c + P], ident[:, :])
                end(ins)
            for j in range(2):
                for t in range(TT):
                    b = job(f"qkT{j}{t}")
                    pe.wait_ge(roped, TT * j + t + 1)
                    for h in range(HEADS):
                        ins = pe.transpose(b[:, h * P:(h + 1) * P], qkv[:, j, t, h * P:(h + 1) * P], ident[:, :])
                    end(ins)
            wait_emptied(pe, "qkT11")

            def scores(h):
                for c in range(2):
                    b = job(f"score{h}{c}")
                    r = slice(c * HD, (c + 1) * HD)
                    for t in range(TT):
                        ins = pe.matmul(b[:, t * SEQ:(t + 1) * SEQ], qkT[r, 0, h, t * P:(t + 1) * P],
                                        qkT[r, 1, h, :], start=True, stop=True)
                    end(ins)

            def turn_weights(h):
                b = job(f"aT{h}")
                pe.wait_ge(att_ready, h + 1)
                for kt in range(TT):
                    for t in range(TT):
                        ins = pe.transpose(b[:, kt * SEQ + t * P:kt * SEQ + (t + 1) * P],
                                           prob[:, h % 2, 0, t, kt * P:(kt + 1) * P], ident[:, :])
                end(ins)

            def attend(h):
                b = job(f"o{h}")
                wait_emptied(pe, f"aT{h}")
                wait_emptied(pe, "v1")
                for t in range(TT):
                    for kt in range(TT):
                        ins = pe.matmul(b[:, t * P:(t + 1) * P], attT[:, h % 2, kt, t * P:(t + 1) * P],
                                        qkv[:, 2, kt, h * P:(h + 1) * P], start=kt == 0, stop=kt == TT - 1)
                end(ins)

            for h in range(HEADS + 1):
                if h < HEADS:
                    scores(h)
                if h:
                    gate(h)
                    turn_weights(h - 1)
                    attend(h - 1)
            gate(5)
            gate(6)
            pe.wait_ge(o_ready, 1)
            for i in range(2):
                b = job(f"oT{i}")
                for m in range(2):
                    for t in range(TT):
                        c = (2 * i + m) * P
                        ins = pe.transpose(b[:, (m * TT + t) * P:(m * TT + t + 1) * P],
                                           att[:, t, c:c + P], ident[:, :])
                end(ins)
            for i in range(7, 12):
                gate(i)

            def ada_rows(i):
                b = job(f"adab{i}")
                pe.wait_ge(ada_summed, i + 1)
                end(pe.matmul(b[:, :], ones[:, :], area_2[:, i * W:(i + 1) * W], start=True, stop=True))

            def merge(n, branch):
                w = slot_view("branch", n)
                wait_chunk(pe, "branch", n)
                for mp in range(4):
                    b = job(f"merge{n}{mp}")
                    for m in range(2):
                        c = (2 * mp + m) * P
                        for k in range(WT):
                            ins = pe.matmul(b[:, m * SEQ:(m + 1) * SEQ], w[:, k, c:c + P],
                                            branch[:, k, :], start=k == 0, stop=k == WT - 1)
                    end(ins)

            wait_emptied(pe, "oT1")
            merge(0, br_at)
            wait_emptied(pe, "zT1")
            merge(1, br_hy)
            for i in range(8):
                ada_rows(i)
            pe.wait_ge(br_cf_ready, 1)
            merge(2, br_cf)
            for i in range(2):
                wait_chunk(pe, "wout", i)
            pe.wait_ge(merged_ready, 4)
            for t in range(TT):
                for c in range(2):
                    b = job(f"out{t}{c}")
                    for k in range(KT):
                        w = slot_view("wout", k // WT)
                        ins = pe.matmul(b[:, :], merged[:, k, t * P:(t + 1) * P],
                                        w[:, k % WT, c * W:(c + 1) * W], start=k == 0, stop=k == KT - 1)
                    end(ins)
            for i in range(4):
                b = job(f"h2T{i}")
                pe.wait_ge(h2_ready, TT)
                for kk in range(2):
                    for t in range(TT):
                        c = (2 * i + kk) * P
                        ins = pe.transpose(b[:, (kk * TT + t) * P:(kk * TT + t + 1) * P],
                                           h2[:, t, c:c + P], ident[:, :])
                end(ins)
            b = job("logits")
            pe.wait_ge(router_landed, 32)
            wait_emptied(pe, "h2T3")
            for t in range(TT):
                for k in range(KT):
                    ins = pe.matmul(b[:, t * EXPERTS:(t + 1) * EXPERTS], h2T[:, k, t * P:(t + 1) * P],
                                    w_router[:, k, :], start=k == 0, stop=k == KT - 1)
            end(ins)
            b = job("rank")
            pe.wait_ge(mask_ready, 1)
            pe.matmul(b[:, 0:EXPERTS], before[:, :], mask[:, 0, :], start=True, stop=True)
            pe.matmul(b[:, EXPERTS:2 * EXPERTS], before[:, :], mask[:, 1, :], start=True, stop=False)
            pe.matmul(b[:, EXPERTS:2 * EXPERTS], ones[:, :], mask[:, 0, :], start=False, stop=True)
            pe.matmul(b[:, 64:64 + EXPERTS], ones[:, :], mask[:, 0, :], start=True, stop=False)
            end(pe.matmul(b[:, 64:64 + EXPERTS], ones[:, :], mask[:, 1, :], start=False, stop=True))
            def misc_end(ins):
                ins.then_inc(misc_done, 1)

            def gate_up(i, b):
                pe.wait_ge(bias_landed, i * 32 + 16 * (b + 1))
                pe.wait_ge(gate_up_read, i * 4 + 4 + 2 * b)
                for n in range(4):
                    ins = pe.matmul(bank[n][:, :], row_sel[:, :], bias[0:2, n * 512:(n + 1) * 512],
                                    start=True, stop=False, skip_group_check=True)
                for k in range(KT):
                    wait_moe_chunk(pe, i, b, k)
                    w = moe_slot(b, k).rearrange("p (e m) -> p e m", e=2)
                    for n in (0, 2, 1, 3):
                        for e in range(2):
                            r = slice(e * SLOTS, (e + 1) * SLOTS)
                            c = b * 2 * SLOTS + e * SLOTS
                            ins = pe.matmul(bank[n][r, :], xT[:, k, c:c + SLOTS],
                                            w[:, e, n * 512:(n + 1) * 512],
                                            start=False, stop=k == KT - 1, skip_group_check=True)
                        if k == KT - 1 and n in (2, 3):
                            ins.then_inc(gate_up_done, 1)
                    if k < KT - 1:
                        ins.then_inc(weights_used, 1)

            def turn(i, name, b):
                o = open_misc(pe, i, name)
                for t in range(TT):
                    ins = pe.transpose(o[:, t * P:(t + 1) * P],
                                       weighted[:, t, 2 * b:2 * b + 2, :].rearrange("p e s -> p (e s)"),
                                       ident[:, :])
                misc_end(ins)

            def hidden_turn(i, name, b, half):
                o = open_misc(pe, i, name)
                pe.wait_ge(hid_ready, i * 4 + 2 * b + half + 1)
                for m in range(4):
                    c = 2 * P * (2 * half + m // 2) + m % 2
                    ins = pe.transpose(o[:, m * P:(m + 1) * P], hid[:, c:c + 2 * P - 1:2], ident[:, :])
                misc_end(ins)

            def down(i, b, s):
                pe.wait_ge(y_read, i * 4 + 4 + 2 * b)
                for n in range(2):
                    ins = pe.matmul(bank[4 + n][:, :], row_sel[:, :], bias[0:2, (4 + n) * 512:(5 + n) * 512],
                                    start=True, stop=False, skip_group_check=True)
                ins.then_inc(bias_used, 1)
                for ch in range(4):
                    wait_moe_chunk(pe, i, b, 8 + ch)
                    if ch % 2 == 0:
                        wait_misc_out(pe, i, f"hidT_{s}{ch // 2}")
                    w = moe_slot(b, 8 + ch).rearrange("p (e k m) -> p e k m", e=2, k=2)
                    for n in range(2):
                        for kk in range(2):
                            k = 2 * ch + kk
                            for e in range(2):
                                r = slice(e * SLOTS, (e + 1) * SLOTS)
                                ins = pe.matmul(bank[4 + n][r, :], hidT[:, k, e * SLOTS:(e + 1) * SLOTS],
                                                w[:, e, kk, n * 512:(n + 1) * 512],
                                                start=False, stop=k == KT - 1, skip_group_check=True)
                        if ch == 3:
                            ins.then_inc(y_done, 1)
                    if ch < 3:
                        ins.then_inc(weights_used, 1)

            def scatter(i, s, b):
                pe.wait_ge(y_read, i * 4 + 4 + 2 * b + 2)
                for t in range(TT):
                    for c in range(2):
                        o = open_misc(pe, i, f"add_{s}{2 * t + c}")
                        misc_end(pe.matmul(o[:, :], turned[:, t * P:(t + 1) * P], y_s[:, c * W:(c + 1) * W],
                                           start=True, stop=True))

            def body(i, p):
                pe.wait_ge(member_ready, i + p + 1)
                for g in range(4):
                    o = open_misc(pe, i, f"gather{g}")
                    for kk in range(2):
                        c = (2 * g + kk) * P
                        for t in range(TT):
                            ins = pe.matmul(o[:, kk * 256:(kk + 1) * 256], h2[:, t, c:c + P],
                                            member[:, t, :, :].rearrange("p e s -> p (e s)"),
                                            start=t == 0, stop=t == TT - 1)
                    misc_end(ins)
                wait_misc_out(pe, i, "gather3")
                gate_up(i, 0)
                turn(i, "turn_a", 0)
                hidden_turn(i, "hidT_a0", 0, 0)
                hidden_turn(i, "hidT_a1", 0, 1)
                down(i, 0, "a")
                gate_up(i, 1)
                scatter(i, "a", 0)
                turn(i, "turn_b", 1)
                hidden_turn(i, "hidT_b0", 1, 0)
                hidden_turn(i, "hidT_b1", 1, 1)
                down(i, 1, "b")
                scatter(i, "b", 1)

            def one_pass(p):
                with pe.Fori(0, BODIES) as j:
                    body(p * BODIES + j, p)

            pe.wait_ge(moe_primed, 2)
            one_pass(0)
            pe.wait_ge(flag_ready, 1)
            over = pe.value_load(flag[0:1, 0:1], min_val=0, max_val=SEQ)
            with pe.If(over > SLOTS):
                with pe.Fori(1, PASSES) as p:
                    one_pass(p)

        @block.scalar
        def _(act):
            step = Steps(act, act_step)

            def out_of(name, ins):
                ins.then_inc(emptied["act"], 1)

            def copy_out(name, dst, cols=None):
                b = product(act, name)
                out_of(name, act.activation(dst, b[:, 0:cols] if cols else b[:, :], ACT.Copy))

            def root(n, dst, src):
                act.wait_ge(sqrt_asked, n)
                act.activation(dst, src, ACT.Sqrt).then_inc(sqrt_done, 1)

            act.wait_ge(vec_landed, 16)
            act.activation(cond_sig, vec[:, 0, V_C:V_C + KT], ACT.Sigmoid).then_inc(sig_ready, 1)
            act.wait_ge(x_landed, 16)
            for t in range(TT):
                act.activation(x_n[:, t, :], x[:, t, :], ACT.Square, accum_out=x_ss[:, t:t + 1])\
                    .then_inc(x_squared, 1)
            for n in range(3):
                act.wait_ge(sin_asked, n + 1)
                act.activation(mlp_y[:, 3, :], mlp_y[:, 0, :], ACT.Sin).then_inc(sin_done, 1)
            root(1, x_rt, x_ms)
            act.wait_ge(r_ready, 1)
            act.wait_ge(x_squared, TT)
            for t in range(TT):
                act.activation(x_n[:, t, :], x[:, t, :], ACT.Copy, scale=x_r[:, t:t + 1]).then_inc(xn_ready, 1)
            for i in range(4):
                if i == 2:
                    for j in range(5):
                        copy_out(f"spectrum0{j}", spectra[:, 0, j, :])
                copy_out(f"ada{i}", part[:, i, :])
            act.wait_ge(modcol_ready, 1)
            for i in (0, 2):
                b = product(act, f"xT{i}")
                act.activation(hT[:, 2 * i, :], b[:, 0:SEQ], ACT.Identity,
                               bias=shift1[:, 2 * i:2 * i + 1], scale=n1_gain[:, 2 * i:2 * i + 1])
                out_of("", act.activation(hT[:, 2 * i + 1, :], b[:, SEQ:2 * SEQ], ACT.Identity,
                                          bias=shift1[:, 2 * i + 1:2 * i + 2],
                                          scale=n1_gain[:, 2 * i + 1:2 * i + 2]))
            act.wait_ge(products_ready, JOB["modcol"] + 1)
            act.wait_ge(pads_zeroed, 1)
            for i in range(2):
                b = product(act, f"cg{i}")
                for m in range(2):
                    c = 2 * i + m
                    bias = V_BIN + HY_T + WT + c
                    ins = act.activation(cf_cv[:, c, :], b[:, m * SEQ:(m + 1) * SEQ], ACT.Sigmoid,
                                         bias=vec[:, 0, bias:bias + 1])
                out_of("", ins)
            for i in range(6):
                b = product(act, f"hy{i}")
                for m in range(2):
                    c = 2 * i + m
                    ins = act.activation(hy_in[:, c, 1:SEQ + 1], b[:, m * SEQ:(m + 1) * SEQ], ACT.Identity,
                                         bias=vec[:, 0, V_BIN + c:V_BIN + c + 1])
                out_of("", ins)
            for j in range(5):
                copy_out(f"spectrum1{j}", spectra[:, 1, j, :])
            for g in range(3):
                for t in range(TT):
                    copy_out(f"hyT{g}{t}", hy[:, g, t, :])

            def gate_out(i):
                b = product(act, f"gate{i}")
                for m in range(2):
                    c = 2 * i + m
                    bias = V_BIN + HY_T + 2 * WT + c
                    ins = act.activation(gates[c // KT][:, c % KT, :], b[:, m * SEQ:(m + 1) * SEQ],
                                         ACT.Identity, bias=vec[:, 0, bias:bias + 1])
                out_of("", ins)

            root(2, ln_rt, ln_ms)
            root(3, qk_ss[:, 1, :, :], qk_ss[:, 0, :, :])
            root(4, qk_ss[:, 1, :, :], qk_ss[:, 0, :, :])
            gate_out(0)
            for i in range(2):
                copy_out(f"zT{i}", br_hy[:, 2 * i:2 * i + 2, :].rearrange("p m s -> p (m s)"))
            for j in range(2):
                for t in range(TT):
                    b = product(act, f"qkT{j}{t}")
                    out_of("", act.activation(qkT[:, j, :, t * P:(t + 1) * P],
                                              b[:, :].rearrange("p (h s) -> p h s", h=HEADS), ACT.Copy))
            for m in range(WT):
                act.wait_ge(cf_scaled, m + 1)
                act.activation(cf_cv[:, m, :], br_cf[:, m, :], ACT.Sigmoid).then_inc(cf_act, 1)
            act.wait_ge(lam_ready, 2)
            act.activation(lam_s[:, 2:4], lam_s[:, 0:2], ACT.Exp).then_inc(lam_exp, 1)
            for h in range(HEADS + 1):
                if h < HEADS:
                    for c in range(2):
                        act.wait_ge(max_ready, 2 * h + c + 1)
                        b = product(act, f"score{h}{c}")
                        for t in range(TT):
                            ins = act.activation(prob[:, h % 2, c, t, :], b[:, t * SEQ:(t + 1) * SEQ], ACT.Exp,
                                                 bias=s_max[:, h, c, t:t + 1], scale=SCALE,
                                                 accum_out=s_sum[:, h, c, t:t + 1])
                        out_of("", ins)
                if h:
                    gate_out(h)
                    if h == 1:
                        act.wait_ge(br_cf_ready, 1)
                    b = product(act, f"aT{h - 1}")
                    out_of("", act.activation(attT[:, (h - 1) % 2, :, :],
                                              b[:, :].rearrange("p (k s) -> p k s", k=TT), ACT.Copy))
            gate_out(5)
            gate_out(6)
            root(5, o_rt, o_ms)
            for i in range(2):
                b = product(act, f"oT{i}")
                out_of("", act.activation(br_at[:, 2 * i:2 * i + 2, :].rearrange("p m s -> p (m s)"), b[:, :],
                                          ACT.Copy, scale=sub_gain))
            gate_out(7)
            def gates_sigmoid(n):
                wait_emptied(act, f"gate{4 * n + 3}")
                act.activation(gates[n], gates[n], ACT.Sigmoid).then_inc(gates_ready, 1)

            gates_sigmoid(0)
            gates_sigmoid(1)
            for i in range(8, 12):
                gate_out(i)
            gates_sigmoid(2)
            for i in range(8):
                copy_out(f"adab{i}", area_2[:, i * W:(i + 1) * W])
            root(6, g2_rt, g2_ms)
            for i in range(4):
                copy_out(f"h2T{i}", h2T[:, 2 * i:2 * i + 2, :].rearrange("p k s -> p (k s)"))
            act.wait_ge(top_ready, TT)
            for t in range(TT):
                act.activation(top_w[:, t, :], top[:, t, 0:TOPK], ACT.Exp, bias=top_s[:, t, 0:1],
                               accum_out=top_s[:, t, 1:2]).then_inc(top_exp, 1)
            act.sem_inc(misc_out["act"], MISC_COUNT["act"])
            act.sem_inc(y_read, 4)
            act.sem_inc(moe_primed, 1)

            def misc_copy(i, name, dst):
                b = misc_product(act, i, name)
                act.activation(dst, b[:, 0:dst.shape[1]], ACT.Copy).then_inc(misc_out["act"], 1)

            def body(i):
                for g in range(4):
                    misc_copy(i, f"gather{g}", xT[:, 2 * g:2 * g + 2, :].rearrange("p k s -> p (k s)"))
                for b, s in enumerate("ab"):
                    for half in range(2):
                        r = slice(half * 512, (half + 1) * 512)
                        act.wait_ge(gate_min, i * 4 + 2 * b + half + 1)
                        act.activation(sig_s[:, r], gate_s[:, r], ACT.Sigmoid, scale=ALPHA)\
                            .then_inc(sigmoid_done, 1)
                    misc_copy(i, f"turn_{s}", turned)
                    for half in range(2):
                        misc_copy(i, f"hidT_{s}{half}",
                                  hidT[:, 4 * half:4 * half + 4, :].rearrange("p k s -> p (k s)"))
                    for n in range(2):
                        act.wait_ge(y_done, i * 4 + 2 * b + n + 1)
                        act.activation(y_s[:, n * W:(n + 1) * W], bank[4 + n][:, :], ACT.Copy)\
                            .then_inc(y_read, 1)

            def one_pass(p):
                with act.Fori(0, BODIES) as j:
                    body(p * BODIES + j)

            one_pass(0)
            act.wait_ge(flag_ready, 1)
            over = act.value_load(flag[0:1, 0:1], min_val=0, max_val=SEQ)
            with act.If(over > SLOTS):
                with act.Fori(1, PASSES) as p:
                    one_pass(p)

        @block.vector
        def _(dve):
            step = Steps(dve, dve_step)
            emptied_here = Steps(dve, emptied["dve"])

            def inverse_root(n, ms, rt, r, t):
                dve.wait_ge(sqrt_done, n)
                step(dve.reciprocal(r, rt))
                step.wait()
                step(dve.tensor_tensor(t, r, r, ALU.mult))
                step.wait()
                step(dve.tensor_tensor(t, t, ms, ALU.mult))
                step.wait()
                step(dve.tensor_scalar(t, t, -0.5, 1.5, ALU.mult, ALU.add))
                step.wait()
                step(dve.tensor_tensor(r, r, t, ALU.mult))
                step.wait()

            dve.wait_ge(vec_landed, 16)
            dve.wait_ge(sig_ready, 1)
            step(dve.tensor_tensor(cond, vec[:, 0, V_C:V_C + KT], cond_sig, ALU.mult))
            step.wait()
            dve.tensor_copy(cond_rep[:, :, :], cond.rearrange("p (k o) -> p k o", o=1).to_broadcast([P, KT, 32]))\
                .then_inc(cond_ready, 1)
            step(dve.tensor_scalar(sub_gain, vec[:, 0, V_SUB:V_SUB + 1], 1.0 - LAM_INIT, None, ALU.mult))
            dve.wait_ge(mlp_landed, 16)
            h = slice(0, HF_HID)
            step(dve.tensor_tensor(w4s[h, :, 0, :], w4[h, :, 0, :], w4[h, :, 1, :], ALU.add))
            dve.tensor_tensor(w4s[h, :, 1, :], w4[h, :, 0, :], w4[h, :, 1, :], ALU.subtract).then_inc(w4_summed, 1)
            y, turns, tmp = mlp_y[:, 0, :], mlp_y[:, 1, :], mlp_y[:, 2, :]
            for n in range(3):
                b = product(dve, f"mlp{n}")
                emptied_here(dve.tensor_scalar(y, b[h, 0:SEQ], hf_col[h, n:n + 1], hf_col[h, 3:4],
                                               ALU.add, ALU.mult))
                emptied_here.wait()
                step(dve.tensor_scalar(turns, y, 1.0 / (2 * math.pi), ROUND, ALU.mult, ALU.add))
                step.wait()
                step(dve.tensor_scalar(turns, turns, -ROUND, None, ALU.add))
                for part_of_pi in (PI_A, PI_B, PI_C):
                    step.wait()
                    step(dve.scalar_tensor_tensor(y, turns, -part_of_pi, y, ALU.mult, ALU.add))
                step.wait()
                dve.tensor_scalar(y, y, 3.1415925, -3.1415925, ALU.min, ALU.max).then_inc(sin_asked, 1)
            dve.wait_ge(x_squared, TT)
            step(dve.tensor_scalar(x_ms, x_ss, 1.0 / D, EPS, ALU.mult, ALU.add))
            step.wait()
            dve.sem_inc(sqrt_asked, 1)
            inverse_root(1, x_ms, x_rt, x_r, x_t)
            dve.sem_inc(r_ready, 1)
            dve.wait_ge(window_landed, 16)
            for o in range(2):
                for s in range(2):
                    for t in range(TT):
                        b = product(dve, f"filter{o}{s}{t}")
                        emptied_here(dve.tensor_tensor(filt[:, t, o, s, :], b[:, :], window[:, t, :], ALU.mult))
            dve.memset(hy_in[:, :, 0:1], 0.0)
            dve.memset(hy_in[:, :, SEQ + 1:SEQ + 2], 0.0).then_inc(pads_zeroed, 1)
            emptied_here.wait()
            half_taps = TAPS // 2
            dve.wait_ge(xn_ready, TT)
            step(dve.memset(cf_in[:, :, 0:half_taps], 0.0))
            step(dve.memset(cf_in[:, :, SEQ + half_taps:], 0.0))
            b = product(dve, "modcol")
            step(dve.tensor_tensor(shift1, b[:, 0:KT], vec[:, 0, V_ADA:V_ADA + KT], ALU.add))
            emptied_here(dve.tensor_tensor(n1_gain, b[:, KT:2 * KT], vec[:, 0, V_ADA + KT:V_ADA + 2 * KT], ALU.add))
            emptied_here.wait()
            dve.scalar_tensor_tensor(n1_gain, n1_gain, 1.0, vec[:, 0, V_N1:V_N1 + KT], ALU.add, ALU.mult)\
                .then_inc(modcol_ready, 1)
            dve.wait_ge(modcol_ready, 1)
            step.wait()
            for i in (1, 3):
                b = product(dve, f"xT{i}")
                for kk in range(2):
                    k = 2 * i + kk
                    ins = dve.tensor_scalar(hT[:, k, :], b[:, kk * SEQ:(kk + 1) * SEQ], n1_gain[:, k:k + 1],
                                            shift1[:, k:k + 1], ALU.mult, ALU.add)
                emptied_here(ins)
            wait_emptied(dve, "cg1")
            for i in range(2):
                b = product(dve, f"ca{i}")
                for m in range(2):
                    c = 2 * i + m
                    bias = V_BIN + HY_T + c
                    ins = dve.scalar_tensor_tensor(cf_in[:, c, half_taps:half_taps + SEQ],
                                                   b[:, m * SEQ:(m + 1) * SEQ], vec[:, 0, bias:bias + 1],
                                                   cf_cv[:, c, :], ALU.add, ALU.mult)
                emptied_here(ins)
            emptied_here.wait()

            def conv(first, last):
                for tap in range(first, last):
                    for c in range(WT):
                        w = vec[:, 2, tap * WT + c:tap * WT + c + 1]
                        src = cf_in[:, c, tap:tap + SEQ]
                        if tap == 0:
                            step(dve.tensor_scalar(cf_cv[:, c, :], src, w, vec[:, 0, V_DWB + c:V_DWB + c + 1],
                                                   ALU.mult, ALU.add))
                        else:
                            step.wait(conv_last[c])
                            ins = dve.scalar_tensor_tensor(cf_cv[:, c, :], src, w, cf_cv[:, c, :],
                                                           ALU.mult, ALU.add)
                            step(ins)
                        conv_last[c] = step.n
            conv_last = [0] * WT

            def short_conv(i):
                wait_emptied(dve, f"hy{i}")
                dve.wait_ge(pads_zeroed, 1)
                for tap in range(3):
                    for m in range(2):
                        c = 2 * i + m
                        w = vec[:, 1, tap * HY_T + c:tap * HY_T + c + 1]
                        src = hy_in[:, c, tap:tap + SEQ]
                        if tap == 0:
                            step(dve.tensor_scalar(hy_cv[:, c, :], src, w, vec[:, 0, V_HYB + c:V_HYB + c + 1],
                                                   ALU.mult, ALU.add))
                        else:
                            ins = dve.scalar_tensor_tensor(hy_cv[:, c, :], src, w, hy_cv[:, c, :],
                                                           ALU.mult, ALU.add)
                            if tap == 1:
                                step(ins)
                            else:
                                ins.then_inc(hy_conv_done, 1)
                    if tap < 2:
                        step.wait()

            def mix(o):
                for half in range(2):
                    k_cos, k_sin, k_cos2 = ((0, 3, 2), (1, 4, 1))[half]
                    u_cos = product(dve, f"u{o}{half}")
                    if half == 0:
                        wait_emptied(dve, f"spectrum{o}4")
                    step(dve.tensor_tensor(ysp[:, half, :], u_cos[:, :], spectra[:, o, k_cos, :], ALU.mult))
                    u_sin = product(dve, f"u{o}{2 + half}")
                    step(dve.tensor_tensor(hy_tmp[:, 0, :], u_sin[:, :], spectra[:, o, k_sin, :], ALU.mult))
                    emptied_here(dve.tensor_tensor(ysp[:, 2 + half, :], u_cos[:, :], spectra[:, o, k_sin, :],
                                                   ALU.mult))
                    emptied_here(dve.tensor_tensor(hy_tmp[:, 1, :], u_sin[:, :], spectra[:, o, k_cos2, :],
                                                   ALU.mult))
                    step.wait()
                    step(dve.tensor_tensor(ysp[:, half, :], ysp[:, half, :], hy_tmp[:, 0, :], ALU.subtract))
                    emptied_here.wait()
                    dve.tensor_tensor(ysp[:, 2 + half, :], ysp[:, 2 + half, :], hy_tmp[:, 1, :], ALU.add)\
                        .then_inc(spectra_mixed, 1)
                    dve.wait_ge(spectra_mixed, 2 * o + half + 1)
                    step.wait()

            def hyena_step(o):
                for t in range(TT):
                    step(dve.tensor_tensor(hy_tmp[:, t, :], hy[:, 0, t, :], hy_bias[:, o, :], ALU.mult))
                for t in range(TT):
                    b = product(dve, f"inv{o}{t}")
                    step.wait()
                    emptied_here(dve.tensor_tensor(hy_tmp[:, t, :], b[:, :], hy_tmp[:, t, :], ALU.add))
                    emptied_here.wait()
                    dve.tensor_tensor(hy[:, 0, t, :], hy_tmp[:, t, :], hy[:, 1 + o, t, :], ALU.mult)\
                        .then_inc(z_ready, 1)
                dve.wait_ge(z_ready, 2 * o + 2)

            def add_bias(j):
                for t in range(TT):
                    b = product(dve, f"{'qkv'[j]}{t}")
                    emptied_here(dve.tensor_tensor(qkv[:, j, t, :], b[:, :], qkv[:, j, t, :], ALU.add))
                emptied_here.wait()

            def heads(v):
                return v.rearrange("p (g d) -> p g d", d=HD)

            def norm_and_rotate(j):
                ms, rt, r, tmp = (qk_ss[:, n, :, :] for n in range(4))
                for t in range(TT):
                    v = qkv[:, j, t, :]
                    step(dve.tensor_tensor(hy_tmp[:, t, :], v, v, ALU.mult))
                step.wait()
                for t in range(TT):
                    step(dve.tensor_reduce(ms[:, t, :], heads(hy_tmp[:, t, :]), AX_X, ALU.add))
                step.wait()
                step(dve.tensor_scalar(ms, ms, 1.0 / HD, EPS, ALU.mult, ALU.add))
                step.wait()
                dve.sem_inc(sqrt_asked, 1)
                inverse_root(3 + j, ms, rt, r, tmp)
                both = [P, GROUPS, HD]
                half = HD // 2
                for t in range(TT):
                    v = heads(qkv[:, j, t, :])
                    step(dve.tensor_tensor(v, v, r[:, t, :].rearrange("p (g o) -> p g o", o=1).to_broadcast(both),
                                           ALU.mult))
                step.wait()
                for t in range(TT):
                    v = heads(qkv[:, j, t, :])
                    step(dve.tensor_tensor(v, v, gain[:, j:j + 1, :].to_broadcast(both), ALU.mult))
                step.wait()
                for t in range(TT):
                    v = heads(qkv[:, j, t, :])
                    c, s = heads(hy_tmp[:, 0, :]), heads(hy_tmp[:, 1, :])
                    step(dve.tensor_tensor(c, v, rope[:, 0, t:t + 1, :].to_broadcast(both), ALU.mult))
                    part_shape = [P, GROUPS, half]
                    step(dve.tensor_tensor(s[:, :, 0:half], v[:, :, half:],
                                           rope[:, 1, t:t + 1, 0:half].to_broadcast(part_shape), ALU.mult))
                    step(dve.tensor_tensor(s[:, :, half:], v[:, :, 0:half],
                                           rope[:, 1, t:t + 1, half:].to_broadcast(part_shape), ALU.mult))
                    step.wait()
                    dve.tensor_tensor(v, c, s, ALU.add).then_inc(roped, 1)
                    dve.wait_ge(roped, TT * j + t + 1)

            all_tiles = [P, WT, SEQ]

            def conformer_mean():
                b = product(dve, "mean")
                emptied_here(dve.scalar_tensor_tensor(
                    cf_cv, b[:, 0:SEQ].rearrange("p (o s) -> p o s", o=1).to_broadcast(all_tiles), -1.0 / W,
                    cf_cv, ALU.mult, ALU.add))
                emptied_here.wait()
                dve.tensor_tensor(cf_sq, cf_cv, cf_cv, ALU.mult).then_inc(centred, 1)

            def conformer_scale():
                b = product(dve, "var")
                emptied_here(dve.tensor_scalar(ln_ms, b[:, 0:SEQ], 1.0 / W, EPS, ALU.mult, ALU.add))
                emptied_here.wait()
                dve.sem_inc(sqrt_asked, 1)
                inverse_root(2, ln_ms, ln_rt, ln_r, ln_t)
                step(dve.tensor_tensor(cf_cv, cf_cv,
                                       ln_r.rearrange("p (o s) -> p o s", o=1).to_broadcast(all_tiles), ALU.mult))
                step.wait()

            for i in range(6):
                conv(4 * i, 4 * i + 4)
                short_conv(i)
            conv(24, TAPS)
            step.wait()
            dve.sem_inc(conv_done, 1)
            mix(0)
            conformer_mean()
            dve.wait_ge(attn_landed, 16 * 4)
            add_bias(0)
            dve.wait_ge(hyena_landed, 32)
            hyena_step(0)
            conformer_scale()
            norm_and_rotate(0)
            add_bias(1)
            mix(1)
            norm_and_rotate(1)
            add_bias(2)
            hyena_step(1)
            for n in range(2):
                dve.tensor_tensor_reduce(lam_v[:, 2 * n, :], lam_v[:, 2 * n, :], lam_v[:, 2 * n + 1, :], 1.0, 0.0,
                                         ALU.mult, ALU.add, lam_s[:, n:n + 1]).then_inc(lam_ready, 1)
            for m in range(WT):
                dve.tensor_scalar(br_cf[:, m, :], cf_cv[:, m, :], vec[:, 0, V_LNG + m:V_LNG + m + 1],
                                  vec[:, 0, V_LNB + m:V_LNB + m + 1], ALU.mult, ALU.add).then_inc(cf_scaled, 1)
            dve.wait_ge(cf_act, WT)
            dve.tensor_tensor(br_cf[:, :, :], br_cf[:, :, :], cf_cv, ALU.mult).then_inc(br_cf_ready, 1)
            dve.wait_ge(lam_exp, 1)
            step(dve.tensor_tensor(lam_s[:, 4:5], lam_s[:, 3:4], lam_s[:, 2:3], ALU.subtract))
            step.wait()
            step(dve.tensor_scalar(lam_s[:, 5:6], lam_s[:, 4:5], -LAM_INIT, None, ALU.add))
            step.wait()

            def score_max(h):
                for c in range(2):
                    b = product(dve, f"score{h}{c}")
                    step(dve.tensor_reduce(s_max[:, h, c, :], b[:, :].rearrange("p (t k) -> p t k", t=TT),
                                           AX_X, ALU.max))
                    step.wait()
                    dve.tensor_scalar(s_max[:, h, c, :], s_max[:, h, c, :], -SCALE, None, ALU.mult)\
                        .then_inc(max_ready, 1)

            def combine(h):
                wait_emptied(dve, f"score{h}1")
                step(dve.reciprocal(s_inv[:, h, :, :], s_sum[:, h, :, :]))
                step.wait()
                step(dve.tensor_scalar(s_inv[:, h, 1, :], s_inv[:, h, 1, :], lam_s[:, 5:6], None, ALU.mult))
                step.wait()
                for t in range(TT):
                    v = prob[:, h % 2, 1, t, :]
                    step(dve.tensor_scalar(v, v, s_inv[:, h, 1, t:t + 1], None, ALU.mult))
                step.wait()
                for t in range(TT):
                    v = prob[:, h % 2, 0, t, :]
                    ins = dve.scalar_tensor_tensor(v, v, s_inv[:, h, 0, t:t + 1], prob[:, h % 2, 1, t, :],
                                                   ALU.mult, ALU.add)
                ins.then_inc(att_ready, 1)

            score_max(0)
            score_max(1)
            for h in range(HEADS):
                combine(h)
                b = product(dve, f"o{h}")
                emptied_here(dve.tensor_copy(att[:, :, h * P:(h + 1) * P],
                                             b[:, 0:2 * P].rearrange("p (t e) -> p t e", t=TT)))
                if h + 2 < HEADS:
                    score_max(h + 2)
            emptied_here.wait()
            tiny = 2.0 ** -64
            o_a, o_b = o_ms[:, 0:8], o_ms[:, 8:16]

            def by_head(v):
                return v.rearrange("p (h e) -> p h e", h=HEADS)

            for t in range(TT):
                r = slice(4 * t, 4 * t + 4)
                step(dve.tensor_scalar(hy_tmp[:, 0, :], att[:, t, :], 1e17, -1e17, ALU.min, ALU.max))
                step(dve.tensor_scalar(hy_tmp[:, 1, :], att[:, t, :], tiny, None, ALU.mult))
                step.wait()
                for n in range(2):
                    step(dve.tensor_tensor(hy_tmp[:, n, :], hy_tmp[:, n, :], hy_tmp[:, n, :], ALU.mult))
                step.wait()
                step(dve.tensor_reduce(o_a[:, r], by_head(hy_tmp[:, 0, :]), AX_X, ALU.add))
                step(dve.tensor_reduce(o_b[:, r], by_head(hy_tmp[:, 1, :]), AX_X, ALU.add))
                step.wait()
            small_sum, large_sum = o_sel[:, 0:8], o_sel[:, 8:16]
            step(dve.tensor_scalar(o_b, o_b, 1e30, None, ALU.min))
            step.wait()
            step(dve.tensor_scalar(small_sum, o_b, 1e-5, None, ALU.is_lt))
            step(dve.tensor_scalar(o_sel[:, 16:24], o_b, 1.0, None, ALU.is_lt))
            step.wait()
            step(dve.tensor_tensor(large_sum, o_sel[:, 16:24], small_sum, ALU.subtract))
            step(dve.tensor_scalar(o_a, o_a, 1.0 / P, EPS, ALU.mult, ALU.add))
            step(dve.tensor_scalar(o_b, o_b, 1.0 / P, 1e-12, ALU.mult, ALU.add))
            step.wait()
            step(dve.tensor_scalar(large_sum, large_sum, tiny, None, ALU.mult))
            dve.sem_inc(sqrt_asked, 1)
            inverse_root(5, o_ms, o_rt, o_r, o_t)
            step(dve.tensor_tensor(o_r, o_r, o_sel[:, 0:16], ALU.mult))
            step.wait()
            step(dve.tensor_tensor(o_t[:, 0:8], o_r[:, 0:8], o_r[:, 8:16], ALU.add))
            step.wait()
            for t in range(TT):
                r = o_t[:, 4 * t:4 * t + 4].rearrange("p (h o) -> p h o", o=1).to_broadcast([P, HEADS, P])
                v = by_head(att[:, t, :])
                ins = dve.tensor_tensor(v, v, r, ALU.mult)
                step(ins)
            step.wait()
            dve.sem_inc(o_ready, 1)

            dve.wait_ge(mod_bias_landed, 16)
            for i in range(8):
                wait_chunk(dve, "ada", 4 + i)
                w = slot_view("ada", 4 + i)
                acc = area_2[:, i * W:(i + 1) * W]
                for k in range(KT):
                    ins = dve.scalar_tensor_tensor(acc, w[:, k, :], cond[:, k:k + 1], acc, ALU.mult, ALU.add)
                    if k < KT - 1:
                        step(ins)
                        step.wait()
                ins.then_inc(ada_summed, 1)

            for g, n in enumerate((0, 1, 2)):
                dve.wait_ge(gates_ready, g + 1)
                for m in range(4):
                    b = product(dve, f"merge{n}{m}")
                    gate_v = gates[n][:, 2 * m:2 * m + 2, :].rearrange("p k s -> p (k s)")
                    sum_v = merged[:, 2 * m:2 * m + 2, :].rearrange("p k s -> p (k s)")
                    if g == 0:
                        emptied_here(dve.tensor_tensor(sum_v, b[:, :], gate_v, ALU.mult))
                        continue
                    emptied_here(dve.tensor_tensor(hy_tmp[:, m % 2, :], b[:, :], gate_v, ALU.mult))
                    emptied_here.wait()
                    ins = dve.tensor_tensor(sum_v, sum_v, hy_tmp[:, m % 2, :], ALU.add)
                    if g == 1:
                        step(ins)
                    else:
                        ins.then_inc(merged_ready, 1)
                if g == 1:
                    step.wait()
            wait_emptied(dve, "adab7")
            dve.wait_ge(gain2_landed, 16)
            step(dve.scalar_tensor_tensor(sc2, sc2, 1.0, scratch, ALU.add, ALU.mult))
            dve.wait_ge(x_again_landed, 16)
            for t in range(TT):
                for c in range(2):
                    b = product(dve, f"out{t}{c}")
                    r = slice(c * W, (c + 1) * W)
                    emptied_here(dve.tensor_tensor(hy_tmp[:, c, :], b[:, :], g1[:, r], ALU.mult))
                    emptied_here.wait()
                    step(dve.tensor_tensor(x[:, t, r], x[:, t, r], hy_tmp[:, c, :], ALU.add))
                step.wait()
                step(dve.tensor_tensor_reduce(area_1[:, 0:D], x[:, t, :], x[:, t, :], 1.0, 0.0,
                                              ALU.mult, ALU.add, g2_ss[:, t:t + 1]))
                step.wait()
            step(dve.tensor_scalar(g2_ms, g2_ss, 1.0 / D, EPS, ALU.mult, ALU.add))
            step.wait()
            dve.sem_inc(sqrt_asked, 1)
            inverse_root(6, g2_ms, g2_rt, g2_r, g2_t)
            for t in range(TT):
                step(dve.scalar_tensor_tensor(h2[:, t, :], x[:, t, :], g2_r[:, t:t + 1], sc2, ALU.mult, ALU.mult))
            step.wait()
            for t in range(TT):
                dve.tensor_tensor(h2[:, t, :], h2[:, t, :], sh2, ALU.add).then_inc(h2_ready, 1)

            b = product(dve, "logits")
            dve.wait_ge(router_landed, 32)
            emptied_here(dve.tensor_tensor(
                logit[:, :, :], b[:, 0:TT * EXPERTS].rearrange("p (t e) -> p t e", t=TT),
                b_router[:, :].rearrange("p (o e) -> p o e", o=1).to_broadcast([P, TT, EXPERTS]), ALU.add))
            emptied_here.wait()
            for t in range(TT):
                step(dve.max(top[:, t, :], logit[:, t, :]))
            step.wait()
            for t in range(TT):
                step(dve.max_index(top_i[:, t, :], top[:, t, :], logit[:, t, :]))
                dve.tensor_scalar(top_s[:, t, 0:1], top[:, t, 0:1], -1.0, None, ALU.mult).then_inc(top_ready, 1)
            step.wait()
            step(dve.tensor_copy(top_f[:, :, :], top_i[:, :, :]))
            step.wait()
            for k in range(TOPK):
                for t in range(TT):
                    idx = top_f[:, t, k:k + 1]
                    if k == 0:
                        step(dve.tensor_scalar(mask[:, t, :], expert_no[:, :], idx, None, ALU.is_equal))
                    else:
                        step(dve.scalar_tensor_tensor(mask[:, t, :], expert_no[:, :], idx, mask[:, t, :],
                                                      ALU.is_equal, ALU.add))
                step.wait()
            dve.sem_inc(mask_ready, 1)
            dve.wait_ge(top_exp, TT)
            step(dve.reciprocal(top_s[:, :, 2:3], top_s[:, :, 1:2]))
            step.wait()
            for t in range(TT):
                step(dve.tensor_scalar(top_w[:, t, :], top_w[:, t, :], top_s[:, t, 2:3], None, ALU.mult))
            step.wait()
            for k in range(TOPK):
                for t in range(TT):
                    step(dve.tensor_scalar(logit[:, t, :] if k else comb[:, t, 0:EXPERTS], expert_no[:, :],
                                           top_f[:, t, k:k + 1], top_w[:, t, k:k + 1], ALU.is_equal, ALU.mult))
                step.wait()
                if k:
                    step(dve.tensor_tensor(comb[:, :, 0:EXPERTS], comb[:, :, 0:EXPERTS], logit[:, :, :], ALU.add))
                    step.wait()
            b = product(dve, "rank")
            step(dve.tensor_reduce(most, b[:, 64:64 + EXPERTS], AX_X, ALU.max))
            emptied_here(dve.scalar_tensor_tensor(pos[:, :, 0:EXPERTS], mask[:, :, :], -FAR,
                                                  b[:, 0:TT * EXPERTS].rearrange("p (t e) -> p t e", t=TT),
                                                  ALU.mult, ALU.add))
            emptied_here.wait()
            step(dve.tensor_scalar(pos[:, :, 0:EXPERTS], pos[:, :, 0:EXPERTS], FAR, None, ALU.add))
            step.wait()
            dve.tensor_copy(flag[:, :], most).then_inc(flag_ready, 1)

            def members(j, done):
                shape = [P, 4, SLOTS]
                for t in range(TT):
                    p_of = pos[:, t, bass.ds(j * 4, 4)].rearrange("p (e o) -> p e o", o=1)
                    i_of = iota[:, :].rearrange("p (o s) -> p o s", o=1)
                    done(dve.tensor_tensor(member[:, t, :, :], i_of.to_broadcast(shape),
                                           p_of.to_broadcast(shape), ALU.is_equal))
                done.wait()
                for t in range(TT):
                    c_of = comb[:, t, bass.ds(j * 4, 4)].rearrange("p (e o) -> p e o", o=1)
                    ins = dve.tensor_tensor(weighted[:, t, :, :], member[:, t, :, :],
                                            c_of.to_broadcast(shape), ALU.mult)
                    if t < TT - 1:
                        done(ins)
                ins.then_inc(member_ready, 1)

            def gate_up_half(i, b, half, done):
                r = slice(half * 512, (half + 1) * 512)
                n = 2 * b + half + 1
                dve.wait_ge(gate_up_done, i * 4 + n)
                dve.tensor_scalar(gate_s[:, r], bank[half][:, :], LIMIT, None, ALU.min).then_inc(gate_min, 1)
                dve.tensor_scalar(up_s[:, r], bank[2 + half][:, :], LIMIT, -LIMIT, ALU.min, ALU.max)\
                    .then_inc(gate_up_read, 1)

            def hidden_half(i, b, half, done):
                r = slice(half * 512, (half + 1) * 512)
                n = 2 * b + half + 1
                dve.wait_ge(sigmoid_done, i * 4 + n)
                done(dve.tensor_tensor(gate_s[:, r], gate_s[:, r], sig_s[:, r], ALU.mult))
                done.wait()
                dve.wait_ge(gate_up_read, i * 4 + 4 + n)
                dve.scalar_tensor_tensor(hid[:, r], up_s[:, r], 1.0, gate_s[:, r], ALU.add, ALU.mult)\
                    .then_inc(hid_ready, 1)

            def add(i, s, n):
                name = f"add_{s}{n}"
                b = misc_product(dve, i, name)
                prev = MISC_ORD[f"add_{'b' if s == 'a' else 'a'}{n}"] + (0 if s == "a" else MISC_COUNT["dve"])
                dve.wait_ge(misc_out["dve"], i * MISC_COUNT["dve"] + prev)
                quarter = total[:, n // 2, (n % 2) * W:(n % 2 + 1) * W]
                dve.tensor_tensor(quarter, quarter, b[:, :], ALU.add).then_inc(misc_out["dve"], 1)

            def body(i, j):
                done = LoopSteps(dve, moe_step, i * BODY_STEPS)
                for b in range(2):
                    for half in range(2):
                        gate_up_half(i, b, half, done)
                    hidden_half(i, b, 0, done)
                    if b:
                        add(i, "a", 0)
                    hidden_half(i, b, 1, done)
                for n in range(1, 4):
                    add(i, "a", n)
                dve.wait_ge(misc_done, i * len(MISC) + MISC_NO["turn_b"] + 1)
                members(j + 1, done)
                for n in range(4):
                    add(i, "b", n)
                assert done.n == BODY_STEPS

            def one_pass(p, first=False):
                if first:
                    done = LoopSteps(dve, pass_step, 0)
                else:
                    done = LoopSteps(dve, pass_step, p * 4 - 1)
                    done(dve.tensor_scalar(pos[:, :, 0:EXPERTS], pos[:, :, 0:EXPERTS], -float(SLOTS), None, ALU.add))
                    done.wait()
                    dve.wait_ge(misc_done, p * (BODIES * len(MISC)))
                members(0, done)
                assert done.n == (3 if first else 4)
                with dve.Fori(0, BODIES) as j:
                    body(p * BODIES + j, j)

            dve.wait_ge(total_zeroed, 1)
            dve.wait_ge(flag_ready, 1)
            dve.sem_inc(misc_out["dve"], MISC_COUNT["dve"])
            dve.sem_inc(gate_up_read, 4)
            dve.sem_inc(moe_primed, 1)
            one_pass(0, first=True)
            over = dve.value_load(flag[0:1, 0:1], min_val=0, max_val=SEQ)
            with dve.If(over > SLOTS):
                with dve.Fori(1, PASSES) as p:
                    one_pass(p)
            dve.wait_ge(misc_out["dve"], MISC_COUNT["dve"] * (BODIES + 1))
            dve.drain()
            for t in range(TT):
                step(dve.tensor_tensor(total[:, t, :], total[:, t, :], g2, ALU.mult))
            step.wait()
            for t in range(TT):
                dve.tensor_tensor(total[:, t, :], total[:, t, :], x[:, t, :], ALU.add).then_inc(out_ready, 1)

    return nc


def shape_constants():
    f32 = np.float32
    n = 2 * SEQ
    t, f = np.arange(SEQ)[:, None], np.arange(SEQ)[None, :]
    cos, sin = np.cos(2 * np.pi * t * f / n), np.sin(2 * np.pi * t * f / n)
    nyquist = np.cos(np.pi * np.arange(SEQ))
    sin_ny = sin.copy()
    sin_ny[:, 0] = nyquist
    cos_ny = cos[:, 0:P].copy()
    cos_ny[:, 0] = nyquist
    dft_f = np.concatenate([cos, sin_ny, cos_ny, sin[:, 0:P]], axis=1)
    weight = np.full((SEQ, 1), 2.0 / n)
    weight[0] = 1.0 / n
    dft_i = np.concatenate([cos.T * weight, sin_ny.T * weight], axis=0)

    pos = np.arange(SEQ, dtype=f32)
    time = np.linspace(0.0, 1.0, SEQ, dtype=f32)[:, None]
    bands = np.linspace(1e-4, BANDS - 1, BANDS, dtype=f32)
    ang = f32(2.0 * math.pi / SEQ) * pos[:, None] * bands[None, :]
    z = np.concatenate([time, np.cos(ang), -np.sin(ang)], axis=-1)
    deltas = np.abs(np.linspace(math.log(1e-2) / 0.3, math.log(1e-2) / 1.5, W, dtype=f32))
    window = np.exp(-time * deltas[None, :]) + f32(0.05)

    inv = f32(1.0) / (f32(10000.0) ** (np.arange(0, HD, 2, dtype=f32) / f32(HD)))
    ra = pos[:, None] * inv[None, :]
    rc, rs = np.cos(ra), np.sin(ra)
    rope = np.stack([np.concatenate([rc, rc], axis=1), np.concatenate([-rs, rs], axis=1)])
    made = {"dft_f": dft_f, "dft_i": dft_i, "z_features": z.T, "window": window, "rope": rope}
    return {k: np.ascontiguousarray(v, dtype=f32) for k, v in made.items()}


PACKED = ("norm1_g", "q_norm_g", "k_norm_g", "lam_q1", "lam_k1", "lam_q2", "lam_k2", "subln_g", "hy_conv_w",
          "hy_conv_b", "hf_w1", "hf_b1", "hf_w2", "hf_b2", "hf_w3", "hf_b3", "hf_freq", "hf_w4", "cf_dw_w",
          "cf_dw_b", "cf_ln_g", "cf_ln_b", "b_gu", "b_down", "c")


def packed(inputs):
    v = {k: np.asarray(inputs[k]) for k in PACKED}
    b_ada, b_in = np.asarray(inputs["b_ada"]), np.asarray(inputs["b_in"])
    columns = np.zeros((3, P, P), np.float32)
    parts = [(0, V_ADA, b_ada[0, 0:2 * D]), (0, V_N1, v["norm1_g"]), (0, V_BIN, b_in[0, 3 * W:]),
             (0, V_SUB, v["subln_g"]), (0, V_DWB, v["cf_dw_b"]), (0, V_LNG, v["cf_ln_g"]),
             (0, V_LNB, v["cf_ln_b"]), (0, V_C, v["c"]), (0, V_HYB, v["hy_conv_b"]),
             (1, 0, v["hy_conv_w"]), (2, 0, v["cf_dw_w"])]
    for i, row, x in parts:
        x = x.reshape(-1, P)
        columns[i, row:row + len(x)] = x
    net = np.zeros((HF_HID, 2048 + SEQ + 3 * HF_HID + 4), np.float32)
    net[:, 0:2048] = v["hf_w4"][0]
    net[0:HF_EMB, 2048:2304] = shape_constants()["z_features"]
    net[0:HF_EMB, 2304:2368] = v["hf_w1"][0]
    net[:, 2368:2432] = v["hf_w2"][0]
    net[:, 2432:2496] = v["hf_w3"][0]
    for n, name in enumerate(("hf_b1", "hf_b2", "hf_b3", "hf_freq")):
        net[:, 2496 + n] = v[name][0]
    head_rows = np.concatenate([v[n] for n in ("q_norm_g", "k_norm_g", "lam_q1", "lam_k1", "lam_q2", "lam_k2")],
                               axis=1)
    return {"columns": columns.reshape(3 * P, P).T, "filter_net": net, "head_rows": head_rows,
            "b_experts": np.concatenate([v["b_gu"][0], v["b_down"][0]], axis=1)}


def kernel(**inputs):
    import concourse.bacc as _bacc
    from concourse.bass_utils import run_bass_kernel_spmd as _run

    nc = _bacc.Bacc("TRN2", target_bir_lowering=False, num_devices=1)
    arrays, args = {}, {}
    for name, v in {**inputs, **packed(inputs), **shape_constants()}.items():
        if name in PACKED:
            continue
        v = np.ascontiguousarray(v)
        arrays[name] = v
        args[name] = nc.dram_tensor(name, v.shape, mybir.dt.from_np(v.dtype), kind="ExternalInput").ap()
    out = nc.dram_tensor("layer_out", (1, SEQ, D), F32, kind="ExternalOutput").ap()
    build_layer(nc, args, out)
    r = _run(nc, [arrays], core_ids=[0])
    return r.results[0]["layer_out"]
```

```python
import math
from contextlib import ExitStack

import numpy as np
import concourse.bass as bass
from concourse import mybir

P = 128
D = 1024
SEQ = 256
TT = SEQ // P
KT = D // P
W = 512
WT = W // P
HEADS, HD = 4, 64
GROUPS = 2 * HEADS
HY_T = 3 * WT
BANDS, HF_EMB, HF_HID = 16, 33, 64
TAPS = 31
EXPERTS, TOPK, FF = 32, 4, 1024
EPS = 1e-6
LIMIT, ALPHA = 7.0, 1.702
LAM_INIT = 0.8 - 0.6 * math.exp(-0.3 * 0)
SCALE = HD ** -0.5

WEIGHT_SLOTS = 6
MOE_SLOTS = 8
CHUNK = 4096

SLOTS = 64
PASSES = SEQ // SLOTS
PAIRS = EXPERTS // 2
BODIES = PAIRS // 2
PAIR_CHUNKS = 12
AHEAD = MOE_SLOTS
FAR = 4096.0

F32 = mybir.dt.float32
I32 = mybir.dt.int32
U32 = mybir.dt.uint32
ALU = mybir.AluOpType
ACT = mybir.ActivationFunctionType
AX_X = mybir.AxisListType.X

V_ADA, V_N1, V_BIN, V_SUB, V_DWB, V_LNG, V_LNB, V_C, V_HYB = 0, 16, 24, 68, 69, 73, 77, 81, 89

NET_Z = 2 * W
NET_W = NET_Z + SEQ
NET_B = NET_W + 3 * HF_HID
NET_COLS = NET_B + 4

PI_A, PI_B, PI_C = 6.28125, 0.0019350051879882812, 3.0199159819e-07
ROUND = 12582912.0

HY_CHUNKS, CF_GATE, CF_VALUE, QKV_CHUNKS, GATE_CHUNKS = (3, 4, 5), 7, 6, (0, 1, 2), range(8, 14)


def front_jobs():
    jobs = [("mlp0", "dve"), ("mlp1", "dve"), ("ada0", "act"), ("mlp2", "dve"), ("ada1", "act")]
    jobs += [(f"filter{o}{s}{t}", "dve") for s in range(2) for t in range(TT) for o in range(2)]
    jobs += [("ada2", "act")]
    jobs += [(f"spectrum0{j}", "act") for j in range(5)]
    jobs += [("ada3", "act")]
    jobs += [("xT0", "act"), ("xT2", "act"), ("modcol", "dve"), ("xT1", "dve"), ("xT3", "dve")]
    jobs += [("cg0", "act"), ("cg1", "act"), ("ca0", "dve"), ("ca1", "dve")]
    jobs += [(f"hy{i}", "act") for i in range(6)]
    jobs += [(f"spectrum1{j}", "act") for j in range(5)]
    jobs += [(f"hyT{g}{t}", "act") for g in range(3) for t in range(TT)]
    jobs += [(f"u0{m}", "dve") for m in (0, 2, 1, 3)] + [("q0", "dve"), ("q1", "dve"), ("mean", "dve")]
    jobs += [("inv00", "dve"), ("inv01", "dve"), ("var", "dve"), ("k0", "dve"), ("k1", "dve")]
    jobs += [(f"u1{m}", "dve") for m in (0, 2, 1, 3)] + [("v0", "dve"), ("v1", "dve")]
    jobs += [("inv10", "dve"), ("inv11", "dve"), ("gate0", "act"), ("zT0", "act"), ("zT1", "act")]
    jobs += [(f"qkT{j}{t}", "act") for j in range(2) for t in range(TT)]
    for h in range(HEADS + 2):
        if h < HEADS:
            jobs += [(f"score{h}{c}", "act") for c in range(2)]
        if h:
            jobs += [(f"gate{h}", "act")]
        if h > 1:
            jobs += [(f"o{h - 2}", "dve")]
        if 0 < h <= HEADS:
            jobs += [(f"aT{h - 1}", "act")]
    jobs += [("gate6", "act"), ("gate7", "act"), ("oT0", "act"), ("oT1", "act")]
    jobs += [(f"gate{i}", "act") for i in range(8, 12)]
    jobs += [(f"merge{n}{m}", "dve") for n in range(3) for m in range(4)]
    jobs += [(f"adab{i}", "act") for i in range(8)]
    jobs += [(f"out{t}{c}", "dve") for t in range(TT) for c in range(2)]
    jobs += [(f"h2T{t}{c}", "act") for t in range(TT) for c in range(2)]
    jobs += [("logits", "dve"), ("rank", "dve")]
    return jobs


JOBS = front_jobs()
JOB = {name: n for n, (name, _) in enumerate(JOBS)}
EMPTIED_BY = dict(JOBS)
ORDINAL = {}
for _e in ("act", "dve"):
    for _n, _name in enumerate(n for n, e in JOBS if e == _e):
        ORDINAL[_name] = _n + 1

CHUNKS = [("ada", i, f"ada{i}") for i in range(4)]
CHUNKS += [("in", CF_GATE, "cg1"), ("in", CF_VALUE, "ca1")]
CHUNKS += [("in", c, f"hy{2 * i + 1}") for i, c in enumerate(HY_CHUNKS)]
CHUNKS += [("in", 0, "q1"), ("in", 1, "k1"), ("in", 2, "v1")]
_gates = [("in", c, f"gate{2 * i + 1}") for i, c in enumerate(GATE_CHUNKS)]
_ada = [("ada", 4 + i, i + 1) for i in range(8)]
_branch = [("branch", n, f"merge{n}3") for n in range(3)]
CHUNKS += _gates[0:4] + _ada[0:2] + _gates[4:5] + _ada[2:4] + _gates[5:6] + _ada[4:6]
CHUNKS += _branch[0:1] + _ada[6:7] + _branch[1:2] + _ada[7:8] + _branch[2:3]
CHUNKS += [("wout", i, "out11") for i in range(2)]
CHUNK_NO = {(kind, i): n for n, (kind, i, _) in enumerate(CHUNKS)}
NF = len(CHUNKS)

MISC = [(f"gather{i}", "act") for i in range(4)]
MISC += [("turn_a", "act"), ("hidT_a0", "act"), ("hidT_a1", "act")]
MISC += [(f"add_a{i}", "dve") for i in range(4)]
MISC += [("turn_b", "act"), ("hidT_b0", "act"), ("hidT_b1", "act")]
MISC += [(f"add_b{i}", "dve") for i in range(4)]
MISC_NO = {name: n for n, (name, _) in enumerate(MISC)}
MISC_BY = dict(MISC)
MISC_ORD = {}
MISC_COUNT = {}
for _e in ("act", "dve"):
    _names = [n for n, e in MISC if e == _e]
    MISC_COUNT[_e] = len(_names)
    for _n, _name in enumerate(_names):
        MISC_ORD[_name] = _n + 1


class Steps:

    def __init__(self, eng, sem):
        self.eng, self.sem, self.n = eng, sem, 0

    def __call__(self, instruction):
        instruction.then_inc(self.sem, 1)
        self.n += 1
        return self.n

    def wait(self, n=None):
        self.eng.wait_ge(self.sem, self.n if n is None else n)


class LoopSteps:

    def __init__(self, eng, sem, before):
        self.eng, self.sem, self.before, self.n = eng, sem, before, 0

    def __call__(self, instruction):
        instruction.then_inc(self.sem, 1)
        self.n += 1

    def wait(self):
        self.eng.wait_ge(self.sem, self.before + self.n)


BODY_STEPS = 4


def build_layer(nc, a, out):
    ctx = ExitStack()
    with ctx:
        def sb(name, shape, dt=F32):
            return ctx.enter_context(nc.sbuf_tensor(f"{name}_sb", shape, dt))

        def sem(name):
            return ctx.enter_context(nc.semaphore(name))

        bank = [ctx.enter_context(nc.psum_tensor(f"bank{i}", [P, 512], F32)) for i in range(8)]

        ring = sb("ring", [P, WEIGHT_SLOTS, CHUNK])
        ident = sb("ident", [P, P])
        ones = sb("ones", [P, P])
        vec = sb("vec", [P, 3, P])
        small = sb("small", [P, 256])
        area_1 = sb("area_1", [P, 4096])
        area_2 = sb("area_2", [P, 5120])
        area_3h = sb("area_3h", [P, 6144])
        area_3, area_h = area_3h[:, 0:4096], area_3h[:, 4096:6144]
        area_4 = sb("area_4", [P, 2048])
        area_5 = sb("area_5", [P, 2176])
        area_6 = sb("area_6", [P, 3072])
        area_7 = sb("area_7", [P, 2560])
        area_8 = sb("area_8", [P, 1024])
        rope = sb("rope", [P, 2, TT, HD])
        head_rows = sb("head_rows", [P, 6 * HD])
        gain = head_rows[:, 0:2 * HD].rearrange("p (n d) -> p n d", d=HD)
        lam_v = head_rows[:, 2 * HD:].rearrange("p (n d) -> p n d", d=HD)
        pos = sb("pos", [P, TT, EXPERTS + 4])
        comb = sb("comb", [P, TT, EXPERTS + 4])
        iota = sb("iota", [P, SLOTS])
        before = sb("before", [P, P])
        row_sel = sb("row_sel", [2, P])
        flag = sb("flag", [P, 1], I32)

        def view(area, start, shape):
            n = math.prod(shape)
            v = area[:, start:start + n]
            if len(shape) == 1:
                return v
            names = "abcd"[:len(shape)]
            return v.rearrange(f"p ({' '.join(names)}) -> p {' '.join(names)}",
                               **dict(zip(names[1:], shape[1:])))

        hT = view(area_h, 0, [KT, SEQ])
        merged = hT
        w4 = view(area_1, 0, [2, W])
        w4s = view(area_4, 0, [2, W])
        x_n = view(area_2, 2560, [TT, D])
        hy_in = view(area_1, 0, [HY_T, SEQ + 2])
        hy_cv = view(area_6, 0, [HY_T, SEQ])
        dft_f = view(area_7, 0, [TT, 768])
        dft_i = view(area_7, 1536, [4, SEQ])
        gates = [view(area_7, 0, [KT, SEQ]), view(area_1, 0, [KT, SEQ]), view(area_1, 2048, [KT, SEQ])]
        w_router = view(area_7, 2048, [KT, EXPERTS])
        spectra = view(area_2, 0, [2, 5, W])
        mod_rows = view(area_2, D, [4, D])
        g1, sh2, sc2, g2 = (mod_rows[:, i, :] for i in range(4))

        def mod_half(i):
            return area_2[:, D + i * W:D + (i + 1) * W]

        filt = view(area_3, 0, [TT, 2, 2, W])
        hy = view(area_3, 0, [3, TT, W])
        hy_tmp = view(area_3, 3072, [2, W])
        qkT = view(area_3, 0, [2, HEADS, SEQ])
        prob = view(area_3, 2048, [2, 2, TT, SEQ])
        part = view(area_1, 2048, [4, 512])
        ysp = view(area_4, 0, [4, W])
        br_hy = view(area_4, 0, [WT, SEQ])
        br_at = view(area_4, 1024, [WT, SEQ])
        window = view(area_6, 512, [TT, W])
        x = view(area_5, 0, [TT, D])
        cf_in = view(area_5, 0, [WT, SEQ + TAPS - 1])
        cf_cv = view(area_5, WT * (SEQ + TAPS - 1), [4, SEQ])
        cf_sq = view(area_5, 0, [WT, SEQ])
        ln_ms, ln_rt, ln_r, ln_t = (area_5[:, i * SEQ:(i + 1) * SEQ] for i in range(4))
        attT = view(area_5, 0, [2, TT, SEQ])
        att = view(area_5, 1024, [TT, W])
        qkv = view(area_6, 0, [3, TT, W])
        xT = view(area_1, 0, [KT, 4 * SLOTS])
        hid = view(area_1, 2048, [FF])
        gate_s = view(area_1, 3072, [FF])
        up_s = view(area_7, 0, [FF])
        sig_s = view(area_7, 1024, [FF])
        h2 = view(area_3, 0, [TT, D])
        h2T = hT
        hidT = view(area_4, 0, [KT, P])
        y_s = view(area_4, 1024, [D])
        bias = area_6
        extra_slots = [area_2[:, 0:CHUNK], area_3h[:, 2048:2048 + CHUNK]]
        member = view(area_7, 2048, [TT, 4, SLOTS])
        weighted = view(area_8, 0, [TT, 4, SLOTS])
        turned = view(area_8, 512, [SEQ])
        scratch = view(area_6, 2048, [D])
        squares = view(area_1, 0, [W])
        chosen = view(area_1, 1024, [TT, TOPK, EXPERTS])
        chosen_w = view(area_1, 1280, [TT, TOPK, EXPERTS])

        cond, cond_sig = small[:, 0:8], small[:, 8:16]
        n1_gain = small[:, 16:24]
        shift1 = small[:, 24:32]
        x_ss, x_ms, x_rt, x_r, x_t = (small[:, 32 + 2 * i:34 + 2 * i] for i in range(5))
        lam_s = small[:, 42:48]
        s_max = small[:, 52:68].rearrange("p (h c t) -> p h c t", c=2, t=TT)
        s_sum = small[:, 68:84].rearrange("p (h c t) -> p h c t", c=2, t=TT)
        s_inv = small[:, 84:100].rearrange("p (h c t) -> p h c t", c=2, t=TT)
        o_ms, o_rt, o_r, o_t = (small[:, 100 + 16 * i:116 + 16 * i] for i in range(4))
        top = small[:, 164:180].rearrange("p (t k) -> p t k", t=TT)
        top_w = small[:, 180:188].rearrange("p (t k) -> p t k", t=TT)
        top_s = small[:, 188:194].rearrange("p (t k) -> p t k", t=TT)
        g2_ss, g2_ms, g2_rt, g2_r, g2_t = (small[:, 196 + 2 * i:198 + 2 * i] for i in range(5))
        most = small[:, 206:207]
        x1_ss = small[:, 212:216].rearrange("p (t c) -> p t c", t=TT)
        mean_col = small[:, 208:210]
        sub_gain = small[:, 210:211]
        o_sel = sb("o_sel", [P, 24])
        top_i = sb("top_i", [P, TT, 8], U32)
        top_f = sb("top_f", [P, TT, 8])
        mask = sb("mask", [P, TT, EXPERTS])
        logit = sb("logit", [P, TT, EXPERTS])
        expert_no = sb("expert_no", [P, EXPERTS])
        b_router = sb("b_router", [P, EXPERTS])
        
        cond_rep = view(area_h, 1472, [KT, 32])
        mlp_y = view(area_h, 0, [4, SEQ])
        filter_net = area_1[:, 0:NET_COLS]
        zT = area_1[0:HF_EMB, NET_Z:NET_Z + SEQ]
        mlp_w = area_1[0:HF_HID, NET_W:NET_B].rearrange("p (n m) -> p n m", n=3)
        hf_col = area_1[:, NET_B:NET_COLS]
        qk_ss = sb("qk_ss", [P, 5, 2, GROUPS])
        hy_bias = view(area_8, 0, [2, W])
        br_cf = view(area_8, 0, [WT, SEQ])

        products_ready = sem("products_ready")
        emptied = {"act": sem("emptied_by_act"), "dve": sem("emptied_by_dve")}
        slot_landed = [sem(f"slot_landed{i}") for i in range(WEIGHT_SLOTS)]
        moe_landed = [sem(f"moe_landed{i}") for i in range(MOE_SLOTS)]
        ada_summed = sem("ada_summed")
        consts_made = sem("consts_made")
        vec_landed = sem("vec_landed")
        mlp_landed = sem("mlp_landed")
        x_landed = sem("x_landed")
        x_again_landed = sem("x_again_landed")
        window_landed = sem("window_landed")
        dft_landed = sem("dft_landed")
        hyena_landed = sem("hyena_landed")
        attn_landed = sem("attn_landed")
        router_landed = sem("router_landed")
        mod_bias_landed = sem("mod_bias_landed")
        gain2_landed = sem("gain2_landed")
        dve_step = sem("dve_step")
        act_step = sem("act_step")
        pool_step = sem("pool_step")
        sqrt_asked = sem("sqrt_asked")
        sqrt_done = sem("sqrt_done")
        sin_asked = sem("sin_asked")
        sin_done = sem("sin_done")
        w4_summed = sem("w4_summed")
        cond_ready = sem("cond_ready")
        xn_ready = sem("xn_ready")
        x_squared = sem("x_squared")
        r_ready = sem("r_ready")
        modcol_ready = sem("modcol_ready")
        hy_conv_done = sem("hy_conv_done")
        pads_zeroed = sem("pads_zeroed")
        sig_ready = sem("sig_ready")
        spectra_mixed = sem("spectra_mixed")
        z_ready = sem("z_ready")
        conv_done = sem("conv_done")
        centred = sem("centred")
        cf_scaled = sem("cf_scaled")
        cf_act = sem("cf_act")
        br_cf_ready = sem("br_cf_ready")
        roped = sem("roped")
        max_ready = sem("max_ready")
        lam_ready = sem("lam_ready")
        lam_exp = sem("lam_exp")
        att_ready = sem("att_ready")
        o_ready = sem("o_ready")
        gates_ready = sem("gates_ready")
        mod_zeroed = sem("mod_zeroed")
        merged_ready = sem("merged_ready")
        h2_ready = sem("h2_ready")
        top_ready = sem("top_ready")
        top_exp = sem("top_exp")
        mask_ready = sem("mask_ready")
        flag_ready = sem("flag_ready")
        stored = sem("stored")
        out_ready = sem("out_ready")
        weights_used = sem("weights_used")
        gate_up_done = sem("gate_up_done")
        gate_up_read = sem("gate_up_read")
        y_done = sem("y_done")
        y_read = sem("y_read")
        misc_done = sem("misc_done")
        misc_out = {"act": sem("misc_out_act"), "dve": sem("misc_out_dve")}
        bias_landed = sem("bias_landed")
        bias_used = sem("bias_used")
        gate_min = sem("gate_min")
        sigmoid_done = sem("sigmoid_done")
        hid_ready = sem("hid_ready")
        member_ready = sem("member_ready")
        weighted_ready = sem("weighted_ready")
        moe_step = sem("moe_step")
        moe_primed = sem("moe_primed")
        pass_step = sem("pass_step")

        def slot_of(kind, i):
            return ring[:, CHUNK_NO[kind, i] % WEIGHT_SLOTS, :]

        def wait_chunk(eng, kind, i):
            n = CHUNK_NO[kind, i]
            eng.wait_ge(slot_landed[n % WEIGHT_SLOTS], 16 * (n // WEIGHT_SLOTS + 1))

        def wait_emptied(eng, name):
            eng.wait_ge(emptied[EMPTIED_BY[name]], ORDINAL[name])

        def open_bank(pe, name):
            n = JOB[name]
            if n >= 8:
                wait_emptied(pe, JOBS[n - 8][0])
            return bank[n % 8]

        def product(eng, name):
            eng.wait_ge(products_ready, JOB[name] + 1)
            return bank[JOB[name] % 8]

        def chunk_source(kind, i):
            if kind == "ada":
                return a["w_ada"][0, :, i * W:(i + 1) * W].rearrange("(k p) m -> p k m", p=P)
            if kind == "in":
                return a["w_in"][0, :, i * W:(i + 1) * W].rearrange("(k p) m -> p k m", p=P)
            if kind == "branch":
                return a["w_branch"][0, i].rearrange("(k p) m -> p k m", p=P)
            return a["w_out"][0, i * W:(i + 1) * W, :].rearrange("(k p) m -> p k m", p=P)

        def slot_view(kind, i):
            cols = W if kind in ("ada", "in") else D
            return slot_of(kind, i).rearrange("p (k m) -> p k m", m=cols)

        def moe_slot(b, c):
            n = (PAIR_CHUNKS * b + c) % MOE_SLOTS
            return ring[:, (NF + n) % WEIGHT_SLOTS, :] if n < WEIGHT_SLOTS else extra_slots[n - WEIGHT_SLOTS]

        def moe_chunk_landed(b, c):
            return moe_landed[(PAIR_CHUNKS * b + c) % MOE_SLOTS]

        def wait_moe_chunk(eng, i, b, c):
            per_body = 2 * PAIR_CHUNKS // MOE_SLOTS
            eng.wait_ge(moe_chunk_landed(b, c),
                        i * (16 * per_body) + 16 * ((PAIR_CHUNKS * b + c) // MOE_SLOTS + 1))

        def moe_bank(name):
            return bank[6 + MISC_NO[name] % 2]

        def open_misc(pe, i, name):
            n = MISC_NO[name]
            prev = MISC[n - 2][0]
            by = MISC_BY[prev]
            body = 1 if n >= 2 else 0
            pe.wait_ge(misc_out[by], i * MISC_COUNT[by] + body * MISC_COUNT[by] + MISC_ORD[prev])
            return moe_bank(name)

        def misc_product(eng, i, name):
            eng.wait_ge(misc_done, i * len(MISC) + MISC_NO[name] + 1)
            return moe_bank(name)

        def wait_misc_out(pe, i, name):
            by = MISC_BY[name]
            pe.wait_ge(misc_out[by], i * MISC_COUNT[by] + MISC_COUNT[by] + MISC_ORD[name])

        block = ctx.enter_context(nc.Block())

        @block.sync
        def _(sp):
            sp.dma_start(vec[:, :, :], a["columns"].rearrange("p (i j) -> p i j", j=P)).then_inc(vec_landed, 16)
            sp.dma_start(filter_net, a["filter_net"]).then_inc(mlp_landed, 16)

            def load_chunk(n):
                kind, i, _ = CHUNKS[n]
                if n >= WEIGHT_SLOTS:
                    wait_freed(n - WEIGHT_SLOTS)
                sp.dma_start(slot_view(kind, i), chunk_source(kind, i))\
                    .then_inc(slot_landed[n % WEIGHT_SLOTS], 16)

            def wait_freed(n):
                user = CHUNKS[n][2]
                if isinstance(user, str):
                    sp.wait_ge(products_ready, JOB[user] + 1)
                else:
                    sp.wait_ge(ada_summed, user)

            load_chunk(0)
            sp.dma_start(x[:, :, :], a["x"][0].rearrange("(t p) m -> p t m", p=P)).then_inc(x_landed, 16)
            load_chunk(1)
            sp.dma_start(window, a["window"].rearrange("(t p) m -> p t m", p=P)).then_inc(window_landed, 16)
            load_chunk(2)
            sp.dma_start(dft_f, a["dft_f"].rearrange("(t p) m -> p t m", p=P)).then_inc(dft_landed, 16)
            load_chunk(3)
            load_chunk(4)
            sp.dma_start(dft_i, a["dft_i"].rearrange("(t p) m -> p t m", p=P)).then_inc(hyena_landed, 16)
            sp.dma_start(hy_bias, a["hy_bias"][0:1].to_broadcast([P, 2, W])).then_inc(hyena_landed, 16)
            for n in range(5, NF):
                load_chunk(n)

            def wait_used(i, b, c):
                if c < 7:
                    sp.wait_ge(weights_used, i * 20 + 10 * b + c + 1)
                elif c == 7:
                    sp.wait_ge(gate_up_done, i * 4 + 2 * b + 2)
                elif c < 11:
                    sp.wait_ge(weights_used, i * 20 + 10 * b + c)
                else:
                    sp.wait_ge(y_done, i * 4 + 2 * b + 2)

            def wait_slot(i, b, c):
                if c >= MOE_SLOTS:
                    wait_used(i, b, c - MOE_SLOTS)
                else:
                    wait_used(i, b - 1, c - MOE_SLOTS + PAIR_CHUNKS)

            def load_moe(b, c, j):
                e0 = j * 4 + 2 * b
                dst = moe_slot(b, c).rearrange("p (e m) -> p e m", e=2)
                if c < 8:
                    src = a["w_gu"][0, bass.ds(e0, 2), c * P:(c + 1) * P, :].rearrange("e p m -> p e m")
                else:
                    k = 2 * (c - 8)
                    src = a["w_down"][0, bass.ds(e0, 2), k * P:(k + 2) * P, :]\
                        .rearrange("e (p k) m -> p e (k m)", k=2)
                sp.dma_start(dst, src).then_inc(moe_chunk_landed(b, c), 16)

            def load_bias(b, j):
                e0 = j * 4 + 2 * b
                sp.dma_start(bias[0:2, :], a["b_experts"][bass.ds(e0, 2), :]).then_inc(bias_landed, 16)

            def body(i, j, last):
                for b in range(2):
                    for c in range(AHEAD, PAIR_CHUNKS):
                        wait_slot(i, b, c)
                        load_moe(b, c, j)
                    if not (last and b == 1):
                        for c in range(AHEAD):
                            wait_slot(i, b + 1, c)
                            if c == 4:
                                load_bias(b + 1, j)
                            load_moe(b + 1, c, j)

            def one_pass(p, first=False):
                i0 = p * BODIES
                for c in range(AHEAD):
                    if not first:
                        wait_slot(i0, 0, c)
                    elif c < WEIGHT_SLOTS:
                        wait_freed(NF + c - WEIGHT_SLOTS)
                    elif c == WEIGHT_SLOTS:
                        sp.wait_ge(h2_ready, 2 * TT)
                    else:
                        sp.wait_ge(products_ready, JOB["logits"] + 1)
                    if c == 6:
                        load_bias(0, 0)
                    load_moe(0, c, 0)
                with sp.Fori(0, BODIES - 1) as j:
                    body(i0 + j, j, False)
                body(i0 + (BODIES - 1), BODIES - 1, True)

            one_pass(0, first=True)
            sp.wait_ge(flag_ready, 1)
            over = sp.value_load(flag[0:1, 0:1], min_val=0, max_val=SEQ)
            with sp.If(over > SLOTS):
                with sp.Fori(1, PASSES) as p:
                    one_pass(p)

            for t in range(TT):
                if t == 0:
                    sp.wait_ge(out_ready, 1)
                sp.dma_start(out[0, t * P:(t + 1) * P, :], x[:, t, :]).then_inc(stored, 16)
            sp.wait_ge(stored, 16 * TT)

        @block.gpsimd
        def _(pool):
            step = Steps(pool, pool_step)
            step(pool.memset(ident[:, :], 0.0))
            step(pool.memset(before[:, :], 1.0))
            step(pool.memset(row_sel[:, :], 1.0))
            step.wait()
            step(pool.affine_select(out=ident[:, :], in_=ident[:, :], compare_op=ALU.not_equal, fill=1.0,
                                    base=0, pattern=[[-1, P]], channel_multiplier=1))
            step(pool.affine_select(out=before[:, :], in_=before[:, :], compare_op=ALU.is_gt, fill=0.0,
                                    base=0, pattern=[[1, P]], channel_multiplier=-1))
            step(pool.affine_select(out=row_sel[:, :], in_=row_sel[:, :], compare_op=ALU.is_ge, fill=0.0,
                                    base=0, pattern=[[1, P]], channel_multiplier=-SLOTS))
            step.wait()
            step(pool.affine_select(out=row_sel[:, :], in_=row_sel[:, :], compare_op=ALU.is_ge, fill=0.0,
                                    base=SLOTS - 1, pattern=[[-1, P]], channel_multiplier=SLOTS))
            step(pool.iota(iota[:, :], pattern=[[1, SLOTS]], base=0, channel_multiplier=0,
                           allow_small_or_imprecise_dtypes=True))
            step(pool.iota(expert_no[:, :], pattern=[[1, EXPERTS]], base=0, channel_multiplier=0,
                           allow_small_or_imprecise_dtypes=True))
            step(pool.memset(ones[:, :], 1.0))
            step(pool.memset(pos[:, :, :], FAR))
            step(pool.memset(comb[:, :, :], 0.0))
            step.wait()
            pool.memset(mean_col, 1.0 / 32).then_inc(consts_made, 1)
            pool.wait_ge(products_ready, JOB["hyT21"] + 1)
            for t in range(TT):
                pool.dma_start(qkv[:, :, t, :], a["b_in"][0:1, 0:3 * W].rearrange("o (j m) -> o j m", m=W)
                               .to_broadcast([P, 3, W])).then_inc(attn_landed, 16)
            pool.dma_start(rope[:, :, :, :], a["rope"].rearrange("c (t p) m -> p c t m", p=P)).then_inc(attn_landed, 16)
            pool.dma_start(head_rows[:, :], a["head_rows"].to_broadcast([P, 6 * HD])).then_inc(attn_landed, 16)
            pool.wait_ge(products_ready, JOB["inv11"] + 1)
            pool.dma_start(w_router[:, :, :], a["w_router"][0].rearrange("(k p) m -> p k m", p=P)).then_inc(router_landed, 16)
            pool.dma_start(b_router[:, :], a["b_router"].to_broadcast([P, EXPERTS])).then_inc(router_landed, 16)
            pool.wait_ge(spectra_mixed, 4)
            pool.memset(mod_rows[:, :, :], 0.0).then_inc(mod_zeroed, 1)
            pool.wait_ge(mod_zeroed, 1)
            pool.dma_start(area_2[0:1, D:5 * D], a["b_ada"][0:1, 2 * D:6 * D]).then_inc(mod_bias_landed, 16)
            pool.wait_ge(products_ready, JOB["oT1"] + 1)
            pool.dma_start(x[:, :, :], a["x"][0].rearrange("(t p) m -> p t m", p=P)).then_inc(x_again_landed, 16)
            pool.dma_start(scratch, a["norm2_g"].to_broadcast([P, D])).then_inc(gain2_landed, 16)

        @block.tensor
        def _(pe):
            def job(name):
                return open_bank(pe, name)

            def end(ins):
                ins.then_inc(products_ready, 1)

            pe.wait_ge(consts_made, 1)
            pe.wait_ge(mlp_landed, 16)
            def ada(i):
                b = job(f"ada{i}")
                w = slot_view("ada", i)
                pe.wait_ge(cond_ready, 1)
                wait_chunk(pe, "ada", i)
                for k in range(KT):
                    g = k % 4
                    ins = pe.matmul(b[32 * g:32 * g + 32, :], cond_rep[:, k, :], w[:, k, :],
                                    start=k < 4, stop=k >= 4, skip_group_check=True)
                end(ins)

            def spectrum(o):
                parts = [(0, 0), (P, 0), (512, 0), (640, 1), (384, 1)]
                for j, (col, s) in enumerate(parts):
                    b = job(f"spectrum{o}{j}")
                    for t in range(TT):
                        ins = pe.matmul(b[:, :], dft_f[:, t, col:col + P], filt[:, t, o, s, :],
                                        start=t == 0, stop=t == TT - 1)
                    end(ins)

            def mlp(n):
                b = job(f"mlp{n}")
                w, x_in = (mlp_w[0:HF_EMB, 0, :], zT[:, :]) if n == 0 else (mlp_w[:, n, :], mlp_y[0:HF_HID, 3, :])
                if n:
                    pe.wait_ge(sin_done, n)
                for half in range(2):
                    ins = pe.matmul(b[half * HF_HID:(half + 1) * HF_HID, 0:SEQ], w, x_in, start=True, stop=True)
                end(ins)

            mlp(0)
            mlp(1)
            ada(0)
            mlp(2)
            ada(1)
            pe.wait_ge(sin_done, 3)
            pe.wait_ge(w4_summed, 1)
            for s in range(2):
                for t in range(TT):
                    for o in range(2):
                        b = job(f"filter{o}{s}{t}")
                        r = slice(o * HF_HID, (o + 1) * HF_HID)
                        end(pe.matmul(b[:, :], mlp_y[r, 3, t * P:(t + 1) * P], w4s[r, s, :],
                                      start=True, stop=True))
            ada(2)
            pe.wait_ge(dft_landed, 16)
            wait_emptied(pe, "filter011")
            spectrum(0)
            ada(3)
            pe.wait_ge(xn_ready, TT)

            def turn_x(i):
                b = job(f"xT{i}")
                for kk in range(2):
                    for t in range(TT):
                        c = (2 * i + kk) * P
                        ins = pe.transpose(b[:, (kk * TT + t) * P:(kk * TT + t + 1) * P],
                                           x_n[:, t, c:c + P], ident[:, :])
                end(ins)

            turn_x(0)
            turn_x(2)
            b = job("modcol")
            for i in range(4):
                wait_emptied(pe, f"ada{i}")
                for m in range(4):
                    c = 4 * i + m
                    ins = pe.matmul(b[:, c:c + 1], part[:, i, m * P:(m + 1) * P], mean_col[:, 0:1],
                                    start=True, stop=True)
            end(ins)
            turn_x(1)
            turn_x(3)

            def channel_major(name, kind, i, m0):
                b = job(name)
                w = slot_view(kind, i)
                wait_chunk(pe, kind, i)
                for m in range(2):
                    for k in range(KT):
                        ins = pe.matmul(b[:, m * SEQ:(m + 1) * SEQ], w[:, k, (m0 + m) * P:(m0 + m + 1) * P],
                                        hT[:, k, :], start=k == 0, stop=k == KT - 1)
                end(ins)

            def token_major(name, i, t):
                b = job(name)
                w = slot_view("in", i)
                wait_chunk(pe, "in", i)
                for k in range(KT):
                    ins = pe.matmul(b[:, :], hT[:, k, t * P:(t + 1) * P], w[:, k, :],
                                    start=k == 0, stop=k == KT - 1)
                end(ins)

            wait_emptied(pe, "xT2")
            wait_emptied(pe, "xT3")
            for i in range(2):
                channel_major(f"cg{i}", "in", CF_GATE, 2 * i)
            for i in range(2):
                channel_major(f"ca{i}", "in", CF_VALUE, 2 * i)
            for i in range(6):
                channel_major(f"hy{i}", "in", HY_CHUNKS[i // 2], 2 * (i % 2))
            wait_emptied(pe, "filter111")
            spectrum(1)

            for g in range(3):
                pe.wait_ge(hy_conv_done, WT * (g + 1))
                for t in range(TT):
                    b = job(f"hyT{g}{t}")
                    for m in range(WT):
                        ins = pe.transpose(b[:, m * P:(m + 1) * P],
                                           hy_cv[:, g * WT + m, t * P:(t + 1) * P], ident[:, :])
                    end(ins)

            def to_frequency(o):
                for m in (0, 2, 1, 3):
                    b = job(f"u{o}{m}")
                    for t in range(TT):
                        ins = pe.matmul(b[:, :], dft_f[:, t, m * P:(m + 1) * P], hy[:, 0, t, :],
                                        start=t == 0, stop=t == TT - 1)
                    end(ins)

            def to_time(o):
                pe.wait_ge(spectra_mixed, 2 * o + 2)
                for t in range(TT):
                    b = job(f"inv{o}{t}")
                    for m in range(4):
                        ins = pe.matmul(b[:, :], dft_i[:, m, t * P:(t + 1) * P], ysp[:, m, :],
                                        start=m == 0, stop=m == 3)
                    end(ins)

            wait_emptied(pe, "hyT01")
            to_frequency(0)
            for t in range(TT):
                token_major(f"q{t}", 0, t)
            b = job("mean")
            pe.wait_ge(conv_done, 1)
            for m in range(WT):
                ins = pe.matmul(b[:, 0:SEQ], ones[:, :], cf_cv[:, m, :], start=m == 0, stop=m == WT - 1)
            end(ins)
            pe.wait_ge(hyena_landed, 32)
            to_time(0)
            b = job("var")
            pe.wait_ge(centred, 1)
            for m in range(WT):
                ins = pe.matmul(b[:, 0:SEQ], ones[:, :], cf_sq[:, m, :], start=m == 0, stop=m == WT - 1)
            end(ins)
            for t in range(TT):
                token_major(f"k{t}", 1, t)
            pe.wait_ge(z_ready, TT)
            to_frequency(1)
            for t in range(TT):
                token_major(f"v{t}", 2, t)
            to_time(1)

            def gate(i):
                channel_major(f"gate{i}", "in", GATE_CHUNKS[i // 2], 2 * (i % 2))

            gate(0)
            pe.wait_ge(z_ready, 2 * TT)
            for i in range(2):
                b = job(f"zT{i}")
                for m in range(2):
                    for t in range(TT):
                        c = (2 * i + m) * P
                        ins = pe.transpose(b[:, (m * TT + t) * P:(m * TT + t + 1) * P],
                                           hy[:, 0, t, c:c + P], ident[:, :])
                end(ins)
            for j in range(2):
                for t in range(TT):
                    b = job(f"qkT{j}{t}")
                    pe.wait_ge(roped, TT * j + t + 1)
                    for h in range(HEADS):
                        ins = pe.transpose(b[:, h * P:(h + 1) * P], qkv[:, j, t, h * P:(h + 1) * P], ident[:, :])
                    end(ins)
            wait_emptied(pe, "qkT11")

            def scores(h):
                for c in range(2):
                    b = job(f"score{h}{c}")
                    r = slice(c * HD, (c + 1) * HD)
                    for t in range(TT):
                        ins = pe.matmul(b[:, t * SEQ:(t + 1) * SEQ], qkT[r, 0, h, t * P:(t + 1) * P],
                                        qkT[r, 1, h, :], start=True, stop=True)
                    end(ins)

            def turn_weights(h):
                b = job(f"aT{h}")
                pe.wait_ge(att_ready, h + 1)
                for kt in range(TT):
                    for t in range(TT):
                        ins = pe.transpose(b[:, kt * SEQ + t * P:kt * SEQ + (t + 1) * P],
                                           prob[:, h % 2, 0, t, kt * P:(kt + 1) * P], ident[:, :])
                end(ins)

            def attend(h):
                b = job(f"o{h}")
                wait_emptied(pe, f"aT{h}")
                wait_emptied(pe, "v1")
                for t in range(TT):
                    for kt in range(TT):
                        ins = pe.matmul(b[:, t * P:(t + 1) * P], attT[:, h % 2, kt, t * P:(t + 1) * P],
                                        qkv[:, 2, kt, h * P:(h + 1) * P], start=kt == 0, stop=kt == TT - 1)
                end(ins)

            for h in range(HEADS + 2):
                if h < HEADS:
                    scores(h)
                if h:
                    gate(h)
                if h > 1:
                    attend(h - 2)
                if 0 < h <= HEADS:
                    turn_weights(h - 1)
            gate(6)
            gate(7)
            pe.wait_ge(o_ready, 1)
            for i in range(2):
                b = job(f"oT{i}")
                for m in range(2):
                    for t in range(TT):
                        c = (2 * i + m) * P
                        ins = pe.transpose(b[:, (m * TT + t) * P:(m * TT + t + 1) * P],
                                           att[:, t, c:c + P], ident[:, :])
                end(ins)
            for i in range(8, 12):
                gate(i)

            def ada_rows(i):
                b = job(f"adab{i}")
                pe.wait_ge(ada_summed, i + 1)
                end(pe.matmul(b[:, :], ones[:, :], mod_half(i), start=True, stop=True))

            def merge(n, branch):
                w = slot_view("branch", n)
                wait_chunk(pe, "branch", n)
                for mp in range(4):
                    b = job(f"merge{n}{mp}")
                    for m in range(2):
                        c = (2 * mp + m) * P
                        for k in range(WT):
                            ins = pe.matmul(b[:, m * SEQ:(m + 1) * SEQ], w[:, k, c:c + P],
                                            branch[:, k, :], start=k == 0, stop=k == WT - 1)
                    end(ins)

            wait_emptied(pe, "oT1")
            merge(0, br_at)
            wait_emptied(pe, "zT1")
            merge(1, br_hy)
            pe.wait_ge(br_cf_ready, 1)
            merge(2, br_cf)
            for i in range(8):
                ada_rows(i)
            for i in range(2):
                wait_chunk(pe, "wout", i)
            pe.wait_ge(merged_ready, 4)
            for t in range(TT):
                for c in range(2):
                    b = job(f"out{t}{c}")
                    for k in range(KT):
                        w = slot_view("wout", k // WT)
                        ins = pe.matmul(b[:, :], merged[:, k, t * P:(t + 1) * P],
                                        w[:, k % WT, c * W:(c + 1) * W], start=k == 0, stop=k == KT - 1)
                    end(ins)
            for t in range(TT):
                for c in range(2):
                    b = job(f"h2T{t}{c}")
                    pe.wait_ge(h2_ready, 2 * t + c + 1)
                    for k in range(4):
                        ins = pe.transpose(b[:, k * P:(k + 1) * P], h2[:, t, c * W + k * P:c * W + (k + 1) * P],
                                           ident[:, :])
                    end(ins)
            b = job("logits")
            pe.wait_ge(router_landed, 32)
            for t in range(TT):
                wait_emptied(pe, f"h2T{t}1")
                for k in range(KT):
                    ins = pe.matmul(b[:, t * EXPERTS:(t + 1) * EXPERTS], h2T[:, k, t * P:(t + 1) * P],
                                    w_router[:, k, :], start=k == 0, stop=k == KT - 1)
            end(ins)
            b = job("rank")
            pe.wait_ge(mask_ready, 1)
            pe.matmul(b[:, 0:EXPERTS], before[:, :], mask[:, 0, :], start=True, stop=True)
            pe.matmul(b[:, EXPERTS:2 * EXPERTS], before[:, :], mask[:, 1, :], start=True, stop=False)
            pe.matmul(b[:, EXPERTS:2 * EXPERTS], ones[:, :], mask[:, 0, :], start=False, stop=True)
            pe.matmul(b[:, 64:64 + EXPERTS], ones[:, :], mask[:, 0, :], start=True, stop=False)
            end(pe.matmul(b[:, 64:64 + EXPERTS], ones[:, :], mask[:, 1, :], start=False, stop=True))
            def misc_end(ins):
                ins.then_inc(misc_done, 1)

            def gather(i, g):
                o = open_misc(pe, i, f"gather{g}")
                for kk in range(2):
                    c = (2 * g + kk) * P
                    for t in range(TT):
                        ins = pe.matmul(o[:, kk * 256:(kk + 1) * 256], h2[:, t, c:c + P],
                                        member[:, t, :, :].rearrange("p e s -> p (e s)"),
                                        start=t == 0, stop=t == TT - 1)
                misc_end(ins)

            def gate_up(i, b, p):
                pe.wait_ge(bias_landed, i * 32 + 16 * (b + 1))
                pe.wait_ge(gate_up_read, i * 4 + 4 + 2 * b)
                for n in range(4):
                    ins = pe.matmul(bank[n][:, :], row_sel[:, :], bias[0:2, n * 512:(n + 1) * 512],
                                    start=True, stop=False, skip_group_check=True)
                if b == 0:
                    pe.wait_ge(member_ready, (i + p) * 2 + 2)
                    gather(i, 0)
                for k in range(KT):
                    if b == 0 and k % 2 == 0:
                        if k // 2 < 3:
                            gather(i, k // 2 + 1)
                        wait_misc_out(pe, i, f"gather{k // 2}")
                    wait_moe_chunk(pe, i, b, k)
                    w = moe_slot(b, k).rearrange("p (e m) -> p e m", e=2)
                    for n in (0, 2, 1, 3):
                        for e in range(2):
                            r = slice(e * SLOTS, (e + 1) * SLOTS)
                            c = b * 2 * SLOTS + e * SLOTS
                            ins = pe.matmul(bank[n][r, :], xT[:, k, c:c + SLOTS],
                                            w[:, e, n * 512:(n + 1) * 512],
                                            start=False, stop=k == KT - 1, skip_group_check=True)
                        if k == KT - 1 and n in (2, 3):
                            ins.then_inc(gate_up_done, 1)
                    if k < KT - 1:
                        ins.then_inc(weights_used, 1)

            def turn(i, name, b, p):
                pe.wait_ge(weighted_ready, (i + p) * 2 + 2)
                o = open_misc(pe, i, name)
                for t in range(TT):
                    ins = pe.transpose(o[:, t * P:(t + 1) * P],
                                       weighted[:, t, 2 * b:2 * b + 2, :].rearrange("p e s -> p (e s)"),
                                       ident[:, :])
                misc_end(ins)

            def hidden_turn(i, name, b, half):
                o = open_misc(pe, i, name)
                pe.wait_ge(hid_ready, i * 4 + 2 * b + half + 1)
                for m in range(4):
                    c = 2 * P * (2 * half + m // 2) + m % 2
                    ins = pe.transpose(o[:, m * P:(m + 1) * P], hid[:, c:c + 2 * P - 1:2], ident[:, :])
                misc_end(ins)

            def down(i, b, s):
                pe.wait_ge(y_read, i * 4 + 4 + 2 * b)
                for n in range(2):
                    ins = pe.matmul(bank[4 + n][:, :], row_sel[:, :], bias[0:2, (4 + n) * 512:(5 + n) * 512],
                                    start=True, stop=False, skip_group_check=True)
                ins.then_inc(bias_used, 1)
                for ch in range(4):
                    wait_moe_chunk(pe, i, b, 8 + ch)
                    if ch % 2 == 0:
                        wait_misc_out(pe, i, f"hidT_{s}{ch // 2}")
                    w = moe_slot(b, 8 + ch).rearrange("p (e k m) -> p e k m", e=2, k=2)
                    for n in range(2):
                        for kk in range(2):
                            k = 2 * ch + kk
                            for e in range(2):
                                r = slice(e * SLOTS, (e + 1) * SLOTS)
                                ins = pe.matmul(bank[4 + n][r, :], hidT[:, k, e * SLOTS:(e + 1) * SLOTS],
                                                w[:, e, kk, n * 512:(n + 1) * 512],
                                                start=False, stop=k == KT - 1, skip_group_check=True)
                        if ch == 3:
                            ins.then_inc(y_done, 1)
                    if ch < 3:
                        ins.then_inc(weights_used, 1)

            def scatter(i, s, b):
                pe.wait_ge(y_read, i * 4 + 4 + 2 * b + 2)
                for t in range(TT):
                    for c in range(2):
                        o = open_misc(pe, i, f"add_{s}{2 * t + c}")
                        misc_end(pe.matmul(o[:, :], turned[:, t * P:(t + 1) * P], y_s[:, c * W:(c + 1) * W],
                                           start=True, stop=True))

            def body(i, p):
                gate_up(i, 0, p)
                turn(i, "turn_a", 0, p)
                hidden_turn(i, "hidT_a0", 0, 0)
                hidden_turn(i, "hidT_a1", 0, 1)
                down(i, 0, "a")
                gate_up(i, 1, p)
                scatter(i, "a", 0)
                turn(i, "turn_b", 1, p)
                hidden_turn(i, "hidT_b0", 1, 0)
                hidden_turn(i, "hidT_b1", 1, 1)
                down(i, 1, "b")
                scatter(i, "b", 1)

            def one_pass(p):
                with pe.Fori(0, BODIES) as j:
                    body(p * BODIES + j, p)

            pe.wait_ge(moe_primed, 2)
            one_pass(0)
            pe.wait_ge(flag_ready, 1)
            over = pe.value_load(flag[0:1, 0:1], min_val=0, max_val=SEQ)
            with pe.If(over > SLOTS):
                with pe.Fori(1, PASSES) as p:
                    one_pass(p)

        @block.scalar
        def _(act):
            step = Steps(act, act_step)

            def out_of(name, ins):
                ins.then_inc(emptied["act"], 1)

            def copy_out(name, dst, cols=None):
                b = product(act, name)
                out_of(name, act.activation(dst, b[:, 0:cols] if cols else b[:, :], ACT.Copy))

            def root(n, dst, src):
                act.wait_ge(sqrt_asked, n)
                act.activation(dst, src, ACT.Sqrt).then_inc(sqrt_done, 1)

            act.wait_ge(vec_landed, 16)
            act.activation(cond_sig, vec[:, 0, V_C:V_C + KT], ACT.Sigmoid).then_inc(sig_ready, 1)
            def sine(n):
                act.wait_ge(sin_asked, n)
                act.activation(mlp_y[:, 3, :], mlp_y[:, 0, :], ACT.Sin).then_inc(sin_done, 1)

            sine(1)
            sine(2)
            copy_out("ada0", part[:, 0, :])
            act.wait_ge(x_landed, 16)
            for t in range(TT):
                act.activation(x_n[:, t, :], x[:, t, :], ACT.Square, accum_out=x_ss[:, t:t + 1])\
                    .then_inc(x_squared, 1)
            sine(3)
            root(1, x_rt, x_ms)
            copy_out("ada1", part[:, 1, :])
            act.wait_ge(r_ready, 1)
            act.wait_ge(x_squared, TT)
            for t in range(TT):
                act.activation(x_n[:, t, :], x[:, t, :], ACT.Copy, scale=x_r[:, t:t + 1]).then_inc(xn_ready, 1)
            copy_out("ada2", part[:, 2, :])
            for j in range(5):
                copy_out(f"spectrum0{j}", spectra[:, 0, j, :])
            copy_out("ada3", part[:, 3, :])
            act.wait_ge(modcol_ready, 1)
            for i in (0, 2):
                b = product(act, f"xT{i}")
                act.activation(hT[:, 2 * i, :], b[:, 0:SEQ], ACT.Identity,
                               bias=shift1[:, 2 * i:2 * i + 1], scale=n1_gain[:, 2 * i:2 * i + 1])
                out_of("", act.activation(hT[:, 2 * i + 1, :], b[:, SEQ:2 * SEQ], ACT.Identity,
                                          bias=shift1[:, 2 * i + 1:2 * i + 2],
                                          scale=n1_gain[:, 2 * i + 1:2 * i + 2]))
            act.wait_ge(products_ready, JOB["modcol"] + 1)
            act.wait_ge(pads_zeroed, 1)
            for i in range(2):
                b = product(act, f"cg{i}")
                for m in range(2):
                    c = 2 * i + m
                    bias = V_BIN + HY_T + WT + c
                    ins = act.activation(cf_cv[:, c, :], b[:, m * SEQ:(m + 1) * SEQ], ACT.Sigmoid,
                                         bias=vec[:, 0, bias:bias + 1])
                out_of("", ins)
            for i in range(6):
                b = product(act, f"hy{i}")
                for m in range(2):
                    c = 2 * i + m
                    ins = act.activation(hy_in[:, c, 1:SEQ + 1], b[:, m * SEQ:(m + 1) * SEQ], ACT.Identity,
                                         bias=vec[:, 0, V_BIN + c:V_BIN + c + 1])
                out_of("", ins)
            for j in range(5):
                copy_out(f"spectrum1{j}", spectra[:, 1, j, :])
            for g in range(3):
                for t in range(TT):
                    copy_out(f"hyT{g}{t}", hy[:, g, t, :])

            def gate_out(i):
                b = product(act, f"gate{i}")
                for m in range(2):
                    c = 2 * i + m
                    bias = V_BIN + HY_T + 2 * WT + c
                    ins = act.activation(gates[c // KT][:, c % KT, :], b[:, m * SEQ:(m + 1) * SEQ],
                                         ACT.Identity, bias=vec[:, 0, bias:bias + 1])
                out_of("", ins)

            root(2, ln_rt, ln_ms)
            root(3, qk_ss[:, 1, :, :], qk_ss[:, 0, :, :])
            root(4, qk_ss[:, 1, :, :], qk_ss[:, 0, :, :])
            gate_out(0)
            for i in range(2):
                copy_out(f"zT{i}", br_hy[:, 2 * i:2 * i + 2, :].rearrange("p m s -> p (m s)"))
            for j in range(2):
                for t in range(TT):
                    b = product(act, f"qkT{j}{t}")
                    out_of("", act.activation(qkT[:, j, :, t * P:(t + 1) * P],
                                              b[:, :].rearrange("p (h s) -> p h s", h=HEADS), ACT.Copy))
            for m in range(WT):
                act.wait_ge(cf_scaled, m + 1)
                act.activation(cf_cv[:, m, :], br_cf[:, m, :], ACT.Sigmoid).then_inc(cf_act, 1)
            act.wait_ge(lam_ready, 2)
            act.activation(lam_s[:, 2:4], lam_s[:, 0:2], ACT.Exp).then_inc(lam_exp, 1)
            for h in range(HEADS + 2):
                if h < HEADS:
                    for c in range(2):
                        act.wait_ge(max_ready, 2 * h + c + 1)
                        b = product(act, f"score{h}{c}")
                        for t in range(TT):
                            ins = act.activation(prob[:, h % 2, c, t, :], b[:, t * SEQ:(t + 1) * SEQ], ACT.Exp,
                                                 bias=s_max[:, h, c, t:t + 1], scale=SCALE,
                                                 accum_out=s_sum[:, h, c, t:t + 1])
                        out_of("", ins)
                if h:
                    gate_out(h)
                if 0 < h <= HEADS:
                    if h == 1:
                        act.wait_ge(br_cf_ready, 1)
                    if h > 2:
                        act.wait_ge(products_ready, JOB[f"o{h - 3}"] + 1)
                    b = product(act, f"aT{h - 1}")
                    out_of("", act.activation(attT[:, (h - 1) % 2, :, :],
                                              b[:, :].rearrange("p (k s) -> p k s", k=TT), ACT.Copy))
            gate_out(6)
            root(5, o_rt, o_ms)
            gate_out(7)
            for i in range(2):
                b = product(act, f"oT{i}")
                out_of("", act.activation(br_at[:, 2 * i:2 * i + 2, :].rearrange("p m s -> p (m s)"), b[:, :],
                                          ACT.Copy, scale=sub_gain))

            def gates_sigmoid(n):
                wait_emptied(act, f"gate{4 * n + 3}")
                act.activation(gates[n], gates[n], ACT.Sigmoid).then_inc(gates_ready, 1)

            gates_sigmoid(0)
            gates_sigmoid(1)
            for i in range(8, 12):
                gate_out(i)
            gates_sigmoid(2)
            for i in range(8):
                copy_out(f"adab{i}", mod_half(i))
            for t in range(TT):
                root(6 + t, g2_rt[:, t:t + 1], g2_ms[:, t:t + 1])
            for t in range(TT):
                for c in range(2):
                    b = product(act, f"h2T{t}{c}")
                    out_of("", act.activation(h2T[:, 4 * c:4 * c + 4, t * P:(t + 1) * P],
                                              b[:, :].rearrange("p (k s) -> p k s", k=4), ACT.Copy))
            act.wait_ge(top_ready, TT)
            for t in range(TT):
                act.activation(top_w[:, t, :], top[:, t, 0:TOPK], ACT.Exp, bias=top_s[:, t, 0:1],
                               accum_out=top_s[:, t, 1:2]).then_inc(top_exp, 1)
            act.sem_inc(misc_out["act"], MISC_COUNT["act"])
            act.sem_inc(moe_primed, 1)

            def misc_copy(i, name, dst):
                b = misc_product(act, i, name)
                act.activation(dst, b[:, 0:dst.shape[1]], ACT.Copy).then_inc(misc_out["act"], 1)

            def body(i):
                for g in range(4):
                    misc_copy(i, f"gather{g}", xT[:, 2 * g:2 * g + 2, :].rearrange("p k s -> p (k s)"))
                for b, s in enumerate("ab"):
                    for half in range(2):
                        r = slice(half * 512, (half + 1) * 512)
                        act.wait_ge(gate_min, i * 4 + 2 * b + half + 1)
                        act.activation(sig_s[:, r], gate_s[:, r], ACT.Sigmoid, scale=ALPHA)\
                            .then_inc(sigmoid_done, 1)
                    misc_copy(i, f"turn_{s}", turned)
                    for half in range(2):
                        misc_copy(i, f"hidT_{s}{half}",
                                  hidT[:, 4 * half:4 * half + 4, :].rearrange("p k s -> p (k s)"))

            def one_pass(p):
                with act.Fori(0, BODIES) as j:
                    body(p * BODIES + j)

            one_pass(0)
            act.wait_ge(flag_ready, 1)
            over = act.value_load(flag[0:1, 0:1], min_val=0, max_val=SEQ)
            with act.If(over > SLOTS):
                with act.Fori(1, PASSES) as p:
                    one_pass(p)

        @block.vector
        def _(dve):
            step = Steps(dve, dve_step)
            emptied_here = Steps(dve, emptied["dve"])

            def inverse_root(n, ms, rt, r, t):
                dve.wait_ge(sqrt_done, n)
                step(dve.reciprocal(r, rt))
                step.wait()
                step(dve.tensor_tensor(t, r, r, ALU.mult))
                step.wait()
                step(dve.tensor_tensor(t, t, ms, ALU.mult))
                step.wait()
                step(dve.tensor_scalar(t, t, -0.5, 1.5, ALU.mult, ALU.add))
                step.wait()
                step(dve.tensor_tensor(r, r, t, ALU.mult))
                step.wait()

            dve.wait_ge(vec_landed, 16)
            dve.wait_ge(sig_ready, 1)
            step(dve.tensor_tensor(cond, vec[:, 0, V_C:V_C + KT], cond_sig, ALU.mult))
            step.wait()
            dve.tensor_copy(cond_rep[:, :, :], cond.rearrange("p (k o) -> p k o", o=1).to_broadcast([P, KT, 32]))\
                .then_inc(cond_ready, 1)
            step(dve.tensor_scalar(sub_gain, vec[:, 0, V_SUB:V_SUB + 1], 1.0 - LAM_INIT, None, ALU.mult))
            dve.wait_ge(mlp_landed, 16)
            y, turns = mlp_y[:, 0, :], mlp_y[:, 1, :]
            for n in range(3):
                b = product(dve, f"mlp{n}")
                emptied_here(dve.tensor_scalar(y, b[:, 0:SEQ], hf_col[:, n:n + 1], hf_col[:, 3:4],
                                               ALU.add, ALU.mult))
                emptied_here.wait()
                step(dve.tensor_scalar(turns, y, 1.0 / (2 * math.pi), ROUND, ALU.mult, ALU.add))
                step.wait()
                step(dve.tensor_scalar(turns, turns, -ROUND, None, ALU.add))
                for part_of_pi in (PI_A, PI_B, PI_C):
                    step.wait()
                    step(dve.scalar_tensor_tensor(y, turns, -part_of_pi, y, ALU.mult, ALU.add))
                step.wait()
                dve.tensor_scalar(y, y, 3.1415925, -3.1415925, ALU.min, ALU.max).then_inc(sin_asked, 1)
                if n == 0:
                    step(dve.tensor_tensor(w4s[:, 0, :], w4[:, 0, :], w4[:, 1, :], ALU.add))
                    dve.tensor_tensor(w4s[:, 1, :], w4[:, 0, :], w4[:, 1, :], ALU.subtract).then_inc(w4_summed, 1)
            dve.wait_ge(x_squared, TT)
            step(dve.tensor_scalar(x_ms, x_ss, 1.0 / D, EPS, ALU.mult, ALU.add))
            step.wait()
            dve.sem_inc(sqrt_asked, 1)
            inverse_root(1, x_ms, x_rt, x_r, x_t)
            dve.sem_inc(r_ready, 1)
            dve.wait_ge(window_landed, 16)
            for s in range(2):
                for t in range(TT):
                    for o in range(2):
                        b = product(dve, f"filter{o}{s}{t}")
                        emptied_here(dve.tensor_tensor(filt[:, t, o, s, :], b[:, :], window[:, t, :], ALU.mult))
            half_taps = TAPS // 2
            dve.wait_ge(xn_ready, TT)
            step(dve.memset(cf_in[:, :, 0:half_taps], 0.0))
            step(dve.memset(cf_in[:, :, SEQ + half_taps:], 0.0))
            b = product(dve, "modcol")
            step(dve.tensor_tensor(shift1, b[:, 0:KT], vec[:, 0, V_ADA:V_ADA + KT], ALU.add))
            emptied_here(dve.tensor_tensor(n1_gain, b[:, KT:2 * KT], vec[:, 0, V_ADA + KT:V_ADA + 2 * KT], ALU.add))
            emptied_here.wait()
            dve.scalar_tensor_tensor(n1_gain, n1_gain, 1.0, vec[:, 0, V_N1:V_N1 + KT], ALU.add, ALU.mult)\
                .then_inc(modcol_ready, 1)
            dve.memset(hy_in[:, :, 0:1], 0.0)
            dve.memset(hy_in[:, :, SEQ + 1:SEQ + 2], 0.0).then_inc(pads_zeroed, 1)
            dve.wait_ge(modcol_ready, 1)
            step.wait()
            for i in (1, 3):
                b = product(dve, f"xT{i}")
                for kk in range(2):
                    k = 2 * i + kk
                    ins = dve.tensor_scalar(hT[:, k, :], b[:, kk * SEQ:(kk + 1) * SEQ], n1_gain[:, k:k + 1],
                                            shift1[:, k:k + 1], ALU.mult, ALU.add)
                emptied_here(ins)
            wait_emptied(dve, "cg1")
            for i in range(2):
                b = product(dve, f"ca{i}")
                for m in range(2):
                    c = 2 * i + m
                    bias = V_BIN + HY_T + c
                    ins = dve.scalar_tensor_tensor(cf_in[:, c, half_taps:half_taps + SEQ],
                                                   b[:, m * SEQ:(m + 1) * SEQ], vec[:, 0, bias:bias + 1],
                                                   cf_cv[:, c, :], ALU.add, ALU.mult)
                emptied_here(ins)
            emptied_here.wait()

            def conv(first, last):
                for tap in range(first, last):
                    for c in range(WT):
                        w = vec[:, 2, tap * WT + c:tap * WT + c + 1]
                        src = cf_in[:, c, tap:tap + SEQ]
                        if tap == 0:
                            step(dve.tensor_scalar(cf_cv[:, c, :], src, w, vec[:, 0, V_DWB + c:V_DWB + c + 1],
                                                   ALU.mult, ALU.add))
                        else:
                            step.wait(conv_last[c])
                            ins = dve.scalar_tensor_tensor(cf_cv[:, c, :], src, w, cf_cv[:, c, :],
                                                           ALU.mult, ALU.add)
                            step(ins)
                        conv_last[c] = step.n
            conv_last = [0] * WT

            def short_conv(i):
                wait_emptied(dve, f"hy{i}")
                dve.wait_ge(pads_zeroed, 1)
                for tap in range(3):
                    for m in range(2):
                        c = 2 * i + m
                        w = vec[:, 1, tap * HY_T + c:tap * HY_T + c + 1]
                        src = hy_in[:, c, tap:tap + SEQ]
                        if tap == 0:
                            step(dve.tensor_scalar(hy_cv[:, c, :], src, w, vec[:, 0, V_HYB + c:V_HYB + c + 1],
                                                   ALU.mult, ALU.add))
                        else:
                            ins = dve.scalar_tensor_tensor(hy_cv[:, c, :], src, w, hy_cv[:, c, :],
                                                           ALU.mult, ALU.add)
                            if tap == 1:
                                step(ins)
                            else:
                                ins.then_inc(hy_conv_done, 1)
                    if tap < 2:
                        step.wait()

            def mix(o):
                for half in range(2):
                    k_cos, k_sin, k_cos2 = ((0, 3, 2), (1, 4, 1))[half]
                    u_cos = product(dve, f"u{o}{half}")
                    if half == 0:
                        wait_emptied(dve, f"spectrum{o}4")
                    step(dve.tensor_tensor(ysp[:, half, :], u_cos[:, :], spectra[:, o, k_cos, :], ALU.mult))
                    u_sin = product(dve, f"u{o}{2 + half}")
                    step(dve.tensor_tensor(hy_tmp[:, 0, :], u_sin[:, :], spectra[:, o, k_sin, :], ALU.mult))
                    emptied_here(dve.tensor_tensor(ysp[:, 2 + half, :], u_cos[:, :], spectra[:, o, k_sin, :],
                                                   ALU.mult))
                    emptied_here(dve.tensor_tensor(hy_tmp[:, 1, :], u_sin[:, :], spectra[:, o, k_cos2, :],
                                                   ALU.mult))
                    step.wait()
                    step(dve.tensor_tensor(ysp[:, half, :], ysp[:, half, :], hy_tmp[:, 0, :], ALU.subtract))
                    emptied_here.wait()
                    dve.tensor_tensor(ysp[:, 2 + half, :], ysp[:, 2 + half, :], hy_tmp[:, 1, :], ALU.add)\
                        .then_inc(spectra_mixed, 1)
                    dve.wait_ge(spectra_mixed, 2 * o + half + 1)
                    step.wait()

            def hyena_step(o):
                for t in range(TT):
                    step(dve.tensor_tensor(hy_tmp[:, t, :], hy[:, 0, t, :], hy_bias[:, o, :], ALU.mult))
                for t in range(TT):
                    b = product(dve, f"inv{o}{t}")
                    step.wait()
                    emptied_here(dve.tensor_tensor(hy_tmp[:, t, :], b[:, :], hy_tmp[:, t, :], ALU.add))
                    emptied_here.wait()
                    dve.tensor_tensor(hy[:, 0, t, :], hy_tmp[:, t, :], hy[:, 1 + o, t, :], ALU.mult)\
                        .then_inc(z_ready, 1)
                dve.wait_ge(z_ready, 2 * o + 2)

            def add_bias(j):
                for t in range(TT):
                    b = product(dve, f"{'qkv'[j]}{t}")
                    emptied_here(dve.tensor_tensor(qkv[:, j, t, :], b[:, :], qkv[:, j, t, :], ALU.add))
                emptied_here.wait()

            def heads(v):
                return v.rearrange("p (g d) -> p g d", d=HD)

            def norm_and_rotate(j):
                ms, rt, r, tmp = (qk_ss[:, n, :, :] for n in range(4))
                for t in range(TT):
                    v = qkv[:, j, t, :]
                    step(dve.tensor_tensor(hy_tmp[:, t, :], v, v, ALU.mult))
                step.wait()
                for t in range(TT):
                    step(dve.tensor_reduce(ms[:, t, :], heads(hy_tmp[:, t, :]), AX_X, ALU.add))
                step.wait()
                step(dve.tensor_scalar(ms, ms, 1.0 / HD, EPS, ALU.mult, ALU.add))
                step.wait()
                dve.sem_inc(sqrt_asked, 1)
                inverse_root(3 + j, ms, rt, r, tmp)
                both = [P, GROUPS, HD]
                half = HD // 2
                for t in range(TT):
                    v = heads(qkv[:, j, t, :])
                    step(dve.tensor_tensor(v, v, r[:, t, :].rearrange("p (g o) -> p g o", o=1).to_broadcast(both),
                                           ALU.mult))
                step.wait()
                for t in range(TT):
                    v = heads(qkv[:, j, t, :])
                    step(dve.tensor_tensor(v, v, gain[:, j:j + 1, :].to_broadcast(both), ALU.mult))
                step.wait()
                for t in range(TT):
                    v = heads(qkv[:, j, t, :])
                    c, s = heads(hy_tmp[:, 0, :]), heads(hy_tmp[:, 1, :])
                    step(dve.tensor_tensor(c, v, rope[:, 0, t:t + 1, :].to_broadcast(both), ALU.mult))
                    part_shape = [P, GROUPS, half]
                    step(dve.tensor_tensor(s[:, :, 0:half], v[:, :, half:],
                                           rope[:, 1, t:t + 1, 0:half].to_broadcast(part_shape), ALU.mult))
                    step(dve.tensor_tensor(s[:, :, half:], v[:, :, 0:half],
                                           rope[:, 1, t:t + 1, half:].to_broadcast(part_shape), ALU.mult))
                    step.wait()
                    dve.tensor_tensor(v, c, s, ALU.add).then_inc(roped, 1)
                    dve.wait_ge(roped, TT * j + t + 1)

            all_tiles = [P, WT, SEQ]

            def conformer_mean():
                b = product(dve, "mean")
                emptied_here(dve.scalar_tensor_tensor(
                    cf_cv, b[:, 0:SEQ].rearrange("p (o s) -> p o s", o=1).to_broadcast(all_tiles), -1.0 / W,
                    cf_cv, ALU.mult, ALU.add))
                emptied_here.wait()
                dve.tensor_tensor(cf_sq, cf_cv, cf_cv, ALU.mult).then_inc(centred, 1)

            def conformer_scale():
                b = product(dve, "var")
                emptied_here(dve.tensor_scalar(ln_ms, b[:, 0:SEQ], 1.0 / W, EPS, ALU.mult, ALU.add))
                emptied_here.wait()
                dve.sem_inc(sqrt_asked, 1)
                inverse_root(2, ln_ms, ln_rt, ln_r, ln_t)
                step(dve.tensor_tensor(cf_cv, cf_cv,
                                       ln_r.rearrange("p (o s) -> p o s", o=1).to_broadcast(all_tiles), ALU.mult))
                step.wait()

            for i in range(6):
                conv(3 * i, 3 * i + 3)
                short_conv(i)
            conv(18, TAPS)
            step.wait()
            dve.sem_inc(conv_done, 1)
            mix(0)
            dve.wait_ge(attn_landed, 16 * 4)
            add_bias(0)
            conformer_mean()
            dve.wait_ge(hyena_landed, 32)
            hyena_step(0)
            conformer_scale()
            norm_and_rotate(0)
            add_bias(1)
            mix(1)
            norm_and_rotate(1)
            add_bias(2)
            hyena_step(1)
            for n in range(2):
                dve.tensor_tensor_reduce(lam_v[:, 2 * n, :], lam_v[:, 2 * n, :], lam_v[:, 2 * n + 1, :], 1.0, 0.0,
                                         ALU.mult, ALU.add, lam_s[:, n:n + 1]).then_inc(lam_ready, 1)
            for m in range(WT):
                dve.tensor_scalar(br_cf[:, m, :], cf_cv[:, m, :], vec[:, 0, V_LNG + m:V_LNG + m + 1],
                                  vec[:, 0, V_LNB + m:V_LNB + m + 1], ALU.mult, ALU.add).then_inc(cf_scaled, 1)
            dve.wait_ge(cf_act, WT)
            dve.tensor_tensor(br_cf[:, :, :], br_cf[:, :, :], cf_cv, ALU.mult).then_inc(br_cf_ready, 1)
            dve.wait_ge(lam_exp, 1)
            step(dve.tensor_tensor(lam_s[:, 4:5], lam_s[:, 3:4], lam_s[:, 2:3], ALU.subtract))
            step.wait()
            step(dve.tensor_scalar(lam_s[:, 5:6], lam_s[:, 4:5], -LAM_INIT, None, ALU.add))
            step.wait()

            def score_max(h):
                for c in range(2):
                    b = product(dve, f"score{h}{c}")
                    step(dve.tensor_reduce(s_max[:, h, c, :], b[:, :].rearrange("p (t k) -> p t k", t=TT),
                                           AX_X, ALU.max))
                    step.wait()
                    dve.tensor_scalar(s_max[:, h, c, :], s_max[:, h, c, :], -SCALE, None, ALU.mult)\
                        .then_inc(max_ready, 1)

            def combine(h):
                wait_emptied(dve, f"score{h}1")
                step(dve.reciprocal(s_inv[:, h, :, :], s_sum[:, h, :, :]))
                step.wait()
                step(dve.tensor_scalar(s_inv[:, h, 1, :], s_inv[:, h, 1, :], lam_s[:, 5:6], None, ALU.mult))
                step.wait()
                for t in range(TT):
                    v = prob[:, h % 2, 1, t, :]
                    step(dve.tensor_scalar(v, v, s_inv[:, h, 1, t:t + 1], None, ALU.mult))
                step.wait()
                for t in range(TT):
                    v = prob[:, h % 2, 0, t, :]
                    ins = dve.scalar_tensor_tensor(v, v, s_inv[:, h, 0, t:t + 1], prob[:, h % 2, 1, t, :],
                                                   ALU.mult, ALU.add)
                ins.then_inc(att_ready, 1)

            score_max(0)
            score_max(1)
            def o_out(h):
                b = product(dve, f"o{h}")
                emptied_here(dve.tensor_copy(att[:, :, h * P:(h + 1) * P],
                                             b[:, 0:2 * P].rearrange("p (t e) -> p t e", t=TT)))

            for h in range(HEADS):
                combine(h)
                if h + 2 < HEADS:
                    score_max(h + 2)
                if h:
                    o_out(h - 1)
            o_out(HEADS - 1)
            emptied_here.wait()
            tiny = 2.0 ** -64
            o_a, o_b = o_ms[:, 0:8], o_ms[:, 8:16]

            def by_head(v):
                return v.rearrange("p (h e) -> p h e", h=HEADS)

            for t in range(TT):
                r = slice(4 * t, 4 * t + 4)
                step(dve.tensor_scalar(hy_tmp[:, 0, :], att[:, t, :], 1e17, -1e17, ALU.min, ALU.max))
                step(dve.tensor_scalar(hy_tmp[:, 1, :], att[:, t, :], tiny, None, ALU.mult))
                step.wait()
                for n in range(2):
                    step(dve.tensor_tensor(hy_tmp[:, n, :], hy_tmp[:, n, :], hy_tmp[:, n, :], ALU.mult))
                step.wait()
                step(dve.tensor_reduce(o_a[:, r], by_head(hy_tmp[:, 0, :]), AX_X, ALU.add))
                step(dve.tensor_reduce(o_b[:, r], by_head(hy_tmp[:, 1, :]), AX_X, ALU.add))
                step.wait()
            small_sum, large_sum = o_sel[:, 0:8], o_sel[:, 8:16]
            step(dve.tensor_scalar(o_b, o_b, 1e30, None, ALU.min))
            step.wait()
            step(dve.tensor_scalar(small_sum, o_b, 1e-5, None, ALU.is_lt))
            step(dve.tensor_scalar(o_sel[:, 16:24], o_b, 1.0, None, ALU.is_lt))
            step.wait()
            step(dve.tensor_tensor(large_sum, o_sel[:, 16:24], small_sum, ALU.subtract))
            step(dve.tensor_scalar(o_a, o_a, 1.0 / P, EPS, ALU.mult, ALU.add))
            step(dve.tensor_scalar(o_b, o_b, 1.0 / P, 1e-12, ALU.mult, ALU.add))
            step.wait()
            step(dve.tensor_scalar(large_sum, large_sum, tiny, None, ALU.mult))
            dve.sem_inc(sqrt_asked, 1)
            inverse_root(5, o_ms, o_rt, o_r, o_t)
            step(dve.tensor_tensor(o_r, o_r, o_sel[:, 0:16], ALU.mult))
            step.wait()
            step(dve.tensor_tensor(o_t[:, 0:8], o_r[:, 0:8], o_r[:, 8:16], ALU.add))
            step.wait()
            for t in range(TT):
                r = o_t[:, 4 * t:4 * t + 4].rearrange("p (h o) -> p h o", o=1).to_broadcast([P, HEADS, P])
                v = by_head(att[:, t, :])
                ins = dve.tensor_tensor(v, v, r, ALU.mult)
                step(ins)
            step.wait()
            dve.sem_inc(o_ready, 1)

            dve.wait_ge(mod_bias_landed, 16)
            for i in range(8):
                wait_chunk(dve, "ada", 4 + i)
                w = slot_view("ada", 4 + i)
                acc = mod_half(i)
                for k in range(KT):
                    ins = dve.scalar_tensor_tensor(acc, w[:, k, :], cond[:, k:k + 1], acc, ALU.mult, ALU.add)
                    if k < KT - 1:
                        step(ins)
                        step.wait()
                ins.then_inc(ada_summed, 1)

            for g, n in enumerate((0, 1, 2)):
                dve.wait_ge(gates_ready, g + 1)
                for m in range(4):
                    b = product(dve, f"merge{n}{m}")
                    gate_v = gates[n][:, 2 * m:2 * m + 2, :].rearrange("p k s -> p (k s)")
                    sum_v = merged[:, 2 * m:2 * m + 2, :].rearrange("p k s -> p (k s)")
                    if g == 0:
                        emptied_here(dve.tensor_tensor(sum_v, b[:, :], gate_v, ALU.mult))
                        continue
                    emptied_here(dve.tensor_tensor(hy_tmp[:, m % 2, :], b[:, :], gate_v, ALU.mult))
                    emptied_here.wait()
                    ins = dve.tensor_tensor(sum_v, sum_v, hy_tmp[:, m % 2, :], ALU.add)
                    if g == 1:
                        step(ins)
                    else:
                        ins.then_inc(merged_ready, 1)
                if g == 1:
                    step.wait()
            wait_emptied(dve, "adab7")
            dve.wait_ge(gain2_landed, 16)
            step(dve.scalar_tensor_tensor(sc2, sc2, 1.0, scratch, ALU.add, ALU.mult))
            dve.wait_ge(x_again_landed, 16)
            for t in range(TT):
                one = slice(t, t + 1)
                for c in range(2):
                    b = product(dve, f"out{t}{c}")
                    r = slice(c * W, (c + 1) * W)
                    emptied_here(dve.tensor_tensor(hy_tmp[:, c, :], b[:, :], g1[:, r], ALU.mult))
                    emptied_here.wait()
                    step(dve.tensor_tensor(x[:, t, r], x[:, t, r], hy_tmp[:, c, :], ALU.add))
                    step.wait()
                    step(dve.tensor_tensor_reduce(squares, x[:, t, r], x[:, t, r], 1.0, 0.0,
                                                  ALU.mult, ALU.add, x1_ss[:, t, c:c + 1]))
                    step.wait()
                step(dve.tensor_tensor(g2_ss[:, one], x1_ss[:, t, 0:1], x1_ss[:, t, 1:2], ALU.add))
                step.wait()
                step(dve.tensor_scalar(g2_ms[:, one], g2_ss[:, one], 1.0 / D, EPS, ALU.mult, ALU.add))
                step.wait()
                dve.sem_inc(sqrt_asked, 1)
                inverse_root(6 + t, g2_ms[:, one], g2_rt[:, one], g2_r[:, one], g2_t[:, one])
                for c in range(2):
                    r = slice(c * W, (c + 1) * W)
                    step(dve.scalar_tensor_tensor(h2[:, t, r], x[:, t, r], g2_r[:, one], sc2[:, r],
                                                  ALU.mult, ALU.mult))
                    step.wait()
                    dve.tensor_tensor(h2[:, t, r], h2[:, t, r], sh2[:, r], ALU.add).then_inc(h2_ready, 1)

            b = product(dve, "logits")
            dve.wait_ge(router_landed, 32)
            emptied_here(dve.tensor_tensor(
                logit[:, :, :], b[:, 0:TT * EXPERTS].rearrange("p (t e) -> p t e", t=TT),
                b_router[:, :].rearrange("p (o e) -> p o e", o=1).to_broadcast([P, TT, EXPERTS]), ALU.add))
            emptied_here.wait()
            for t in range(TT):
                step(dve.max(top[:, t, :], logit[:, t, :]))
            step.wait()
            for t in range(TT):
                step(dve.max_index(top_i[:, t, :], top[:, t, :], logit[:, t, :]))
                dve.tensor_scalar(top_s[:, t, 0:1], top[:, t, 0:1], -1.0, None, ALU.mult).then_inc(top_ready, 1)
            step.wait()
            step(dve.tensor_copy(top_f[:, :, :], top_i[:, :, :]))
            step.wait()
            one_hot = [P, TT, TOPK, EXPERTS]
            step(dve.tensor_tensor(chosen, expert_no[:, :].rearrange("p (a b e) -> p a b e", a=1, b=1)
                                   .to_broadcast(one_hot),
                                   top_f[:, :, 0:TOPK].rearrange("p t (k o) -> p t k o", o=1)
                                   .to_broadcast(one_hot), ALU.is_equal))
            step.wait()
            dve.tensor_reduce(mask[:, :, :], chosen.rearrange("p t k e -> p t e k"), AX_X, ALU.add)\
                .then_inc(mask_ready, 1)
            dve.wait_ge(top_exp, TT)
            step(dve.reciprocal(top_s[:, :, 2:3], top_s[:, :, 1:2]))
            step.wait()
            step(dve.tensor_tensor(top_w[:, :, :], top_w[:, :, :],
                                   top_s[:, :, 2:3].to_broadcast([P, TT, TOPK]), ALU.mult))
            step.wait()
            step(dve.tensor_tensor(chosen_w, chosen, top_w[:, :, :].rearrange("p t (k o) -> p t k o", o=1)
                                   .to_broadcast(one_hot), ALU.mult))
            step.wait()
            step(dve.tensor_reduce(comb[:, :, 0:EXPERTS], chosen_w.rearrange("p t k e -> p t e k"), AX_X, ALU.add))
            b = product(dve, "rank")
            dve.wait_ge(mask_ready, 1)
            step(dve.scalar_tensor_tensor(pos[:, :, 0:EXPERTS], mask[:, :, :], -FAR,
                                          b[:, 0:TT * EXPERTS].rearrange("p (t e) -> p t e", t=TT),
                                          ALU.mult, ALU.add))
            step.wait()
            step(dve.tensor_scalar(pos[:, :, 0:EXPERTS], pos[:, :, 0:EXPERTS], FAR, None, ALU.add))
            step.wait()

            def members(j, call):
                shape = [P, 4, SLOTS]
                for t in range(TT):
                    p_of = pos[:, t, bass.ds(j * 4, 4)].rearrange("p (e o) -> p e o", o=1)
                    i_of = iota[:, :].rearrange("p (o s) -> p o s", o=1)
                    dve.tensor_tensor(member[:, t, :, :], i_of.to_broadcast(shape),
                                      p_of.to_broadcast(shape), ALU.is_equal).then_inc(member_ready, 1)
                dve.wait_ge(member_ready, call * 2)
                for t in range(TT):
                    c_of = comb[:, t, bass.ds(j * 4, 4)].rearrange("p (e o) -> p e o", o=1)
                    dve.tensor_tensor(weighted[:, t, :, :], member[:, t, :, :],
                                      c_of.to_broadcast(shape), ALU.mult).then_inc(weighted_ready, 1)

            def gate_up_half(i, b, half):
                r = slice(half * 512, (half + 1) * 512)
                n = 2 * b + half + 1
                dve.wait_ge(gate_up_done, i * 4 + n)
                dve.tensor_scalar(gate_s[:, r], bank[half][:, :], LIMIT, None, ALU.min).then_inc(gate_min, 1)
                dve.tensor_scalar(up_s[:, r], bank[2 + half][:, :], LIMIT, -LIMIT, ALU.min, ALU.max)\
                    .then_inc(gate_up_read, 1)

            def hidden_half(i, b, half, done):
                r = slice(half * 512, (half + 1) * 512)
                n = 2 * b + half + 1
                dve.wait_ge(sigmoid_done, i * 4 + n)
                done(dve.tensor_tensor(gate_s[:, r], gate_s[:, r], sig_s[:, r], ALU.mult))
                done.wait()
                dve.wait_ge(gate_up_read, i * 4 + 4 + n)
                dve.scalar_tensor_tensor(hid[:, r], up_s[:, r], 1.0, gate_s[:, r], ALU.add, ALU.mult)\
                    .then_inc(hid_ready, 1)

            def add(i, s, n):
                name = f"add_{s}{n}"
                b = misc_product(dve, i, name)
                prev = MISC_ORD[f"add_{'b' if s == 'a' else 'a'}{n}"] + (0 if s == "a" else MISC_COUNT["dve"])
                dve.wait_ge(misc_out["dve"], i * MISC_COUNT["dve"] + prev)
                quarter = x[:, n // 2, (n % 2) * W:(n % 2 + 1) * W]
                dve.tensor_tensor(quarter, quarter, b[:, :], ALU.add).then_inc(misc_out["dve"], 1)

            def y_out(i, b):
                for n in range(2):
                    dve.wait_ge(y_done, i * 4 + 2 * b + n + 1)
                    r = slice(n * W, (n + 1) * W)
                    dve.tensor_tensor(y_s[:, r], bank[4 + n][:, :], g2[:, r], ALU.mult).then_inc(y_read, 1)

            def body(i, j, p):
                done = LoopSteps(dve, moe_step, i * BODY_STEPS)
                for b in range(2):
                    for half in range(2):
                        gate_up_half(i, b, half)
                    hidden_half(i, b, 0, done)
                    if b:
                        add(i, "a", 0)
                    hidden_half(i, b, 1, done)
                    if b:
                        for n in range(1, 4):
                            add(i, "a", n)
                        dve.wait_ge(misc_done, i * len(MISC) + MISC_NO["turn_b"] + 1)
                        members(j + 1, i + p + 2)
                    y_out(i, b)
                for n in range(4):
                    add(i, "b", n)
                assert done.n == BODY_STEPS

            def one_pass(p, first=False):
                if not first:
                    dve.tensor_scalar(pos[:, :, 0:EXPERTS], pos[:, :, 0:EXPERTS], -float(SLOTS), None, ALU.add)\
                        .then_inc(pass_step, 1)
                    dve.wait_ge(pass_step, p)
                    dve.wait_ge(misc_done, p * (BODIES * len(MISC)))
                members(0, p * (BODIES + 1) + 1)
                if first:
                    b = bank[JOB["rank"] % 8]
                    emptied_here(dve.tensor_reduce(most, b[:, 64:64 + EXPERTS], AX_X, ALU.max))
                    emptied_here.wait()
                    dve.tensor_copy(flag[:, :], most).then_inc(flag_ready, 1)
                    dve.sem_inc(misc_out["dve"], MISC_COUNT["dve"])
                    dve.sem_inc(gate_up_read, 4)
                    dve.sem_inc(y_read, 4)
                    dve.sem_inc(moe_primed, 1)
                with dve.Fori(0, BODIES) as j:
                    body(p * BODIES + j, j, p)

            one_pass(0, first=True)
            over = dve.value_load(flag[0:1, 0:1], min_val=0, max_val=SEQ)
            with dve.If(over > SLOTS):
                with dve.Fori(1, PASSES) as p:
                    one_pass(p)
            dve.wait_ge(misc_out["dve"], MISC_COUNT["dve"] * (BODIES + 1))
            dve.drain()
            dve.sem_inc(out_ready, 1)

    return nc


def shape_constants():
    f32 = np.float32
    n = 2 * SEQ
    t, f = np.arange(SEQ)[:, None], np.arange(SEQ)[None, :]
    cos, sin = np.cos(2 * np.pi * t * f / n), np.sin(2 * np.pi * t * f / n)
    nyquist = np.cos(np.pi * np.arange(SEQ))
    sin_ny = sin.copy()
    sin_ny[:, 0] = nyquist
    cos_ny = cos[:, 0:P].copy()
    cos_ny[:, 0] = nyquist
    dft_f = np.concatenate([cos, sin_ny, cos_ny, sin[:, 0:P]], axis=1)
    weight = np.full((SEQ, 1), 2.0 / n)
    weight[0] = 1.0 / n
    dft_i = np.concatenate([cos.T * weight, sin_ny.T * weight], axis=0)

    pos = np.arange(SEQ, dtype=f32)
    time = np.linspace(0.0, 1.0, SEQ, dtype=f32)[:, None]
    deltas = np.abs(np.linspace(math.log(1e-2) / 0.3, math.log(1e-2) / 1.5, W, dtype=f32))
    window = np.exp(-time * deltas[None, :]) + f32(0.05)

    inv = f32(1.0) / (f32(10000.0) ** (np.arange(0, HD, 2, dtype=f32) / f32(HD)))
    ra = pos[:, None] * inv[None, :]
    rc, rs = np.cos(ra), np.sin(ra)
    rope = np.stack([np.concatenate([rc, rc], axis=1), np.concatenate([-rs, rs], axis=1)])
    made = {"dft_f": dft_f, "dft_i": dft_i, "window": window, "rope": rope}
    return {k: np.ascontiguousarray(v, dtype=f32) for k, v in made.items()}


def position_features():
    f32 = np.float32
    time = np.linspace(0.0, 1.0, SEQ, dtype=f32)[:, None]
    bands = np.linspace(1e-4, BANDS - 1, BANDS, dtype=f32)
    ang = f32(2.0 * math.pi / SEQ) * np.arange(SEQ, dtype=f32)[:, None] * bands[None, :]
    return np.concatenate([time, np.cos(ang), -np.sin(ang)], axis=-1).T


PACKED = ("norm1_g", "q_norm_g", "k_norm_g", "lam_q1", "lam_k1", "lam_q2", "lam_k2", "subln_g", "hy_conv_w",
          "hy_conv_b", "hf_w1", "hf_b1", "hf_w2", "hf_b2", "hf_w3", "hf_b3", "hf_freq", "hf_w4", "cf_dw_w",
          "cf_dw_b", "cf_ln_g", "cf_ln_b", "b_gu", "b_down", "c")


def packed(inputs):
    v = {k: np.asarray(inputs[k]) for k in PACKED}
    b_ada, b_in = np.asarray(inputs["b_ada"]), np.asarray(inputs["b_in"])
    columns = np.zeros((3, P, P), np.float32)
    parts = [(0, V_ADA, b_ada[0, 0:2 * D]), (0, V_N1, v["norm1_g"]), (0, V_BIN, b_in[0, 3 * W:]),
             (0, V_SUB, v["subln_g"]), (0, V_DWB, v["cf_dw_b"]), (0, V_LNG, v["cf_ln_g"]),
             (0, V_LNB, v["cf_ln_b"]), (0, V_C, v["c"]), (0, V_HYB, v["hy_conv_b"]),
             (1, 0, v["hy_conv_w"]), (2, 0, v["cf_dw_w"])]
    for i, row, x in parts:
        x = x.reshape(-1, P)
        columns[i, row:row + len(x)] = x
    net = np.zeros((P, NET_COLS), np.float32)
    for o in range(2):
        rows = slice(o * HF_HID, (o + 1) * HF_HID)
        net[rows, 0:2 * W] = v["hf_w4"][0, :, o * 2 * W:(o + 1) * 2 * W]
        for n, name in enumerate(("hf_b1", "hf_b2", "hf_b3", "hf_freq")):
            net[rows, NET_B + n] = v[name][0]
    net[0:HF_EMB, NET_Z:NET_W] = position_features()
    for n, name in enumerate(("hf_w1", "hf_w2", "hf_w3")):
        w = v[name][0]
        net[0:len(w), NET_W + n * HF_HID:NET_W + (n + 1) * HF_HID] = w
    head_rows = np.concatenate([v[n] for n in ("q_norm_g", "k_norm_g", "lam_q1", "lam_k1", "lam_q2", "lam_k2")],
                               axis=1)
    return {"columns": columns.reshape(3 * P, P).T, "filter_net": net, "head_rows": head_rows,
            "b_experts": np.concatenate([v["b_gu"][0], v["b_down"][0]], axis=1)}


def kernel(**inputs):
    import concourse.bacc as _bacc
    from concourse.bass_utils import run_bass_kernel_spmd as _run

    nc = _bacc.Bacc("TRN2", target_bir_lowering=False, num_devices=1)
    arrays, args = {}, {}
    for name, v in {**inputs, **packed(inputs), **shape_constants()}.items():
        if name in PACKED:
            continue
        v = np.ascontiguousarray(v)
        arrays[name] = v
        args[name] = nc.dram_tensor(name, v.shape, mybir.dt.from_np(v.dtype), kind="ExternalInput").ap()
    out = nc.dram_tensor("layer_out", (1, SEQ, D), F32, kind="ExternalOutput").ap()
    build_layer(nc, args, out)
    r = _run(nc, [arrays], core_ids=[0])
    return r.results[0]["layer_out"]
```

```python
import math
from contextlib import ExitStack

import numpy as np
import concourse.bass as bass
from concourse import mybir

P = 128
D = 1024
SEQ = 256
TT = SEQ // P
KT = D // P
W = 512
WT = W // P
HEADS, HD = 4, 64
GROUPS = 2 * HEADS
HY_T = 3 * WT
BANDS, HF_EMB, HF_HID = 16, 33, 64
TAPS = 31
EXPERTS, TOPK, FF = 32, 4, 1024
EPS = 1e-6
LIMIT, ALPHA = 7.0, 1.702
LAM_INIT = 0.8 - 0.6 * math.exp(-0.3 * 0)
SCALE = HD ** -0.5

WEIGHT_SLOTS = 6
MOE_SLOTS = 9
CHUNK = 4096

SLOTS = 64
PASSES = SEQ // SLOTS
PAIRS = EXPERTS // 2
BODIES = PAIRS // 2
PAIR_CHUNKS = 12
BODY_CHUNKS = 2 * PAIR_CHUNKS
SLOT_OF = list(range(MOE_SLOTS)) + list(range(7)) + list(range(8))
BIAS_AT = 20
FAR = 4096.0

F32 = mybir.dt.float32
I32 = mybir.dt.int32
U32 = mybir.dt.uint32
ALU = mybir.AluOpType
ACT = mybir.ActivationFunctionType
AX_X = mybir.AxisListType.X

V_ADA, V_N1, V_BIN, V_SUB, V_DWB, V_LNG, V_LNB, V_C, V_HYB = 0, 16, 24, 68, 69, 73, 77, 81, 89

NET_Z = 2 * W
NET_W = NET_Z + SEQ
NET_B = NET_W + 3 * HF_HID
NET_COLS = NET_B + 4

PI_A, PI_B, PI_C = 6.28125, 0.0019350051879882812, 3.0199159819e-07
ROUND = 12582912.0

HY_CHUNKS, CF_GATE, CF_VALUE, QKV_CHUNKS, GATE_CHUNKS = (3, 4, 5), 7, 6, (0, 1, 2), range(8, 14)


def front_jobs():
    jobs = [("mlp0", "dve"), ("mlp1", "dve"), ("ada0", "act"), ("mlp2", "dve"), ("ada1", "act")]
    jobs += [(f"filter{o}{s}{t}", "dve") for s in range(2) for t in range(TT) for o in range(2)]
    jobs += [("spectrum00", "act"), ("spectrum01", "act"), ("ada2", "act")]
    jobs += [("spectrum02", "act"), ("ada3", "act"), ("spectrum03", "act"), ("xT0", "act"), ("modcol", "dve")]
    jobs += [("xT1", "dve"), ("xT2", "act"), ("xT3", "dve"), ("spectrum04", "act")]
    jobs += [("cg0", "act"), ("cg1", "act"), ("ca0", "dve"), ("ca1", "dve")]
    jobs += [(f"hy{i}", "act") for i in range(6)]
    jobs += [(f"spectrum1{j}", "act") for j in range(5)]
    jobs += [(f"hyT{g}{t}", "act") for g in range(3) for t in range(TT)]
    jobs += [(f"u0{m}", "dve") for m in (0, 2, 1, 3)] + [("q0", "dve"), ("q1", "dve"), ("mean", "dve")]
    jobs += [("inv00", "dve"), ("inv01", "dve"), ("var", "dve"), ("k0", "dve"), ("k1", "dve")]
    jobs += [(f"u1{m}", "dve") for m in (0, 2, 1, 3)] + [("v0", "dve"), ("v1", "dve")]
    jobs += [("inv10", "dve"), ("inv11", "dve"), ("gate0", "act"), ("zT0", "act"), ("zT1", "act")]
    jobs += [(f"qkT{j}{t}", "act") for j in range(2) for t in range(TT)] + [("gate1", "act")]
    for h in range(HEADS + 2):
        if h < HEADS:
            jobs += [(f"score{h}{c}", "act") for c in range(2)]
        if h:
            jobs += [(f"gate{h + 1}", "act")]
        if h > 1:
            jobs += [(f"o{h - 2}", "dve")]
        if 0 < h <= HEADS:
            jobs += [(f"aT{h - 1}", "act")]
    jobs += [("gate7", "act"), ("gate8", "act"), ("oT0", "act"), ("oT1", "act")]
    jobs += [(f"gate{i}", "act") for i in range(9, 12)]
    jobs += [(f"merge{n}{m}", "dve") for n in range(3) for m in range(4)]
    jobs += [(f"adab{i}", "act") for i in range(8)]
    jobs += [(f"out{t}{c}", "dve") for t in range(TT) for c in range(2)]
    jobs += [(f"h2T{t}{c}", "act") for t in range(TT) for c in range(2)]
    jobs += [("partial", "act"), ("logits", "dve"), ("rank", "dve")]
    return jobs


JOBS = front_jobs()
JOB = {name: n for n, (name, _) in enumerate(JOBS)}
EMPTIED_BY = dict(JOBS)
ROUTER_BANKS = [4, 5, 6, 7, 6, 7, 4]
BANK = [n % 8 for n in range(len(JOBS) - len(ROUTER_BANKS))] + ROUTER_BANKS


def before_in_bank(bank_no, n):
    earlier = [m for m in range(n) if BANK[m] == bank_no]
    return JOBS[earlier[-1]][0] if earlier else None


ORDINAL = {}
for _e in ("act", "dve"):
    for _n, _name in enumerate(n for n, e in JOBS if e == _e):
        ORDINAL[_name] = _n + 1

CHUNKS = [("ada", i, f"ada{i}") for i in range(4)]
CHUNKS += [("in", CF_GATE, "cg1"), ("in", CF_VALUE, "ca1")]
CHUNKS += [("in", c, f"hy{2 * i + 1}") for i, c in enumerate(HY_CHUNKS)]
CHUNKS += [("in", 0, "q1"), ("in", 1, "k1"), ("in", 2, "v1")]
_gates = [("in", c, f"gate{2 * i + 1}") for i, c in enumerate(GATE_CHUNKS)]
_ada = [("ada", 4 + i, i + 1) for i in range(8)]
_branch = [("branch", n, f"merge{n}3") for n in range(3)]
CHUNKS += _gates[0:2] + _ada[0:2] + _gates[2:3] + _ada[2:3] + _gates[3:4] + _ada[3:4] + _gates[4:5]
CHUNKS += _ada[4:6] + _gates[5:6] + _branch[0:1] + _ada[6:7] + _branch[1:2] + _ada[7:8] + _branch[2:3]
CHUNKS += [("wout", i, "out11") for i in range(2)]
CHUNK_NO = {(kind, i): n for n, (kind, i, _) in enumerate(CHUNKS)}
NF = len(CHUNKS)

MISC = [("gather_a0", "act"), ("gather_a1", "act"), ("turn_a", "act"), ("hidT_a0", "act"), ("hidT_a1", "act")]
MISC += [("gather_b0", "act"), ("add_a0", "dve"), ("gather_b1", "act")]
MISC += [(f"add_a{i}", "dve") for i in (1, 2, 3)]
MISC += [("turn_b", "act"), ("hidT_b0", "act"), ("hidT_b1", "act")]
MISC += [(f"add_b{i}", "dve") for i in range(4)]
MISC_NO = {name: n for n, (name, _) in enumerate(MISC)}
MISC_BY = dict(MISC)
MISC_ORD = {}
MISC_COUNT = {}
for _e in ("act", "dve"):
    _names = [n for n, e in MISC if e == _e]
    MISC_COUNT[_e] = len(_names)
    for _n, _name in enumerate(_names):
        MISC_ORD[_name] = _n + 1


class Steps:

    def __init__(self, eng, sem):
        self.eng, self.sem, self.n = eng, sem, 0

    def __call__(self, instruction):
        instruction.then_inc(self.sem, 1)
        self.n += 1
        return self.n

    def wait(self, n=None):
        self.eng.wait_ge(self.sem, self.n if n is None else n)


class LoopSteps:

    def __init__(self, eng, sem, before):
        self.eng, self.sem, self.before, self.n = eng, sem, before, 0

    def __call__(self, instruction):
        instruction.then_inc(self.sem, 1)
        self.n += 1

    def wait(self):
        self.eng.wait_ge(self.sem, self.before + self.n)


BODY_STEPS = 4


def build_layer(nc, a, out):
    ctx = ExitStack()
    with ctx:
        def sb(name, shape, dt=F32):
            return ctx.enter_context(nc.sbuf_tensor(f"{name}_sb", shape, dt))

        def sem(name):
            return ctx.enter_context(nc.semaphore(name))

        bank = [ctx.enter_context(nc.psum_tensor(f"bank{i}", [P, 512], F32)) for i in range(8)]

        ring = sb("ring", [P, WEIGHT_SLOTS, CHUNK])
        ident = sb("ident", [P, P])
        ones = sb("ones", [P, P])
        small = sb("small", [P, 256])
        area_614 = sb("area_614", [P, 10240])
        area_6, area_1, area_4 = area_614[:, 0:3072], area_614[:, 4096:8192], area_614[:, 8192:10240]
        vec = area_614[:, 3072:3456].rearrange("p (i j) -> p i j", j=P)
        head_rows = area_614[:, 3456:3840]
        rope = area_614[:, 3840:4096].rearrange("p (c t d) -> p c t d", c=2, t=TT)
        area_2 = sb("area_2", [P, 5120])
        area_3h = sb("area_3h", [P, 6144])
        area_3, area_h = area_3h[:, 0:4096], area_3h[:, 4096:6144]
        area_5 = sb("area_5", [P, 2176])
        area_7 = sb("area_7", [P, 2560])
        area_8 = sb("area_8", [P, 1024])
        gain = head_rows[:, 0:2 * HD].rearrange("p (n d) -> p n d", d=HD)
        lam_v = head_rows[:, 2 * HD:].rearrange("p (n d) -> p n d", d=HD)
        pos = sb("pos", [P, TT, EXPERTS + 4])
        comb = sb("comb", [P, TT, EXPERTS + 4])
        iota = sb("iota", [P, SLOTS])
        before = sb("before", [P, P])
        row_sel = sb("row_sel", [6, 3, P])
        flag = sb("flag", [P, 1], I32)

        def view(area, start, shape):
            n = math.prod(shape)
            v = area[:, start:start + n]
            if len(shape) == 1:
                return v
            names = "abcd"[:len(shape)]
            return v.rearrange(f"p ({' '.join(names)}) -> p {' '.join(names)}",
                               **dict(zip(names[1:], shape[1:])))

        hT = view(area_h, 0, [KT, SEQ])
        merged = hT
        w4 = view(area_1, 0, [2, W])
        w4s = view(area_4, 0, [2, W])
        x_n = view(area_2, 2560, [TT, D])
        hy_in = view(area_1, 0, [HY_T, SEQ + 2])
        hy_cv = view(area_6, 0, [HY_T, SEQ])
        dft_f = view(area_7, 0, [TT, 768])
        dft_i = view(area_7, 1536, [4, SEQ])
        gates = [view(area_7, 0, [KT, SEQ]), view(area_1, 0, [KT, SEQ]), view(area_1, 2048, [KT, SEQ])]
        w_router = view(area_7, 2048, [KT, EXPERTS])
        spectra = view(area_2, 0, [2, 5, W])
        mod_rows = view(area_2, D, [4, D])
        g1, sh2, sc2, g2 = (mod_rows[:, i, :] for i in range(4))

        def mod_half(i):
            return area_2[:, D + i * W:D + (i + 1) * W]

        filt = view(area_3, 0, [TT, 2, 2, W])
        hy = view(area_3, 0, [3, TT, W])
        hy_tmp = view(area_3, 3072, [2, W])
        qkT = view(area_3, 0, [2, HEADS, SEQ])
        prob = view(area_3, 2048, [2, 2, TT, SEQ])
        part = view(area_1, 2048, [4, 512])
        ysp = view(area_4, 0, [4, W])
        br_hy = view(area_4, 0, [WT, SEQ])
        br_at = view(area_4, 1024, [WT, SEQ])
        x = view(area_5, 0, [TT, D])
        cf_in = view(area_5, 0, [WT, SEQ + TAPS - 1])
        cf_cv = view(area_5, WT * (SEQ + TAPS - 1), [4, SEQ])
        cf_sq = view(area_5, 0, [WT, SEQ])
        ln_ms, ln_rt, ln_r, ln_t = (area_5[:, i * SEQ:(i + 1) * SEQ] for i in range(4))
        attT = view(area_5, 0, [2, TT, SEQ])
        att = view(area_5, 1024, [TT, W])
        window = view(area_6, 512, [TT, W])
        qkv = view(area_6, 0, [3, TT, W])
        xT = view(area_2, 0, [KT, 2 * SLOTS])
        gate_s = view(area_2, 1024, [FF])
        up_s = view(area_7, 0, [FF])
        hid = up_s
        sig_s = view(area_7, 1024, [FF])
        h2 = view(area_3, 0, [TT, D])
        h2T = hT
        hidT = view(area_2, 2048, [KT, P])
        y_s = view(area_2, 3072, [D])
        bias = area_6[0:6, 0:2 * FF].rearrange("p (b m) -> p b m", b=2)
        moe_slots = [ring[:, (NF + n) % WEIGHT_SLOTS, :] for n in range(WEIGHT_SLOTS)]
        moe_slots[4:4] = [area_614[:, 2048:2048 + CHUNK], area_614[:, 6144:6144 + CHUNK]]
        moe_slots.append(area_3h[:, 2048:2048 + CHUNK])
        member = view(area_7, 2048, [TT, 4, SLOTS])
        weighted = view(area_8, 0, [TT, 4, SLOTS])
        turned = view(area_8, 512, [SEQ])
        norm2_gain = view(area_6, 2048, [D])
        squares = view(area_2, 0, [W])
        chosen = view(area_2, 1024, [TT, TOPK, EXPERTS])
        chosen_w = view(area_2, 1280, [TT, TOPK, EXPERTS])

        cond, cond_sig = small[:, 0:8], small[:, 8:16]
        n1_gain = small[:, 16:24]
        shift1 = small[:, 24:32]
        x_ss, x_ms, x_rt, x_r, x_t = (small[:, 32 + 2 * i:34 + 2 * i] for i in range(5))
        lam_s = small[:, 42:48]
        s_max = small[:, 52:68].rearrange("p (h c t) -> p h c t", c=2, t=TT)
        s_sum = small[:, 68:84].rearrange("p (h c t) -> p h c t", c=2, t=TT)
        s_inv = small[:, 84:100].rearrange("p (h c t) -> p h c t", c=2, t=TT)
        o_ms, o_rt, o_r, o_t = (small[:, 100 + 16 * i:116 + 16 * i] for i in range(4))
        top = small[:, 164:180].rearrange("p (t k) -> p t k", t=TT)
        top_w = small[:, 180:188].rearrange("p (t k) -> p t k", t=TT)
        top_s = small[:, 188:194].rearrange("p (t k) -> p t k", t=TT)
        g2_ss, g2_ms, g2_rt, g2_r, g2_t = (small[:, 196 + 2 * i:198 + 2 * i] for i in range(5))
        most = small[:, 206:207]
        x1_ss = small[:, 212:216].rearrange("p (t c) -> p t c", t=TT)
        mean_col = small[:, 208:210]
        sub_gain = small[:, 210:211]
        o_sel = sb("o_sel", [P, 24])
        top_i = sb("top_i", [P, TT, 8], U32)
        top_f = sb("top_f", [P, TT, 8])
        chosen_n = view(area_2, 2048, [EXPERTS])
        part_logit = view(area_2, 1664, [SEQ])
        mask = view(area_2, 1536, [TT, EXPERTS])
        logit = view(area_2, 1600, [TT, EXPERTS])
        tile_sum = view(area_5, TT * D, [EXPERTS])
        expert_no = sb("expert_no", [P, EXPERTS])
        b_router = sb("b_router", [P, EXPERTS])
        cond_rep = view(area_h, 1472, [KT, 32])
        mlp_y = view(area_h, 0, [4, SEQ])
        filter_net = area_1[:, 0:NET_COLS]
        zT = area_1[0:HF_EMB, NET_Z:NET_Z + SEQ]
        mlp_w = area_1[0:HF_HID, NET_W:NET_B].rearrange("p (n m) -> p n m", n=3)
        hf_col = area_1[:, NET_B:NET_COLS]
        qk_ss = view(area_5, 1024, [4, TT, GROUPS])
        hy_bias = view(area_8, 0, [2, W])
        br_cf = view(area_8, 0, [WT, SEQ])

        products_ready = sem("products_ready")
        emptied = {"act": sem("emptied_by_act"), "dve": sem("emptied_by_dve")}
        slot_landed = [sem(f"slot_landed{i}") for i in range(WEIGHT_SLOTS)]
        moe_landed = [sem(f"moe_landed{i}") for i in range(MOE_SLOTS)]
        ada_summed = sem("ada_summed")
        consts_made = sem("consts_made")
        vec_landed = sem("vec_landed")
        mlp_landed = sem("mlp_landed")
        x_landed = sem("x_landed")
        x_again_landed = sem("x_again_landed")
        window_landed = sem("window_landed")
        dft_landed = sem("dft_landed")
        hyena_landed = sem("hyena_landed")
        attn_landed = sem("attn_landed")
        router_landed = sem("router_landed")
        mod_bias_landed = sem("mod_bias_landed")
        gain2_landed = sem("gain2_landed")
        merge_done = sem("merge_done")
        dve_step = sem("dve_step")
        act_step = sem("act_step")
        pool_step = sem("pool_step")
        sqrt_asked = sem("sqrt_asked")
        sqrt_done = sem("sqrt_done")
        sin_asked = sem("sin_asked")
        sin_done = sem("sin_done")
        w4_summed = sem("w4_summed")
        cond_ready = sem("cond_ready")
        xn_ready = sem("xn_ready")
        x_squared = sem("x_squared")
        r_ready = sem("r_ready")
        modcol_ready = sem("modcol_ready")
        hy_conv_done = sem("hy_conv_done")
        pads_zeroed = sem("pads_zeroed")
        sig_ready = sem("sig_ready")
        spectra_mixed = sem("spectra_mixed")
        z_ready = sem("z_ready")
        conv_done = sem("conv_done")
        centred = sem("centred")
        cf_scaled = sem("cf_scaled")
        cf_act = sem("cf_act")
        br_cf_ready = sem("br_cf_ready")
        roped = sem("roped")
        max_ready = sem("max_ready")
        lam_ready = sem("lam_ready")
        lam_exp = sem("lam_exp")
        att_ready = sem("att_ready")
        o_ready = sem("o_ready")
        gates_ready = sem("gates_ready")
        mod_zeroed = sem("mod_zeroed")
        merged_ready = sem("merged_ready")
        h2_ready = sem("h2_ready")
        top_ready = sem("top_ready")
        top_exp = sem("top_exp")
        mask_ready = sem("mask_ready")
        flag_ready = sem("flag_ready")
        stored = sem("stored")
        out_ready = sem("out_ready")
        weights_used = sem("weights_used")
        gate_up_done = sem("gate_up_done")
        gate_up_read = sem("gate_up_read")
        y_done = sem("y_done")
        y_read = sem("y_read")
        misc_done = sem("misc_done")
        misc_out = {"act": sem("misc_out_act"), "dve": sem("misc_out_dve")}
        bias_landed = [sem(f"bias_landed{b}") for b in range(2)]
        gate_min = sem("gate_min")
        sigmoid_done = sem("sigmoid_done")
        hid_ready = sem("hid_ready")
        member_ready = sem("member_ready")
        weighted_ready = sem("weighted_ready")
        moe_step = sem("moe_step")
        pass_step = sem("pass_step")

        def slot_of(kind, i):
            return ring[:, CHUNK_NO[kind, i] % WEIGHT_SLOTS, :]

        def wait_chunk(eng, kind, i):
            n = CHUNK_NO[kind, i]
            eng.wait_ge(slot_landed[n % WEIGHT_SLOTS], 16 * (n // WEIGHT_SLOTS + 1))

        def wait_emptied(eng, name):
            eng.wait_ge(emptied[EMPTIED_BY[name]], ORDINAL[name])

        def open_bank(pe, name):
            n = JOB[name]
            before_it = before_in_bank(BANK[n], n)
            if before_it is not None:
                wait_emptied(pe, before_it)
            return bank[BANK[n]]

        def product(eng, name):
            eng.wait_ge(products_ready, JOB[name] + 1)
            return bank[BANK[JOB[name]]]

        def chunk_source(kind, i):
            if kind == "ada":
                return a["w_ada"][0, :, i * W:(i + 1) * W].rearrange("(k p) m -> p k m", p=P)
            if kind == "in":
                return a["w_in"][0, :, i * W:(i + 1) * W].rearrange("(k p) m -> p k m", p=P)
            if kind == "branch":
                return a["w_branch"][0, i].rearrange("(k p) m -> p k m", p=P)
            return a["w_out"][0, i * W:(i + 1) * W, :].rearrange("(k p) m -> p k m", p=P)

        def slot_view(kind, i):
            cols = W if kind in ("ada", "in") else D
            return slot_of(kind, i).rearrange("p (k m) -> p k m", m=cols)

        def moe_slot(b, c):
            return moe_slots[SLOT_OF[PAIR_CHUNKS * b + c]]

        def moe_chunk_landed(b, c):
            return moe_landed[SLOT_OF[PAIR_CHUNKS * b + c]]

        def wait_moe_chunk(eng, i, b, c):
            n = PAIR_CHUNKS * b + c
            eng.wait_ge(moe_chunk_landed(b, c), i * (16 * SLOT_OF.count(SLOT_OF[n]))
                        + 16 * SLOT_OF[:n + 1].count(SLOT_OF[n]))

        def moe_bank(name):
            return bank[6 + MISC_NO[name] % 2]

        def open_misc(pe, i, name):
            n = MISC_NO[name]
            prev = MISC[n - 2][0]
            by = MISC_BY[prev]
            body = 1 if n >= 2 else 0
            pe.wait_ge(misc_out[by], i * MISC_COUNT[by] + body * MISC_COUNT[by] + MISC_ORD[prev])
            return moe_bank(name)

        def misc_product(eng, i, name):
            eng.wait_ge(misc_done, i * len(MISC) + MISC_NO[name] + 1)
            return moe_bank(name)

        def wait_misc_out(pe, i, name):
            by = MISC_BY[name]
            pe.wait_ge(misc_out[by], i * MISC_COUNT[by] + MISC_COUNT[by] + MISC_ORD[name])

        block = ctx.enter_context(nc.Block())

        @block.sync
        def _(sp):
            sp.dma_start(filter_net, a["filter_net"]).then_inc(mlp_landed, 16)
            sp.dma_start(vec[:, :, :], a["columns"].rearrange("p (i j) -> p i j", j=P)).then_inc(vec_landed, 16)

            def load_chunk(n):
                kind, i, _ = CHUNKS[n]
                if n >= WEIGHT_SLOTS:
                    wait_freed(n - WEIGHT_SLOTS)
                sp.dma_start(slot_view(kind, i), chunk_source(kind, i))\
                    .then_inc(slot_landed[n % WEIGHT_SLOTS], 16)

            def wait_freed(n):
                user = CHUNKS[n][2]
                if isinstance(user, str):
                    sp.wait_ge(products_ready, JOB[user] + 1)
                else:
                    sp.wait_ge(ada_summed, user)

            load_chunk(0)
            load_chunk(1)
            sp.dma_start(x[:, :, :], a["x"][0].rearrange("(t p) m -> p t m", p=P)).then_inc(x_landed, 16)
            sp.dma_start(window, a["window"].rearrange("(t p) m -> p t m", p=P)).then_inc(window_landed, 16)
            sp.dma_start(dft_f, a["dft_f"].rearrange("(t p) m -> p t m", p=P)).then_inc(dft_landed, 16)
            load_chunk(2)
            load_chunk(3)
            load_chunk(4)
            sp.dma_start(dft_i, a["dft_i"].rearrange("(t p) m -> p t m", p=P)).then_inc(hyena_landed, 16)
            sp.dma_start(hy_bias, a["hy_bias"][0:1].to_broadcast([P, 2, W])).then_inc(hyena_landed, 16)
            for n in range(5, NF):
                load_chunk(n)

            def wait_used(i, b, c):
                if c < 7:
                    sp.wait_ge(weights_used, i * 20 + 10 * b + c + 1)
                elif c == 7:
                    sp.wait_ge(gate_up_done, i * 4 + 2 * b + 2)
                elif c < 11:
                    sp.wait_ge(weights_used, i * 20 + 10 * b + c)
                else:
                    sp.wait_ge(y_done, i * 4 + 2 * b + 2)

            def wait_slot(i, n):
                earlier = [m for m in range(n) if SLOT_OF[m] == SLOT_OF[n]]
                if earlier:
                    wait_used(i, earlier[-1] // PAIR_CHUNKS, earlier[-1] % PAIR_CHUNKS)
                else:
                    m = max(m for m in range(BODY_CHUNKS) if SLOT_OF[m] == SLOT_OF[n])
                    wait_used(i - 1, m // PAIR_CHUNKS, m % PAIR_CHUNKS)

            def load_moe(b, c, j):
                e0 = j * 4 + 2 * b
                dst = moe_slot(b, c).rearrange("p (e m) -> p e m", e=2)
                if c < 8:
                    src = a["w_gu"][0, bass.ds(e0, 2), c * P:(c + 1) * P, :].rearrange("e p m -> p e m")
                else:
                    k = 2 * (c - 8)
                    src = a["w_down"][0, bass.ds(e0, 2), k * P:(k + 2) * P, :]\
                        .rearrange("e (p k) m -> p e (k m)", k=2)
                sp.dma_start(dst, src).then_inc(moe_chunk_landed(b, c), 16)

            def load_bias(b, j):
                e0 = j * 4 + 2 * b
                sp.dma_start(bias[:, b, :], a["b_experts"][bass.ds(e0, 2), :]
                             .rearrange("e (g m) -> (e g) m", g=3)).then_inc(bias_landed[b], 16)

            def load(i, j, n):
                wait_slot(i, n)
                load_moe(n // PAIR_CHUNKS, n % PAIR_CHUNKS, j)

            def body(i, j, last):
                for n in range(MOE_SLOTS, BODY_CHUNKS):
                    load(i, j, n)
                    if n == BIAS_AT and not last:
                        sp.wait_ge(y_done, i * 4 + 1)
                        load_bias(0, j + 1)
                if not last:
                    for n in range(MOE_SLOTS):
                        load(i + 1, j + 1, n)
                    sp.wait_ge(y_done, i * 4 + 3)
                    load_bias(1, j + 1)

            def one_pass(p, first=False):
                i0 = p * BODIES
                if first:
                    sp.wait_ge(products_ready, JOB["oT1"] + 1)
                else:
                    sp.wait_ge(y_done, i0 * 4)
                for b in range(2):
                    load_bias(b, 0)
                for n in range(MOE_SLOTS):
                    if not first:
                        wait_slot(i0, n)
                    elif n < 4:
                        wait_freed(NF + n - WEIGHT_SLOTS)
                    elif n == 4:
                        sp.wait_ge(merge_done, 1)
                    elif n in (6, 7):
                        wait_freed(NF + n - 2 - WEIGHT_SLOTS)
                    elif n == 8:
                        sp.wait_ge(products_ready, JOB["partial"] + 1)
                    load_moe(n // PAIR_CHUNKS, n % PAIR_CHUNKS, 0)
                with sp.Fori(0, BODIES - 1) as j:
                    body(i0 + j, j, False)
                body(i0 + (BODIES - 1), BODIES - 1, True)

            one_pass(0, first=True)
            sp.wait_ge(flag_ready, 1)
            over = sp.value_load(flag[0:1, 0:1], min_val=0, max_val=SEQ)
            with sp.If(over > SLOTS):
                with sp.Fori(1, PASSES) as p:
                    one_pass(p)

            sp.wait_ge(out_ready, 1)
            for t in range(TT):
                sp.dma_start(out[0, t * P:(t + 1) * P, :], x[:, t, :]).then_inc(stored, 16)
            sp.wait_ge(stored, 16 * TT)

        @block.gpsimd
        def _(pool):
            step = Steps(pool, pool_step)
            step(pool.memset(ident[:, :], 0.0))
            step(pool.memset(before[:, :], 1.0))
            step(pool.memset(row_sel[:, :, :], 0.0))
            step.wait()
            step(pool.affine_select(out=ident[:, :], in_=ident[:, :], compare_op=ALU.not_equal, fill=1.0,
                                    base=0, pattern=[[-1, P]], channel_multiplier=1))
            step(pool.affine_select(out=before[:, :], in_=before[:, :], compare_op=ALU.is_gt, fill=0.0,
                                    base=0, pattern=[[1, P]], channel_multiplier=-1))
            step(pool.affine_select(out=row_sel[:, :, :].rearrange("p g (e s) -> p g e s", e=2),
                                    in_=row_sel[:, :, :].rearrange("p g (e s) -> p g e s", e=2),
                                    compare_op=ALU.not_equal, fill=1.0, base=0,
                                    pattern=[[-1, 3], [-3, 2], [0, SLOTS]], channel_multiplier=1))
            step(pool.iota(iota[:, :], pattern=[[1, SLOTS]], base=0, channel_multiplier=0,
                           allow_small_or_imprecise_dtypes=True))
            step(pool.iota(expert_no[:, :], pattern=[[1, EXPERTS]], base=0, channel_multiplier=0,
                           allow_small_or_imprecise_dtypes=True))
            step(pool.memset(ones[:, :], 1.0))
            step(pool.memset(pos[:, :, :], FAR))
            step(pool.memset(comb[:, :, :], 0.0))
            step.wait()
            pool.memset(mean_col, 1.0 / 32).then_inc(consts_made, 1)
            pool.wait_ge(products_ready, JOB["hyT21"] + 1)
            for t in range(TT):
                pool.dma_start(qkv[:, :, t, :], a["b_in"][0:1, 0:3 * W].rearrange("o (j m) -> o j m", m=W)
                               .to_broadcast([P, 3, W])).then_inc(attn_landed, 16)
            pool.dma_start(rope[:, :, :, :], a["rope"].rearrange("c (t p) m -> p c t m", p=P))\
                .then_inc(attn_landed, 16)
            pool.dma_start(head_rows[:, :], a["head_rows"].to_broadcast([P, 6 * HD])).then_inc(attn_landed, 16)
            pool.wait_ge(products_ready, JOB["inv11"] + 1)
            pool.dma_start(w_router[:, :, :], a["w_router"][0].rearrange("(k p) m -> p k m", p=P))\
                .then_inc(router_landed, 16)
            pool.dma_start(b_router[:, :], a["b_router"].to_broadcast([P, EXPERTS])).then_inc(router_landed, 16)
            pool.wait_ge(spectra_mixed, 4)
            pool.memset(mod_rows[:, :, :], 0.0).then_inc(mod_zeroed, 1)
            pool.wait_ge(mod_zeroed, 1)
            pool.dma_start(area_2[0:1, D:5 * D], a["b_ada"][0:1, 2 * D:6 * D]).then_inc(mod_bias_landed, 16)
            pool.wait_ge(products_ready, JOB["oT1"] + 1)
            pool.dma_start(x[:, :, :], a["x"][0].rearrange("(t p) m -> p t m", p=P))\
                .then_inc(x_again_landed, 16)
            pool.dma_start(norm2_gain, a["norm2_g"].to_broadcast([P, D])).then_inc(gain2_landed, 16)

        @block.tensor
        def _(pe):
            def job(name):
                return open_bank(pe, name)

            def end(ins):
                ins.then_inc(products_ready, 1)

            pe.wait_ge(consts_made, 1)
            pe.wait_ge(mlp_landed, 16)
            def ada(i):
                b = job(f"ada{i}")
                w = slot_view("ada", i)
                pe.wait_ge(cond_ready, 1)
                wait_chunk(pe, "ada", i)
                for k in range(KT):
                    g = k % 4
                    ins = pe.matmul(b[32 * g:32 * g + 32, :], cond_rep[:, k, :], w[:, k, :],
                                    start=k < 4, stop=k >= 4, skip_group_check=True)
                end(ins)

            def spectrum(o, first, last):
                parts = [(0, 0), (P, 0), (512, 0), (640, 1), (384, 1)]
                for j in range(first, last):
                    col, s = parts[j]
                    b = job(f"spectrum{o}{j}")
                    for t in range(TT):
                        ins = pe.matmul(b[:, :], dft_f[:, t, col:col + P], filt[:, t, o, s, :],
                                        start=t == 0, stop=t == TT - 1)
                    end(ins)

            def mlp(n):
                b = job(f"mlp{n}")
                w, x_in = mlp_w[:, n, :], mlp_y[0:HF_HID, 3, :]
                if n == 0:
                    w, x_in = mlp_w[0:HF_EMB, 0, :], zT[:, :]
                else:
                    pe.wait_ge(sin_done, n)
                for half in range(2):
                    ins = pe.matmul(b[half * HF_HID:(half + 1) * HF_HID, 0:SEQ], w, x_in, start=True, stop=True)
                end(ins)

            mlp(0)
            mlp(1)
            ada(0)
            mlp(2)
            ada(1)
            pe.wait_ge(sin_done, 3)
            pe.wait_ge(w4_summed, 1)
            for s in range(2):
                for t in range(TT):
                    for o in range(2):
                        b = job(f"filter{o}{s}{t}")
                        r = slice(o * HF_HID, (o + 1) * HF_HID)
                        end(pe.matmul(b[:, :], mlp_y[r, 3, t * P:(t + 1) * P], w4s[r, s, :],
                                      start=True, stop=True))
            pe.wait_ge(dft_landed, 16)
            wait_emptied(pe, "filter011")
            spectrum(0, 0, 2)
            ada(2)
            spectrum(0, 2, 3)
            ada(3)
            spectrum(0, 3, 4)

            def turn_x(i):
                b = job(f"xT{i}")
                for kk in range(2):
                    for t in range(TT):
                        c = (2 * i + kk) * P
                        ins = pe.transpose(b[:, (kk * TT + t) * P:(kk * TT + t + 1) * P],
                                           x_n[:, t, c:c + P], ident[:, :])
                end(ins)

            pe.wait_ge(xn_ready, TT)
            turn_x(0)
            b = job("modcol")
            for i in range(4):
                wait_emptied(pe, f"ada{i}")
                for m in range(4):
                    c = 4 * i + m
                    ins = pe.matmul(b[:, c:c + 1], part[:, i, m * P:(m + 1) * P], mean_col[:, 0:1],
                                    start=True, stop=True)
            end(ins)
            turn_x(1)
            turn_x(2)
            turn_x(3)
            spectrum(0, 4, 5)

            def channel_major(name, kind, i, m0):
                b = job(name)
                w = slot_view(kind, i)
                wait_chunk(pe, kind, i)
                for m in range(2):
                    for k in range(KT):
                        ins = pe.matmul(b[:, m * SEQ:(m + 1) * SEQ], w[:, k, (m0 + m) * P:(m0 + m + 1) * P],
                                        hT[:, k, :], start=k == 0, stop=k == KT - 1)
                end(ins)

            def token_major(name, i, t):
                b = job(name)
                w = slot_view("in", i)
                wait_chunk(pe, "in", i)
                for k in range(KT):
                    ins = pe.matmul(b[:, :], hT[:, k, t * P:(t + 1) * P], w[:, k, :],
                                    start=k == 0, stop=k == KT - 1)
                end(ins)

            wait_emptied(pe, "xT2")
            wait_emptied(pe, "xT3")
            for i in range(2):
                channel_major(f"cg{i}", "in", CF_GATE, 2 * i)
            for i in range(2):
                channel_major(f"ca{i}", "in", CF_VALUE, 2 * i)
            for i in range(6):
                channel_major(f"hy{i}", "in", HY_CHUNKS[i // 2], 2 * (i % 2))
            wait_emptied(pe, "filter111")
            spectrum(1, 0, 5)

            for g in range(3):
                pe.wait_ge(hy_conv_done, WT * (g + 1))
                for t in range(TT):
                    b = job(f"hyT{g}{t}")
                    for m in range(WT):
                        ins = pe.transpose(b[:, m * P:(m + 1) * P],
                                           hy_cv[:, g * WT + m, t * P:(t + 1) * P], ident[:, :])
                    end(ins)

            def to_frequency(o):
                for m in (0, 2, 1, 3):
                    b = job(f"u{o}{m}")
                    for t in range(TT):
                        ins = pe.matmul(b[:, :], dft_f[:, t, m * P:(m + 1) * P], hy[:, 0, t, :],
                                        start=t == 0, stop=t == TT - 1)
                    end(ins)

            def to_time(o):
                pe.wait_ge(spectra_mixed, 2 * o + 2)
                for t in range(TT):
                    b = job(f"inv{o}{t}")
                    for m in range(4):
                        ins = pe.matmul(b[:, :], dft_i[:, m, t * P:(t + 1) * P], ysp[:, m, :],
                                        start=m == 0, stop=m == 3)
                    end(ins)

            wait_emptied(pe, "hyT01")
            to_frequency(0)
            for t in range(TT):
                token_major(f"q{t}", 0, t)
            b = job("mean")
            pe.wait_ge(conv_done, 1)
            for m in range(WT):
                ins = pe.matmul(b[:, 0:SEQ], ones[:, :], cf_cv[:, m, :], start=m == 0, stop=m == WT - 1)
            end(ins)
            pe.wait_ge(hyena_landed, 32)
            to_time(0)
            b = job("var")
            pe.wait_ge(centred, 1)
            for m in range(WT):
                ins = pe.matmul(b[:, 0:SEQ], ones[:, :], cf_sq[:, m, :], start=m == 0, stop=m == WT - 1)
            end(ins)
            for t in range(TT):
                token_major(f"k{t}", 1, t)
            pe.wait_ge(z_ready, TT)
            to_frequency(1)
            for t in range(TT):
                token_major(f"v{t}", 2, t)
            to_time(1)

            def gate(i):
                channel_major(f"gate{i}", "in", GATE_CHUNKS[i // 2], 2 * (i % 2))

            gate(0)
            pe.wait_ge(z_ready, 2 * TT)
            for i in range(2):
                b = job(f"zT{i}")
                for m in range(2):
                    for t in range(TT):
                        c = (2 * i + m) * P
                        ins = pe.transpose(b[:, (m * TT + t) * P:(m * TT + t + 1) * P],
                                           hy[:, 0, t, c:c + P], ident[:, :])
                end(ins)
            for j in range(2):
                for t in range(TT):
                    b = job(f"qkT{j}{t}")
                    pe.wait_ge(roped, TT * j + t + 1)
                    for h in range(HEADS):
                        ins = pe.transpose(b[:, h * P:(h + 1) * P], qkv[:, j, t, h * P:(h + 1) * P], ident[:, :])
                    end(ins)
            gate(1)
            wait_emptied(pe, "qkT11")

            def scores(h):
                for c in range(2):
                    b = job(f"score{h}{c}")
                    r = slice(c * HD, (c + 1) * HD)
                    for t in range(TT):
                        ins = pe.matmul(b[:, t * SEQ:(t + 1) * SEQ], qkT[r, 0, h, t * P:(t + 1) * P],
                                        qkT[r, 1, h, :], start=True, stop=True)
                    end(ins)

            def turn_weights(h):
                b = job(f"aT{h}")
                pe.wait_ge(att_ready, h + 1)
                for kt in range(TT):
                    for t in range(TT):
                        ins = pe.transpose(b[:, kt * SEQ + t * P:kt * SEQ + (t + 1) * P],
                                           prob[:, h % 2, 0, t, kt * P:(kt + 1) * P], ident[:, :])
                end(ins)

            def attend(h):
                b = job(f"o{h}")
                wait_emptied(pe, f"aT{h}")
                wait_emptied(pe, "v1")
                for t in range(TT):
                    for kt in range(TT):
                        ins = pe.matmul(b[:, t * P:(t + 1) * P], attT[:, h % 2, kt, t * P:(t + 1) * P],
                                        qkv[:, 2, kt, h * P:(h + 1) * P], start=kt == 0, stop=kt == TT - 1)
                end(ins)

            for h in range(HEADS + 2):
                if h < HEADS:
                    scores(h)
                if h:
                    gate(h + 1)
                if h > 1:
                    attend(h - 2)
                if 0 < h <= HEADS:
                    turn_weights(h - 1)
            gate(7)
            gate(8)
            pe.wait_ge(o_ready, 1)
            for i in range(2):
                b = job(f"oT{i}")
                for m in range(2):
                    for t in range(TT):
                        c = (2 * i + m) * P
                        ins = pe.transpose(b[:, (m * TT + t) * P:(m * TT + t + 1) * P],
                                           att[:, t, c:c + P], ident[:, :])
                end(ins)
            for i in range(9, 12):
                gate(i)

            def ada_rows(i):
                b = job(f"adab{i}")
                pe.wait_ge(ada_summed, i + 1)
                end(pe.matmul(b[:, :], ones[:, :], mod_half(i), start=True, stop=True))

            def merge(n, branch):
                w = slot_view("branch", n)
                wait_chunk(pe, "branch", n)
                for mp in range(4):
                    b = job(f"merge{n}{mp}")
                    for m in range(2):
                        c = (2 * mp + m) * P
                        for k in range(WT):
                            ins = pe.matmul(b[:, m * SEQ:(m + 1) * SEQ], w[:, k, c:c + P],
                                            branch[:, k, :], start=k == 0, stop=k == WT - 1)
                    end(ins)

            wait_emptied(pe, "oT1")
            merge(0, br_at)
            wait_emptied(pe, "zT1")
            merge(1, br_hy)
            pe.wait_ge(br_cf_ready, 1)
            merge(2, br_cf)
            for i in range(8):
                ada_rows(i)
            for i in range(2):
                wait_chunk(pe, "wout", i)
            pe.wait_ge(merged_ready, 4)
            for t in range(TT):
                for c in range(2):
                    b = job(f"out{t}{c}")
                    for k in range(KT):
                        w = slot_view("wout", k // WT)
                        ins = pe.matmul(b[:, :], merged[:, k, t * P:(t + 1) * P],
                                        w[:, k % WT, c * W:(c + 1) * W], start=k == 0, stop=k == KT - 1)
                    end(ins)
            def misc_end(ins):
                ins.then_inc(misc_done, 1)

            def gather(i, s, b, g):
                o = open_misc(pe, i, f"gather_{s}{g}")
                for kk in range(4):
                    c = (4 * g + kk) * P
                    for t in range(TT):
                        ins = pe.matmul(o[:, kk * P:(kk + 1) * P], h2[:, t, c:c + P],
                                        member[:, t, 2 * b:2 * b + 2, :].rearrange("p e s -> p (e s)"),
                                        start=t == 0, stop=t == TT - 1)
                misc_end(ins)

            def gate_bias(i, b):
                pe.wait_ge(bias_landed[b], i * 16 + 16)
                pe.wait_ge(gate_up_read, i * 4 + 4 + 2 * b)
                for n in range(4):
                    c = (n % 2) * 512
                    pe.matmul(bank[n][:, :], row_sel[:, n // 2, :], bias[:, b, c:c + 512],
                              start=True, stop=False, skip_group_check=True)

            def router():
                for n in range(4):
                    wait_emptied(pe, before_in_bank(n, len(JOBS)))
                gate_bias(0, 0)
                for t in range(TT):
                    for c in range(2):
                        b = job(f"h2T{t}{c}")
                        pe.wait_ge(h2_ready, 2 * t + c + 1)
                        for k in range(4):
                            ins = pe.transpose(b[:, k * P:(k + 1) * P], h2[:, t, c * W + k * P:c * W + (k + 1) * P],
                                               ident[:, :])
                        end(ins)
                b = job("partial")
                pe.wait_ge(router_landed, 32)
                for t in range(TT):
                    for k in range(KT):
                        if k % 4 == 0:
                            wait_emptied(pe, f"h2T{t}{k // 4}")
                        g = k % 4
                        ins = pe.matmul(b[32 * g:32 * g + 32, t * P:(t + 1) * P], w_router[:, k, :],
                                        h2T[:, k, t * P:(t + 1) * P], start=k < 4, stop=k >= 4,
                                        skip_group_check=True)
                end(ins)
                b = job("logits")
                wait_emptied(pe, "partial")
                for t in range(TT):
                    ins = pe.matmul(b[:, t * EXPERTS:(t + 1) * EXPERTS], part_logit[:, t * P:(t + 1) * P],
                                    tile_sum, start=True, stop=True)
                end(ins)
                b = job("rank")
                pe.wait_ge(mask_ready, 1)
                both = mask.rearrange("p t e -> p (t e)")
                pe.matmul(b[:, 0:2 * EXPERTS], before[:, :], both, start=True, stop=True, skip_group_check=True)
                pe.matmul(b[:, EXPERTS:2 * EXPERTS], ones[:, :], mask[:, 0, :], start=False, stop=True,
                          skip_group_check=True)
                end(pe.matmul(b[:, 64:64 + 2 * EXPERTS], ones[:, :], both, start=True, stop=True,
                              skip_group_check=True))

            def gate_up(i, b, p):
                s = "ab"[b]
                if b == 0:
                    pe.wait_ge(member_ready, (i + p) * 2 + 2)
                gather(i, s, b, 0)
                for k in range(KT):
                    if k == 2:
                        gather(i, s, b, 1)
                    if k % 4 == 0:
                        wait_misc_out(pe, i, f"gather_{s}{k // 4}")
                    if b == 1 and k in (1, 3, 4, 5):
                        scatter(i, "a", 0, (1, 3, 4, 5).index(k))
                    if k == 6:
                        turn(i, f"turn_{s}", b, p)
                    wait_moe_chunk(pe, i, b, k)
                    w = moe_slot(b, k).rearrange("p (e m) -> p e m", e=2)
                    for n in (0, 2, 1, 3):
                        for e in range(2):
                            r = slice(e * SLOTS, (e + 1) * SLOTS)
                            ins = pe.matmul(bank[n][r, :], xT[:, k, r],
                                            w[:, e, n * 512:(n + 1) * 512],
                                            start=False, stop=k == KT - 1, skip_group_check=True)
                        if k == KT - 1 and n in (2, 3):
                            ins.then_inc(gate_up_done, 1)
                    if k < KT - 1:
                        ins.then_inc(weights_used, 1)

            def turn(i, name, b, p):
                pe.wait_ge(weighted_ready, (i + p) * 2 + 2)
                o = open_misc(pe, i, name)
                for t in range(TT):
                    ins = pe.transpose(o[:, t * P:(t + 1) * P],
                                       weighted[:, t, 2 * b:2 * b + 2, :].rearrange("p e s -> p (e s)"),
                                       ident[:, :])
                misc_end(ins)

            def hidden_turn(i, name, b, half):
                o = open_misc(pe, i, name)
                pe.wait_ge(hid_ready, i * 4 + 2 * b + half + 1)
                for m in range(4):
                    c = 2 * P * (2 * half + m // 2) + m % 2
                    ins = pe.transpose(o[:, m * P:(m + 1) * P], hid[:, c:c + 2 * P - 1:2], ident[:, :])
                misc_end(ins)

            def down_bias(i, b):
                pe.wait_ge(y_read, i * 4 + 4 + 2 * b)
                for n in range(2):
                    ins = pe.matmul(bank[4 + n][:, :], row_sel[:, 2, :], bias[:, b, n * 512:(n + 1) * 512],
                                    start=True, stop=False, skip_group_check=True)

            def down(i, b, s):
                for ch in range(4):
                    if ch == 1:
                        hidden_turn(i, f"hidT_{s}1", b, 1)
                    wait_moe_chunk(pe, i, b, 8 + ch)
                    if ch % 2 == 0:
                        wait_misc_out(pe, i, f"hidT_{s}{ch // 2}")
                    w = moe_slot(b, 8 + ch).rearrange("p (e k m) -> p e k m", e=2, k=2)
                    for n in range(2):
                        for kk in range(2):
                            k = 2 * ch + kk
                            for e in range(2):
                                r = slice(e * SLOTS, (e + 1) * SLOTS)
                                ins = pe.matmul(bank[4 + n][r, :], hidT[:, k, e * SLOTS:(e + 1) * SLOTS],
                                                w[:, e, kk, n * 512:(n + 1) * 512],
                                                start=False, stop=k == KT - 1, skip_group_check=True)
                        if ch == 3:
                            ins.then_inc(y_done, 1)
                    if ch < 3:
                        ins.then_inc(weights_used, 1)

            def scatter(i, s, b, n):
                t, c = n % 2, n // 2
                pe.wait_ge(y_read, i * 4 + 4 + 2 * b + c + 1)
                o = open_misc(pe, i, f"add_{s}{n}")
                misc_end(pe.matmul(o[:, :], turned[:, t * P:(t + 1) * P], y_s[:, c * W:(c + 1) * W],
                                   start=True, stop=True))

            def body(i, p, last=False):
                for b, s in enumerate("ab"):
                    gate_up(i, b, p)
                    down_bias(i, b)
                    hidden_turn(i, f"hidT_{s}0", b, 0)
                    down(i, b, s)
                    if b == 0:
                        gate_bias(i, 1)
                    elif not last:
                        gate_bias(i + 1, 0)
                for n in range(4):
                    scatter(i, "b", 1, n)

            def one_pass(p, first=False):
                if not first:
                    gate_bias(p * BODIES, 0)
                with pe.Fori(0, BODIES - 1) as j:
                    body(p * BODIES + j, p)
                body(p * BODIES + (BODIES - 1), p, last=True)

            router()
            one_pass(0, first=True)
            pe.wait_ge(flag_ready, 1)
            over = pe.value_load(flag[0:1, 0:1], min_val=0, max_val=SEQ)
            with pe.If(over > SLOTS):
                with pe.Fori(1, PASSES) as p:
                    one_pass(p)

        @block.scalar
        def _(act):
            step = Steps(act, act_step)

            def out_of(name, ins):
                ins.then_inc(emptied["act"], 1)

            def copy_out(name, dst, cols=None):
                b = product(act, name)
                out_of(name, act.activation(dst, b[:, 0:cols] if cols else b[:, :], ACT.Copy))

            def root(n, dst, src):
                act.wait_ge(sqrt_asked, n)
                act.activation(dst, src, ACT.Sqrt).then_inc(sqrt_done, 1)

            act.wait_ge(vec_landed, 16)
            act.activation(cond_sig, vec[:, 0, V_C:V_C + KT], ACT.Sigmoid).then_inc(sig_ready, 1)
            def sine(n):
                act.wait_ge(sin_asked, n)
                act.activation(mlp_y[:, 3, :], mlp_y[:, 0, :], ACT.Sin).then_inc(sin_done, 1)

            sine(1)
            sine(2)
            copy_out("ada0", part[:, 0, :])
            sine(3)
            copy_out("ada1", part[:, 1, :])
            act.wait_ge(x_landed, 16)
            for t in range(TT):
                act.activation(x_n[:, t, :], x[:, t, :], ACT.Square, accum_out=x_ss[:, t:t + 1])\
                    .then_inc(x_squared, 1)
            root(1, x_rt, x_ms)
            act.wait_ge(r_ready, 1)
            act.wait_ge(x_squared, TT)
            for t in range(TT):
                act.activation(x_n[:, t, :], x[:, t, :], ACT.Copy, scale=x_r[:, t:t + 1]).then_inc(xn_ready, 1)
            copy_out("spectrum00", spectra[:, 0, 0, :])
            copy_out("spectrum01", spectra[:, 0, 1, :])
            copy_out("ada2", part[:, 2, :])
            copy_out("spectrum02", spectra[:, 0, 2, :])
            copy_out("ada3", part[:, 3, :])
            copy_out("spectrum03", spectra[:, 0, 3, :])
            act.wait_ge(modcol_ready, 1)
            for i in (0, 2):
                b = product(act, f"xT{i}")
                act.activation(hT[:, 2 * i, :], b[:, 0:SEQ], ACT.Identity,
                               bias=shift1[:, 2 * i:2 * i + 1], scale=n1_gain[:, 2 * i:2 * i + 1])
                out_of("", act.activation(hT[:, 2 * i + 1, :], b[:, SEQ:2 * SEQ], ACT.Identity,
                                          bias=shift1[:, 2 * i + 1:2 * i + 2],
                                          scale=n1_gain[:, 2 * i + 1:2 * i + 2]))
            copy_out("spectrum04", spectra[:, 0, 4, :])
            act.wait_ge(products_ready, JOB["modcol"] + 1)
            act.wait_ge(pads_zeroed, 1)
            for i in range(2):
                b = product(act, f"cg{i}")
                for m in range(2):
                    c = 2 * i + m
                    bias = V_BIN + HY_T + WT + c
                    ins = act.activation(cf_cv[:, c, :], b[:, m * SEQ:(m + 1) * SEQ], ACT.Sigmoid,
                                         bias=vec[:, 0, bias:bias + 1])
                out_of("", ins)
            for i in range(6):
                b = product(act, f"hy{i}")
                for m in range(2):
                    c = 2 * i + m
                    ins = act.activation(hy_in[:, c, 1:SEQ + 1], b[:, m * SEQ:(m + 1) * SEQ], ACT.Identity,
                                         bias=vec[:, 0, V_BIN + c:V_BIN + c + 1])
                out_of("", ins)
            for j in range(5):
                copy_out(f"spectrum1{j}", spectra[:, 1, j, :])
            for g in range(3):
                for t in range(TT):
                    copy_out(f"hyT{g}{t}", hy[:, g, t, :])

            def gate_out(i):
                b = product(act, f"gate{i}")
                for m in range(2):
                    c = 2 * i + m
                    bias = V_BIN + HY_T + 2 * WT + c
                    ins = act.activation(gates[c // KT][:, c % KT, :], b[:, m * SEQ:(m + 1) * SEQ],
                                         ACT.Identity, bias=vec[:, 0, bias:bias + 1])
                out_of("", ins)

            root(2, ln_rt, ln_ms)
            root(3, qk_ss[:, 1, :, :], qk_ss[:, 0, :, :])
            root(4, qk_ss[:, 1, :, :], qk_ss[:, 0, :, :])
            gate_out(0)
            for i in range(2):
                copy_out(f"zT{i}", br_hy[:, 2 * i:2 * i + 2, :].rearrange("p m s -> p (m s)"))
            for j in range(2):
                for t in range(TT):
                    b = product(act, f"qkT{j}{t}")
                    out_of("", act.activation(qkT[:, j, :, t * P:(t + 1) * P],
                                              b[:, :].rearrange("p (h s) -> p h s", h=HEADS), ACT.Copy))
            gate_out(1)
            for m in range(WT):
                act.wait_ge(cf_scaled, m + 1)
                act.activation(cf_cv[:, m, :], br_cf[:, m, :], ACT.Sigmoid).then_inc(cf_act, 1)
            act.wait_ge(lam_ready, 2)
            act.activation(lam_s[:, 2:4], lam_s[:, 0:2], ACT.Exp).then_inc(lam_exp, 1)
            for h in range(HEADS + 2):
                if h < HEADS:
                    for c in range(2):
                        act.wait_ge(max_ready, 2 * h + c + 1)
                        b = product(act, f"score{h}{c}")
                        for t in range(TT):
                            ins = act.activation(prob[:, h % 2, c, t, :], b[:, t * SEQ:(t + 1) * SEQ], ACT.Exp,
                                                 bias=s_max[:, h, c, t:t + 1], scale=SCALE,
                                                 accum_out=s_sum[:, h, c, t:t + 1])
                        out_of("", ins)
                if h:
                    gate_out(h + 1)
                if 0 < h <= HEADS:
                    if h == 1:
                        act.wait_ge(br_cf_ready, 1)
                    if h > 2:
                        act.wait_ge(products_ready, JOB[f"o{h - 3}"] + 1)
                    b = product(act, f"aT{h - 1}")
                    out_of("", act.activation(attT[:, (h - 1) % 2, :, :],
                                              b[:, :].rearrange("p (k s) -> p k s", k=TT), ACT.Copy))
            root(5, o_rt, o_ms)
            gate_out(7)
            gate_out(8)
            for i in range(2):
                b = product(act, f"oT{i}")
                out_of("", act.activation(br_at[:, 2 * i:2 * i + 2, :].rearrange("p m s -> p (m s)"), b[:, :],
                                          ACT.Copy, scale=sub_gain))

            def gates_sigmoid(n):
                wait_emptied(act, f"gate{4 * n + 3}")
                act.activation(gates[n], gates[n], ACT.Sigmoid).then_inc(gates_ready, 1)

            gates_sigmoid(0)
            gates_sigmoid(1)
            for i in range(9, 12):
                gate_out(i)
            gates_sigmoid(2)
            for i in range(8):
                copy_out(f"adab{i}", mod_half(i))
            for t in range(TT):
                root(6 + t, g2_rt[:, t:t + 1], g2_ms[:, t:t + 1])
            for t in range(TT):
                for c in range(2):
                    b = product(act, f"h2T{t}{c}")
                    out_of("", act.activation(h2T[:, 4 * c:4 * c + 4, t * P:(t + 1) * P],
                                              b[:, :].rearrange("p (k s) -> p k s", k=4), ACT.Copy))
            copy_out("partial", part_logit, SEQ)
            act.sem_inc(misc_out["act"], MISC_COUNT["act"])
            act.wait_ge(top_ready, TT)
            for t in range(TT):
                act.activation(top_w[:, t, :], top[:, t, 0:TOPK], ACT.Exp, bias=top_s[:, t, 0:1],
                               accum_out=top_s[:, t, 1:2]).then_inc(top_exp, 1)

            def misc_copy(i, name, dst):
                b = misc_product(act, i, name)
                act.activation(dst, b[:, 0:dst.shape[1]], ACT.Copy).then_inc(misc_out["act"], 1)

            def body(i):
                for b, s in enumerate("ab"):
                    for g in range(2):
                        misc_copy(i, f"gather_{s}{g}", xT[:, 4 * g:4 * g + 4, :].rearrange("p k s -> p (k s)"))
                    for half in range(2):
                        r = slice(half * 512, (half + 1) * 512)
                        act.wait_ge(gate_min, i * 4 + 2 * b + half + 1)
                        act.activation(sig_s[:, r], gate_s[:, r], ACT.Sigmoid, scale=ALPHA)\
                            .then_inc(sigmoid_done, 1)
                    misc_copy(i, f"turn_{s}", turned)
                    for half in range(2):
                        misc_copy(i, f"hidT_{s}{half}",
                                  hidT[:, 4 * half:4 * half + 4, :].rearrange("p k s -> p (k s)"))

            def one_pass(p):
                with act.Fori(0, BODIES) as j:
                    body(p * BODIES + j)

            one_pass(0)
            act.wait_ge(flag_ready, 1)
            over = act.value_load(flag[0:1, 0:1], min_val=0, max_val=SEQ)
            with act.If(over > SLOTS):
                with act.Fori(1, PASSES) as p:
                    one_pass(p)

        @block.vector
        def _(dve):
            step = Steps(dve, dve_step)
            emptied_here = Steps(dve, emptied["dve"])

            def inverse_root(n, ms, rt, r, t):
                dve.wait_ge(sqrt_done, n)
                step(dve.reciprocal(r, rt))
                step.wait()
                step(dve.tensor_tensor(t, r, r, ALU.mult))
                step.wait()
                step(dve.tensor_tensor(t, t, ms, ALU.mult))
                step.wait()
                step(dve.tensor_scalar(t, t, -0.5, 1.5, ALU.mult, ALU.add))
                step.wait()
                step(dve.tensor_tensor(r, r, t, ALU.mult))
                step.wait()

            dve.wait_ge(mlp_landed, 16)
            y, turns = mlp_y[:, 0, :], mlp_y[:, 1, :]
            for n in range(3):
                b = product(dve, f"mlp{n}")
                emptied_here(dve.tensor_scalar(y, b[:, 0:SEQ], hf_col[:, n:n + 1], hf_col[:, 3:4],
                                               ALU.add, ALU.mult))
                emptied_here.wait()
                step(dve.tensor_scalar(turns, y, 1.0 / (2 * math.pi), ROUND, ALU.mult, ALU.add))
                step.wait()
                step(dve.tensor_scalar(turns, turns, -ROUND, None, ALU.add))
                for part_of_pi in (PI_A, PI_B, PI_C):
                    step.wait()
                    step(dve.scalar_tensor_tensor(y, turns, -part_of_pi, y, ALU.mult, ALU.add))
                step.wait()
                dve.tensor_scalar(y, y, 3.1415925, -3.1415925, ALU.min, ALU.max).then_inc(sin_asked, 1)
                if n == 0:
                    dve.wait_ge(vec_landed, 16)
                    dve.wait_ge(sig_ready, 1)
                    step(dve.tensor_tensor(cond, vec[:, 0, V_C:V_C + KT], cond_sig, ALU.mult))
                    step.wait()
                    dve.tensor_copy(cond_rep[:, :, :], cond.rearrange("p (k o) -> p k o", o=1)
                                    .to_broadcast([P, KT, 32])).then_inc(cond_ready, 1)
                    step(dve.tensor_scalar(sub_gain, vec[:, 0, V_SUB:V_SUB + 1], 1.0 - LAM_INIT, None, ALU.mult))
                    step(dve.tensor_tensor(w4s[:, 0, :], w4[:, 0, :], w4[:, 1, :], ALU.add))
                    dve.tensor_tensor(w4s[:, 1, :], w4[:, 0, :], w4[:, 1, :], ALU.subtract).then_inc(w4_summed, 1)
            dve.wait_ge(window_landed, 16)
            for s in range(2):
                for t in range(TT):
                    for o in range(2):
                        b = product(dve, f"filter{o}{s}{t}")
                        emptied_here(dve.tensor_tensor(filt[:, t, o, s, :], b[:, :], window[:, t, :], ALU.mult))
            dve.wait_ge(x_squared, TT)
            step(dve.tensor_scalar(x_ms, x_ss, 1.0 / D, EPS, ALU.mult, ALU.add))
            step.wait()
            dve.sem_inc(sqrt_asked, 1)
            inverse_root(1, x_ms, x_rt, x_r, x_t)
            dve.sem_inc(r_ready, 1)
            half_taps = TAPS // 2
            dve.wait_ge(xn_ready, TT)
            step(dve.memset(cf_in[:, :, 0:half_taps], 0.0))
            step(dve.memset(cf_in[:, :, SEQ + half_taps:], 0.0))
            b = product(dve, "modcol")
            step(dve.tensor_tensor(shift1, b[:, 0:KT], vec[:, 0, V_ADA:V_ADA + KT], ALU.add))
            emptied_here(dve.tensor_tensor(n1_gain, b[:, KT:2 * KT], vec[:, 0, V_ADA + KT:V_ADA + 2 * KT], ALU.add))
            emptied_here.wait()
            dve.scalar_tensor_tensor(n1_gain, n1_gain, 1.0, vec[:, 0, V_N1:V_N1 + KT], ALU.add, ALU.mult)\
                .then_inc(modcol_ready, 1)
            dve.memset(hy_in[:, :, 0:1], 0.0)
            dve.memset(hy_in[:, :, SEQ + 1:SEQ + 2], 0.0).then_inc(pads_zeroed, 1)
            dve.wait_ge(modcol_ready, 1)
            step.wait()
            for i in (1, 3):
                b = product(dve, f"xT{i}")
                for kk in range(2):
                    k = 2 * i + kk
                    ins = dve.tensor_scalar(hT[:, k, :], b[:, kk * SEQ:(kk + 1) * SEQ], n1_gain[:, k:k + 1],
                                            shift1[:, k:k + 1], ALU.mult, ALU.add)
                emptied_here(ins)
            wait_emptied(dve, "cg1")
            for i in range(2):
                b = product(dve, f"ca{i}")
                for m in range(2):
                    c = 2 * i + m
                    bias = V_BIN + HY_T + c
                    ins = dve.scalar_tensor_tensor(cf_in[:, c, half_taps:half_taps + SEQ],
                                                   b[:, m * SEQ:(m + 1) * SEQ], vec[:, 0, bias:bias + 1],
                                                   cf_cv[:, c, :], ALU.add, ALU.mult)
                emptied_here(ins)
            emptied_here.wait()

            def conv(first, last):
                for tap in range(first, last):
                    for c in range(WT):
                        w = vec[:, 2, tap * WT + c:tap * WT + c + 1]
                        src = cf_in[:, c, tap:tap + SEQ]
                        if tap == 0:
                            step(dve.tensor_scalar(cf_cv[:, c, :], src, w, vec[:, 0, V_DWB + c:V_DWB + c + 1],
                                                   ALU.mult, ALU.add))
                        else:
                            step.wait(conv_last[c])
                            ins = dve.scalar_tensor_tensor(cf_cv[:, c, :], src, w, cf_cv[:, c, :],
                                                           ALU.mult, ALU.add)
                            step(ins)
                        conv_last[c] = step.n
            conv_last = [0] * WT

            def short_conv(i):
                wait_emptied(dve, f"hy{i}")
                dve.wait_ge(pads_zeroed, 1)
                for tap in range(3):
                    for m in range(2):
                        c = 2 * i + m
                        w = vec[:, 1, tap * HY_T + c:tap * HY_T + c + 1]
                        src = hy_in[:, c, tap:tap + SEQ]
                        if tap == 0:
                            step(dve.tensor_scalar(hy_cv[:, c, :], src, w, vec[:, 0, V_HYB + c:V_HYB + c + 1],
                                                   ALU.mult, ALU.add))
                        else:
                            ins = dve.scalar_tensor_tensor(hy_cv[:, c, :], src, w, hy_cv[:, c, :],
                                                           ALU.mult, ALU.add)
                            if tap == 1:
                                step(ins)
                            else:
                                ins.then_inc(hy_conv_done, 1)
                    if tap < 2:
                        step.wait()

            def mix(o):
                for half in range(2):
                    k_cos, k_sin, k_cos2 = ((0, 3, 2), (1, 4, 1))[half]
                    u_cos = product(dve, f"u{o}{half}")
                    if half == 0:
                        wait_emptied(dve, f"spectrum{o}4")
                    step(dve.tensor_tensor(ysp[:, half, :], u_cos[:, :], spectra[:, o, k_cos, :], ALU.mult))
                    u_sin = product(dve, f"u{o}{2 + half}")
                    step(dve.tensor_tensor(hy_tmp[:, 0, :], u_sin[:, :], spectra[:, o, k_sin, :], ALU.mult))
                    emptied_here(dve.tensor_tensor(ysp[:, 2 + half, :], u_cos[:, :], spectra[:, o, k_sin, :],
                                                   ALU.mult))
                    emptied_here(dve.tensor_tensor(hy_tmp[:, 1, :], u_sin[:, :], spectra[:, o, k_cos2, :],
                                                   ALU.mult))
                    step.wait()
                    step(dve.tensor_tensor(ysp[:, half, :], ysp[:, half, :], hy_tmp[:, 0, :], ALU.subtract))
                    emptied_here.wait()
                    dve.tensor_tensor(ysp[:, 2 + half, :], ysp[:, 2 + half, :], hy_tmp[:, 1, :], ALU.add)\
                        .then_inc(spectra_mixed, 1)
                    dve.wait_ge(spectra_mixed, 2 * o + half + 1)
                    step.wait()

            def hyena_step(o):
                for t in range(TT):
                    step(dve.tensor_tensor(hy_tmp[:, t, :], hy[:, 0, t, :], hy_bias[:, o, :], ALU.mult))
                for t in range(TT):
                    b = product(dve, f"inv{o}{t}")
                    step.wait()
                    emptied_here(dve.tensor_tensor(hy_tmp[:, t, :], b[:, :], hy_tmp[:, t, :], ALU.add))
                    emptied_here.wait()
                    dve.tensor_tensor(hy[:, 0, t, :], hy_tmp[:, t, :], hy[:, 1 + o, t, :], ALU.mult)\
                        .then_inc(z_ready, 1)
                dve.wait_ge(z_ready, 2 * o + 2)

            def add_bias(j):
                for t in range(TT):
                    b = product(dve, f"{'qkv'[j]}{t}")
                    emptied_here(dve.tensor_tensor(qkv[:, j, t, :], b[:, :], qkv[:, j, t, :], ALU.add))
                emptied_here.wait()

            def heads(v):
                return v.rearrange("p (g d) -> p g d", d=HD)

            def norm_and_rotate(j):
                ms, rt, r, tmp = (qk_ss[:, n, :, :] for n in range(4))
                for t in range(TT):
                    v = qkv[:, j, t, :]
                    step(dve.tensor_tensor(hy_tmp[:, t, :], v, v, ALU.mult))
                step.wait()
                for t in range(TT):
                    step(dve.tensor_reduce(ms[:, t, :], heads(hy_tmp[:, t, :]), AX_X, ALU.add))
                step.wait()
                step(dve.tensor_scalar(ms, ms, 1.0 / HD, EPS, ALU.mult, ALU.add))
                step.wait()
                dve.sem_inc(sqrt_asked, 1)
                inverse_root(3 + j, ms, rt, r, tmp)
                both = [P, GROUPS, HD]
                half = HD // 2
                for t in range(TT):
                    v = heads(qkv[:, j, t, :])
                    step(dve.tensor_tensor(v, v, r[:, t, :].rearrange("p (g o) -> p g o", o=1).to_broadcast(both),
                                           ALU.mult))
                step.wait()
                for t in range(TT):
                    v = heads(qkv[:, j, t, :])
                    step(dve.tensor_tensor(v, v, gain[:, j:j + 1, :].to_broadcast(both), ALU.mult))
                step.wait()
                for t in range(TT):
                    v = heads(qkv[:, j, t, :])
                    c, s = heads(hy_tmp[:, 0, :]), heads(hy_tmp[:, 1, :])
                    step(dve.tensor_tensor(c, v, rope[:, 0, t:t + 1, :].to_broadcast(both), ALU.mult))
                    part_shape = [P, GROUPS, half]
                    step(dve.tensor_tensor(s[:, :, 0:half], v[:, :, half:],
                                           rope[:, 1, t:t + 1, 0:half].to_broadcast(part_shape), ALU.mult))
                    step(dve.tensor_tensor(s[:, :, half:], v[:, :, 0:half],
                                           rope[:, 1, t:t + 1, half:].to_broadcast(part_shape), ALU.mult))
                    step.wait()
                    dve.tensor_tensor(v, c, s, ALU.add).then_inc(roped, 1)
                    dve.wait_ge(roped, TT * j + t + 1)

            all_tiles = [P, WT, SEQ]

            def conformer_mean():
                b = product(dve, "mean")
                emptied_here(dve.scalar_tensor_tensor(
                    cf_cv, b[:, 0:SEQ].rearrange("p (o s) -> p o s", o=1).to_broadcast(all_tiles), -1.0 / W,
                    cf_cv, ALU.mult, ALU.add))
                emptied_here.wait()
                dve.tensor_tensor(cf_sq, cf_cv, cf_cv, ALU.mult).then_inc(centred, 1)

            def conformer_scale():
                b = product(dve, "var")
                emptied_here(dve.tensor_scalar(ln_ms, b[:, 0:SEQ], 1.0 / W, EPS, ALU.mult, ALU.add))
                emptied_here.wait()
                dve.sem_inc(sqrt_asked, 1)
                inverse_root(2, ln_ms, ln_rt, ln_r, ln_t)
                step(dve.tensor_tensor(cf_cv, cf_cv,
                                       ln_r.rearrange("p (o s) -> p o s", o=1).to_broadcast(all_tiles), ALU.mult))
                step.wait()

            for i in range(6):
                conv(3 * i, 3 * i + 3)
                short_conv(i)
            conv(18, TAPS)
            step.wait()
            dve.sem_inc(conv_done, 1)
            mix(0)
            dve.wait_ge(attn_landed, 16 * 4)
            add_bias(0)
            conformer_mean()
            dve.wait_ge(hyena_landed, 32)
            hyena_step(0)
            conformer_scale()
            norm_and_rotate(0)
            add_bias(1)
            mix(1)
            norm_and_rotate(1)
            add_bias(2)
            hyena_step(1)
            for n in range(2):
                dve.tensor_tensor_reduce(lam_v[:, 2 * n, :], lam_v[:, 2 * n, :], lam_v[:, 2 * n + 1, :], 1.0, 0.0,
                                         ALU.mult, ALU.add, lam_s[:, n:n + 1]).then_inc(lam_ready, 1)
            for m in range(WT):
                dve.tensor_scalar(br_cf[:, m, :], cf_cv[:, m, :], vec[:, 0, V_LNG + m:V_LNG + m + 1],
                                  vec[:, 0, V_LNB + m:V_LNB + m + 1], ALU.mult, ALU.add).then_inc(cf_scaled, 1)
            dve.wait_ge(cf_act, WT)
            dve.tensor_tensor(br_cf[:, :, :], br_cf[:, :, :], cf_cv, ALU.mult).then_inc(br_cf_ready, 1)
            dve.wait_ge(lam_exp, 1)
            step(dve.tensor_tensor(lam_s[:, 4:5], lam_s[:, 3:4], lam_s[:, 2:3], ALU.subtract))
            step.wait()
            step(dve.tensor_scalar(lam_s[:, 5:6], lam_s[:, 4:5], -LAM_INIT, None, ALU.add))
            step.wait()

            def score_max(h):
                for c in range(2):
                    b = product(dve, f"score{h}{c}")
                    step(dve.tensor_reduce(s_max[:, h, c, :], b[:, :].rearrange("p (t k) -> p t k", t=TT),
                                           AX_X, ALU.max))
                    step.wait()
                    dve.tensor_scalar(s_max[:, h, c, :], s_max[:, h, c, :], -SCALE, None, ALU.mult)\
                        .then_inc(max_ready, 1)

            def combine(h):
                wait_emptied(dve, f"score{h}1")
                step(dve.reciprocal(s_inv[:, h, :, :], s_sum[:, h, :, :]))
                step.wait()
                step(dve.tensor_scalar(s_inv[:, h, 1, :], s_inv[:, h, 1, :], lam_s[:, 5:6], None, ALU.mult))
                step.wait()
                for t in range(TT):
                    v = prob[:, h % 2, 1, t, :]
                    step(dve.tensor_scalar(v, v, s_inv[:, h, 1, t:t + 1], None, ALU.mult))
                step.wait()
                for t in range(TT):
                    v = prob[:, h % 2, 0, t, :]
                    ins = dve.scalar_tensor_tensor(v, v, s_inv[:, h, 0, t:t + 1], prob[:, h % 2, 1, t, :],
                                                   ALU.mult, ALU.add)
                ins.then_inc(att_ready, 1)

            score_max(0)
            score_max(1)
            def ada_sum(i):
                if i == 0:
                    dve.wait_ge(mod_bias_landed, 16)
                wait_chunk(dve, "ada", 4 + i)
                w = slot_view("ada", 4 + i)
                acc = mod_half(i)
                for k in range(KT):
                    ins = dve.scalar_tensor_tensor(acc, w[:, k, :], cond[:, k:k + 1], acc, ALU.mult, ALU.add)
                    if k < KT - 1:
                        step(ins)
                        step.wait()
                ins.then_inc(ada_summed, 1)

            def o_out(h):
                b = product(dve, f"o{h}")
                emptied_here(dve.tensor_copy(att[:, :, h * P:(h + 1) * P],
                                             b[:, 0:2 * P].rearrange("p (t e) -> p t e", t=TT)))

            for h in range(HEADS):
                combine(h)
                if h + 2 < HEADS:
                    score_max(h + 2)
                if h:
                    o_out(h - 1)
                    ada_sum(h - 1)
            o_out(HEADS - 1)
            emptied_here.wait()
            tiny = 2.0 ** -64
            o_a, o_b = o_ms[:, 0:8], o_ms[:, 8:16]

            def by_head(v):
                return v.rearrange("p (h e) -> p h e", h=HEADS)

            for t in range(TT):
                r = slice(4 * t, 4 * t + 4)
                step(dve.tensor_scalar(hy_tmp[:, 0, :], att[:, t, :], 1e17, -1e17, ALU.min, ALU.max))
                step(dve.tensor_scalar(hy_tmp[:, 1, :], att[:, t, :], tiny, None, ALU.mult))
                step.wait()
                for n in range(2):
                    step(dve.tensor_tensor(hy_tmp[:, n, :], hy_tmp[:, n, :], hy_tmp[:, n, :], ALU.mult))
                step.wait()
                step(dve.tensor_reduce(o_a[:, r], by_head(hy_tmp[:, 0, :]), AX_X, ALU.add))
                step(dve.tensor_reduce(o_b[:, r], by_head(hy_tmp[:, 1, :]), AX_X, ALU.add))
                step.wait()
            small_sum, large_sum = o_sel[:, 0:8], o_sel[:, 8:16]
            step(dve.tensor_scalar(o_b, o_b, 1e30, None, ALU.min))
            step.wait()
            step(dve.tensor_scalar(small_sum, o_b, 1e-5, None, ALU.is_lt))
            step(dve.tensor_scalar(o_sel[:, 16:24], o_b, 1.0, None, ALU.is_lt))
            step.wait()
            step(dve.tensor_tensor(large_sum, o_sel[:, 16:24], small_sum, ALU.subtract))
            step(dve.tensor_scalar(o_a, o_a, 1.0 / P, EPS, ALU.mult, ALU.add))
            step(dve.tensor_scalar(o_b, o_b, 1.0 / P, 1e-12, ALU.mult, ALU.add))
            step.wait()
            step(dve.tensor_scalar(large_sum, large_sum, tiny, None, ALU.mult))
            dve.sem_inc(sqrt_asked, 1)
            inverse_root(5, o_ms, o_rt, o_r, o_t)
            step(dve.tensor_tensor(o_r, o_r, o_sel[:, 0:16], ALU.mult))
            step.wait()
            step(dve.tensor_tensor(o_t[:, 0:8], o_r[:, 0:8], o_r[:, 8:16], ALU.add))
            step.wait()
            for t in range(TT):
                r = o_t[:, 4 * t:4 * t + 4].rearrange("p (h o) -> p h o", o=1).to_broadcast([P, HEADS, P])
                v = by_head(att[:, t, :])
                ins = dve.tensor_tensor(v, v, r, ALU.mult)
                step(ins)
            step.wait()
            dve.sem_inc(o_ready, 1)

            for i in range(HEADS - 1, 8):
                ada_sum(i)

            for g, n in enumerate((0, 1, 2)):
                dve.wait_ge(gates_ready, g + 1)
                for m in range(4):
                    b = product(dve, f"merge{n}{m}")
                    gate_v = gates[n][:, 2 * m:2 * m + 2, :].rearrange("p k s -> p (k s)")
                    sum_v = merged[:, 2 * m:2 * m + 2, :].rearrange("p k s -> p (k s)")
                    if g == 0:
                        emptied_here(dve.tensor_tensor(sum_v, b[:, :], gate_v, ALU.mult))
                        continue
                    emptied_here(dve.tensor_tensor(hy_tmp[:, m % 2, :], b[:, :], gate_v, ALU.mult))
                    emptied_here.wait()
                    ins = dve.tensor_tensor(sum_v, sum_v, hy_tmp[:, m % 2, :], ALU.add)
                    if g == 1:
                        step(ins)
                    else:
                        ins.then_inc(merged_ready, 1)
                if g == 1:
                    step.wait()
            step(dve.tensor_reduce(tile_sum, ident[:, :].rearrange("p (g e) -> p e g", e=EXPERTS),
                                   AX_X, ALU.add))
            wait_emptied(dve, "adab7")
            dve.wait_ge(gain2_landed, 16)
            step(dve.scalar_tensor_tensor(sc2, sc2, 1.0, norm2_gain, ALU.add, ALU.mult))
            step.wait()
            dve.sem_inc(merge_done, 1)
            dve.sem_inc(gate_up_read, 4)
            dve.wait_ge(x_again_landed, 16)
            for t in range(TT):
                one = slice(t, t + 1)
                for c in range(2):
                    b = product(dve, f"out{t}{c}")
                    r = slice(c * W, (c + 1) * W)
                    emptied_here(dve.tensor_tensor(hy_tmp[:, c, :], b[:, :], g1[:, r], ALU.mult))
                    emptied_here.wait()
                    step(dve.tensor_tensor(x[:, t, r], x[:, t, r], hy_tmp[:, c, :], ALU.add))
                    step.wait()
                    step(dve.tensor_tensor_reduce(squares, x[:, t, r], x[:, t, r], 1.0, 0.0,
                                                  ALU.mult, ALU.add, x1_ss[:, t, c:c + 1]))
                    if c == 0:
                        step(dve.tensor_tensor(h2[:, t, r], x[:, t, r], sc2[:, r], ALU.mult))
                    step.wait()
                step(dve.tensor_tensor(g2_ss[:, one], x1_ss[:, t, 0:1], x1_ss[:, t, 1:2], ALU.add))
                step.wait()
                step(dve.tensor_scalar(g2_ms[:, one], g2_ss[:, one], 1.0 / D, EPS, ALU.mult, ALU.add))
                step.wait()
                dve.sem_inc(sqrt_asked, 1)
                step(dve.tensor_tensor(h2[:, t, r], x[:, t, r], sc2[:, r], ALU.mult))
                inverse_root(6 + t, g2_ms[:, one], g2_rt[:, one], g2_r[:, one], g2_t[:, one])
                for c in range(2):
                    r = slice(c * W, (c + 1) * W)
                    dve.scalar_tensor_tensor(h2[:, t, r], h2[:, t, r], g2_r[:, one], sh2[:, r],
                                             ALU.mult, ALU.add).then_inc(h2_ready, 1)

            b = product(dve, "logits")
            dve.wait_ge(router_landed, 32)
            emptied_here(dve.tensor_tensor(
                logit[:, :, :], b[:, 0:TT * EXPERTS].rearrange("p (t e) -> p t e", t=TT),
                b_router[:, :].rearrange("p (o e) -> p o e", o=1).to_broadcast([P, TT, EXPERTS]), ALU.add))
            emptied_here.wait()
            dve.sem_inc(misc_out["dve"], MISC_COUNT["dve"])
            for t in range(TT):
                step(dve.max(top[:, t, :], logit[:, t, :]))
            step.wait()
            for t in range(TT):
                step(dve.max_index(top_i[:, t, :], top[:, t, :], logit[:, t, :]))
                dve.tensor_scalar(top_s[:, t, 0:1], top[:, t, 0:1], -1.0, None, ALU.mult).then_inc(top_ready, 1)
            step.wait()
            step(dve.tensor_copy(top_f[:, :, :], top_i[:, :, :]))
            step.wait()
            one_hot = [P, TT, TOPK, EXPERTS]
            step(dve.tensor_tensor(chosen, expert_no[:, :].rearrange("p (a b e) -> p a b e", a=1, b=1)
                                   .to_broadcast(one_hot),
                                   top_f[:, :, 0:TOPK].rearrange("p t (k o) -> p t k o", o=1)
                                   .to_broadcast(one_hot), ALU.is_equal))
            step.wait()
            dve.tensor_reduce(mask[:, :, :], chosen.rearrange("p t k e -> p t e k"), AX_X, ALU.add)\
                .then_inc(mask_ready, 1)
            dve.wait_ge(top_exp, TT)
            step(dve.reciprocal(top_s[:, :, 2:3], top_s[:, :, 1:2]))
            step.wait()
            step(dve.tensor_tensor(top_w[:, :, :], top_w[:, :, :],
                                   top_s[:, :, 2:3].to_broadcast([P, TT, TOPK]), ALU.mult))
            step.wait()
            step(dve.tensor_tensor(chosen_w, chosen, top_w[:, :, :].rearrange("p t (k o) -> p t k o", o=1)
                                   .to_broadcast(one_hot), ALU.mult))
            step.wait()
            step(dve.tensor_reduce(comb[:, :, 0:EXPERTS], chosen_w.rearrange("p t k e -> p t e k"), AX_X, ALU.add))
            b = product(dve, "rank")
            dve.wait_ge(mask_ready, 1)
            step(dve.scalar_tensor_tensor(pos[:, :, 0:EXPERTS], mask[:, :, :], -FAR,
                                          b[:, 0:TT * EXPERTS].rearrange("p (t e) -> p t e", t=TT),
                                          ALU.mult, ALU.add))
            step.wait()
            step(dve.tensor_scalar(pos[:, :, 0:EXPERTS], pos[:, :, 0:EXPERTS], FAR, None, ALU.add))
            step.wait()

            def members(j, call):
                shape = [P, 4, SLOTS]
                for t in range(TT):
                    p_of = pos[:, t, bass.ds(j * 4, 4)].rearrange("p (e o) -> p e o", o=1)
                    i_of = iota[:, :].rearrange("p (o s) -> p o s", o=1)
                    dve.tensor_tensor(member[:, t, :, :], i_of.to_broadcast(shape),
                                      p_of.to_broadcast(shape), ALU.is_equal).then_inc(member_ready, 1)
                dve.wait_ge(member_ready, call * 2)
                for t in range(TT):
                    c_of = comb[:, t, bass.ds(j * 4, 4)].rearrange("p (e o) -> p e o", o=1)
                    dve.tensor_tensor(weighted[:, t, :, :], member[:, t, :, :],
                                      c_of.to_broadcast(shape), ALU.mult).then_inc(weighted_ready, 1)

            def gate_up_half(i, b, half):
                r = slice(half * 512, (half + 1) * 512)
                n = 2 * b + half + 1
                dve.wait_ge(gate_up_done, i * 4 + n)
                dve.tensor_scalar(gate_s[:, r], bank[half][:, :], LIMIT, None, ALU.min).then_inc(gate_min, 1)
                dve.tensor_scalar(up_s[:, r], bank[2 + half][:, :], LIMIT, -LIMIT, ALU.min, ALU.max)\
                    .then_inc(gate_up_read, 1)

            def hidden_half(i, b, half, done):
                r = slice(half * 512, (half + 1) * 512)
                n = 2 * b + half + 1
                dve.wait_ge(sigmoid_done, i * 4 + n)
                done(dve.tensor_tensor(gate_s[:, r], gate_s[:, r], sig_s[:, r], ALU.mult))
                done.wait()
                dve.wait_ge(gate_up_read, i * 4 + 4 + n)
                dve.scalar_tensor_tensor(hid[:, r], up_s[:, r], 1.0, gate_s[:, r], ALU.add, ALU.mult)\
                    .then_inc(hid_ready, 1)

            def add(i, s, n):
                name = f"add_{s}{n}"
                b = misc_product(dve, i, name)
                prev = MISC_ORD[f"add_{'b' if s == 'a' else 'a'}{n}"] + (0 if s == "a" else MISC_COUNT["dve"])
                dve.wait_ge(misc_out["dve"], i * MISC_COUNT["dve"] + prev)
                quarter = x[:, n % 2, (n // 2) * W:(n // 2 + 1) * W]
                dve.tensor_tensor(quarter, quarter, b[:, :], ALU.add).then_inc(misc_out["dve"], 1)

            def y_out(i, b):
                for n in range(2):
                    dve.wait_ge(y_done, i * 4 + 2 * b + n + 1)
                    r = slice(n * W, (n + 1) * W)
                    dve.tensor_tensor(y_s[:, r], bank[4 + n][:, :], g2[:, r], ALU.mult).then_inc(y_read, 1)

            def body(i, j, p):
                done = LoopSteps(dve, moe_step, i * BODY_STEPS)
                for b in range(2):
                    if b:
                        for n in range(4):
                            add(i, "a", n)
                    for half in range(2):
                        gate_up_half(i, b, half)
                        hidden_half(i, b, half, done)
                    if b:
                        dve.wait_ge(misc_done, i * len(MISC) + MISC_NO["turn_b"] + 1)
                        members(j + 1, i + p + 2)
                    y_out(i, b)
                for n in range(4):
                    add(i, "b", n)
                assert done.n == BODY_STEPS

            def one_pass(p, first=False):
                if not first:
                    dve.tensor_scalar(pos[:, :, 0:EXPERTS], pos[:, :, 0:EXPERTS], -float(SLOTS), None, ALU.add)\
                        .then_inc(pass_step, 1)
                    dve.wait_ge(pass_step, p)
                    dve.wait_ge(misc_done, p * (BODIES * len(MISC)))
                members(0, p * (BODIES + 1) + 1)
                if first:
                    b = product(dve, "rank")
                    step(dve.tensor_reduce(chosen_n, b[:, 64:64 + 2 * EXPERTS]
                                           .rearrange("p (t e) -> p e t", t=TT), AX_X, ALU.add))
                    step.wait()
                    emptied_here(dve.tensor_reduce(most, chosen_n, AX_X, ALU.max))
                    emptied_here.wait()
                    dve.tensor_copy(flag[:, :], most).then_inc(flag_ready, 1)
                    dve.sem_inc(y_read, 4)
                with dve.Fori(0, BODIES) as j:
                    body(p * BODIES + j, j, p)

            one_pass(0, first=True)
            over = dve.value_load(flag[0:1, 0:1], min_val=0, max_val=SEQ)
            with dve.If(over > SLOTS):
                with dve.Fori(1, PASSES) as p:
                    one_pass(p)
            dve.wait_ge(misc_out["dve"], MISC_COUNT["dve"] * (BODIES + 1))
            dve.drain()
            dve.sem_inc(out_ready, 1)

    return nc


def shape_constants():
    f32 = np.float32
    n = 2 * SEQ
    t, f = np.arange(SEQ)[:, None], np.arange(SEQ)[None, :]
    cos, sin = np.cos(2 * np.pi * t * f / n), np.sin(2 * np.pi * t * f / n)
    nyquist = np.cos(np.pi * np.arange(SEQ))
    sin_ny = sin.copy()
    sin_ny[:, 0] = nyquist
    cos_ny = cos[:, 0:P].copy()
    cos_ny[:, 0] = nyquist
    dft_f = np.concatenate([cos, sin_ny, cos_ny, sin[:, 0:P]], axis=1)
    weight = np.full((SEQ, 1), 2.0 / n)
    weight[0] = 1.0 / n
    dft_i = np.concatenate([cos.T * weight, sin_ny.T * weight], axis=0)

    pos = np.arange(SEQ, dtype=f32)
    time = np.linspace(0.0, 1.0, SEQ, dtype=f32)[:, None]
    deltas = np.abs(np.linspace(math.log(1e-2) / 0.3, math.log(1e-2) / 1.5, W, dtype=f32))
    window = np.exp(-time * deltas[None, :]) + f32(0.05)

    inv = f32(1.0) / (f32(10000.0) ** (np.arange(0, HD, 2, dtype=f32) / f32(HD)))
    ra = pos[:, None] * inv[None, :]
    rc, rs = np.cos(ra), np.sin(ra)
    rope = np.stack([np.concatenate([rc, rc], axis=1), np.concatenate([-rs, rs], axis=1)])
    made = {"dft_f": dft_f, "dft_i": dft_i, "window": window, "rope": rope}
    return {k: np.ascontiguousarray(v, dtype=f32) for k, v in made.items()}


def position_features():
    f32 = np.float32
    time = np.linspace(0.0, 1.0, SEQ, dtype=f32)[:, None]
    bands = np.linspace(1e-4, BANDS - 1, BANDS, dtype=f32)
    ang = f32(2.0 * math.pi / SEQ) * np.arange(SEQ, dtype=f32)[:, None] * bands[None, :]
    return np.concatenate([time, np.cos(ang), -np.sin(ang)], axis=-1).T


PACKED = ("norm1_g", "q_norm_g", "k_norm_g", "lam_q1", "lam_k1", "lam_q2", "lam_k2", "subln_g", "hy_conv_w",
          "hy_conv_b", "hf_w1", "hf_b1", "hf_w2", "hf_b2", "hf_w3", "hf_b3", "hf_freq", "hf_w4", "cf_dw_w",
          "cf_dw_b", "cf_ln_g", "cf_ln_b", "b_gu", "b_down", "c")


def packed(inputs):
    v = {k: np.asarray(inputs[k]) for k in PACKED}
    b_ada, b_in = np.asarray(inputs["b_ada"]), np.asarray(inputs["b_in"])
    columns = np.zeros((3, P, P), np.float32)
    parts = [(0, V_ADA, b_ada[0, 0:2 * D]), (0, V_N1, v["norm1_g"]), (0, V_BIN, b_in[0, 3 * W:]),
             (0, V_SUB, v["subln_g"]), (0, V_DWB, v["cf_dw_b"]), (0, V_LNG, v["cf_ln_g"]),
             (0, V_LNB, v["cf_ln_b"]), (0, V_C, v["c"]), (0, V_HYB, v["hy_conv_b"]),
             (1, 0, v["hy_conv_w"]), (2, 0, v["cf_dw_w"])]
    for i, row, x in parts:
        x = x.reshape(-1, P)
        columns[i, row:row + len(x)] = x
    net = np.zeros((P, NET_COLS), np.float32)
    for o in range(2):
        rows = slice(o * HF_HID, (o + 1) * HF_HID)
        net[rows, 0:2 * W] = v["hf_w4"][0, :, o * 2 * W:(o + 1) * 2 * W]
        for n, name in enumerate(("hf_b1", "hf_b2", "hf_b3", "hf_freq")):
            net[rows, NET_B + n] = v[name][0]
    net[0:HF_EMB, NET_Z:NET_W] = position_features()
    for n, name in enumerate(("hf_w1", "hf_w2", "hf_w3")):
        w = v[name][0]
        net[0:len(w), NET_W + n * HF_HID:NET_W + (n + 1) * HF_HID] = w
    head_rows = np.concatenate([v[n] for n in ("q_norm_g", "k_norm_g", "lam_q1", "lam_k1", "lam_q2", "lam_k2")],
                               axis=1)
    return {"columns": columns.reshape(3 * P, P).T, "filter_net": net, "head_rows": head_rows,
            "b_experts": np.concatenate([v["b_gu"][0], v["b_down"][0]], axis=1)}


def kernel(**inputs):
    import concourse.bacc as _bacc
    from concourse.bass_utils import run_bass_kernel_spmd as _run

    nc = _bacc.Bacc("TRN2", target_bir_lowering=False, num_devices=1)
    arrays, args = {}, {}
    for name, v in {**inputs, **packed(inputs), **shape_constants()}.items():
        if name in PACKED:
            continue
        v = np.ascontiguousarray(v)
        arrays[name] = v
        args[name] = nc.dram_tensor(name, v.shape, mybir.dt.from_np(v.dtype), kind="ExternalInput").ap()
    out = nc.dram_tensor("layer_out", (1, SEQ, D), F32, kind="ExternalOutput").ap()
    build_layer(nc, args, out)
    r = _run(nc, [arrays], core_ids=[0])
    return r.results[0]["layer_out"]
```
